# Optimizing a Trainium2 kernel written in Bass

```python
import jax, jax.numpy as jnp
from jax import lax
import numpy as np

D_MODEL = 1024
BATCH = 1
SEQ = 1024
DEPTH = 2

CHUNK = 64
QBLOCK = 128
PLE_DIM = 256
EPS = 1e-6
NEG_INF = -1e30
MLA_HEADS = 8
MLA_NOPE = 64
MLA_ROPE = 32
MLA_V = 64
MLA_Q_LORA = 384
MLA_KV_LORA = 256
ROPE_THETA = 10000.0
CHK_HEADS = 8
CHK_DIM = 64
LEFT_CHUNKS = 8
REL_CLIP = 256
FOX_HEADS = 16
FOX_DIM = 64
MLA_WIDTH = MLA_HEADS * MLA_V
CHK_WIDTH = CHK_HEADS * CHK_DIM
FOX_WIDTH = FOX_HEADS * FOX_DIM
AB_SIZES = (MLA_Q_LORA, MLA_KV_LORA, MLA_ROPE, MLA_WIDTH, CHK_WIDTH, CHK_WIDTH, CHK_WIDTH, CHK_WIDTH)
AB_IN = sum(AB_SIZES)
FOX_SIZES = (FOX_WIDTH, FOX_WIDTH, FOX_WIDTH, FOX_WIDTH, FOX_HEADS)
FOX_IN = sum(FOX_SIZES)
N_AB = (DEPTH + 1) // 2
N_FOX = DEPTH // 2

kernel_name = 'hybrid_mla_chunkrel_fox_trunk'

def rms_norm(x, g):
    xf = x.astype(jnp.float32)
    y = xf * lax.rsqrt(jnp.mean(xf * xf, axis=-1, keepdims=True) + EPS)
    return (y * g.astype(jnp.float32)).astype(x.dtype)

def split_cols(z, sizes):
    return jnp.split(z, np.cumsum(sizes)[:-1].tolist(), axis=-1)

def apply_rope(x, positions):
    half = x.shape[-1] // 2
    inv_freq = 1.0 / (ROPE_THETA ** (jnp.arange(half, dtype=jnp.float32) / half))
    ang = positions.astype(jnp.float32)[:, :, None, None] * inv_freq
    cos, sin = jnp.cos(ang), jnp.sin(ang)
    xf = x.astype(jnp.float32)
    x1, x2 = xf[..., :half], xf[..., half:]
    return jnp.concatenate([x1 * cos - x2 * sin, x2 * cos + x1 * sin], axis=-1).astype(x.dtype)

def blocked_attention(q, k, v, scale, logit_fn):
    B, S, H, Dk = q.shape
    nb = S // QBLOCK
    qb = q.reshape(B, nb, QBLOCK, H, Dk).transpose(1, 0, 2, 3, 4)

    def one_block(args):
        q_i, b_i = args
        s = jnp.einsum('bqhd,bkhd->bhqk', q_i, k, preferred_element_type=jnp.float32) * scale
        s = logit_fn(s, b_i)
        pr = jax.nn.softmax(s, axis=-1).astype(v.dtype)
        return jnp.einsum('bhqk,bkhd->bqhd', pr, v)

    out = lax.map(one_block, (qb, jnp.arange(nb)))
    return out.transpose(1, 0, 2, 3, 4).reshape(B, S, H, v.shape[-1])

def mla_attention(cq, ckv, kr, positions, q_norm, w_uq, kv_norm, w_ukv, q_gain, k_gain):
    B, S, _ = cq.shape
    q = (rms_norm(cq, q_norm) @ w_uq).reshape(B, S, MLA_HEADS, MLA_NOPE + MLA_ROPE)
    kv = (rms_norm(ckv, kv_norm) @ w_ukv).reshape(B, S, MLA_HEADS, MLA_NOPE + MLA_V)
    k_nope, v = kv[..., :MLA_NOPE], kv[..., MLA_NOPE:]
    k_rope = jnp.broadcast_to(kr[:, :, None, :], (B, S, MLA_HEADS, MLA_ROPE))
    k = jnp.concatenate([k_nope, k_rope], axis=-1)
    q = rms_norm(q, q_gain)
    k = rms_norm(k, k_gain)
    q = jnp.concatenate([q[..., :MLA_NOPE], apply_rope(q[..., MLA_NOPE:], positions)], axis=-1)
    k = jnp.concatenate([k[..., :MLA_NOPE], apply_rope(k[..., MLA_NOPE:], positions)], axis=-1)
    key_chunk = jnp.arange(S) // CHUNK

    def chunk_causal(s, b_i):
        q_chunk = (b_i * QBLOCK + jnp.arange(QBLOCK)) // CHUNK
        mask = key_chunk[None, :] <= q_chunk[:, None]
        return jnp.where(mask[None, None], s, NEG_INF)

    o = blocked_attention(q, k, v, (MLA_NOPE + MLA_ROPE) ** -0.5, chunk_causal)
    return o.reshape(B, S, MLA_WIDTH)

def chunk_rel_attention(q, k, v, rel_bias):
    B, S, H, Dh = q.shape
    nC = S // CHUNK
    band = (LEFT_CHUNKS + 1) * CHUNK
    qc = q.reshape(B, nC, CHUNK, H, Dh)
    pad = ((0, 0), (LEFT_CHUNKS, 0), (0, 0), (0, 0), (0, 0))
    kp = jnp.pad(k.reshape(B, nC, CHUNK, H, Dh), pad)
    vp = jnp.pad(v.reshape(B, nC, CHUNK, H, Dh), pad)
    cidx = jnp.arange(nC)[:, None] + jnp.arange(LEFT_CHUNKS + 1)[None, :]
    kb = kp[:, cidx].reshape(B, nC, band, H, Dh)
    vb = vp[:, cidx].reshape(B, nC, band, H, Dh)
    s = jnp.einsum('bcqhd,bckhd->bhcqk', qc, kb, preferred_element_type=jnp.float32) * (Dh ** -0.5)
    dist = LEFT_CHUNKS * CHUNK + jnp.arange(CHUNK)[:, None] - jnp.arange(band)[None, :]
    ridx = jnp.clip(dist, -REL_CLIP, REL_CLIP) + REL_CLIP
    bias = rel_bias.astype(jnp.float32)[:, ridx]
    valid = jnp.repeat(cidx >= LEFT_CHUNKS, CHUNK, axis=1)
    s = jnp.where(valid[None, None, :, None, :], s + bias[None, :, None], NEG_INF)
    pr = jax.nn.softmax(s, axis=-1).astype(v.dtype)
    o = jnp.einsum('bhcqk,bckhd->bcqhd', pr, vb)
    return o.reshape(B, S, H * Dh)

def forgetting_attention(q, k, v, f_logit, b_f):
    B, S, H, Dh = q.shape
    log_f = jax.nn.log_sigmoid(f_logit.astype(jnp.float32) + b_f.astype(jnp.float32))
    cum = lax.cumsum(log_f, axis=1).transpose(0, 2, 1)
    kpos = jnp.arange(S)

    def decay_causal(s, b_i):
        cq = lax.dynamic_slice_in_dim(cum, b_i * QBLOCK, QBLOCK, axis=2)
        qpos = b_i * QBLOCK + jnp.arange(QBLOCK)
        mask = kpos[None, :] <= qpos[:, None]
        return jnp.where(mask[None, None], s + cq[..., :, None] - cum[..., None, :], NEG_INF)

    o = blocked_attention(q, k, v, Dh ** -0.5, decay_causal)
    return o.reshape(B, S, H * Dh)

def setup_inputs(seed: int = 0) -> dict:
    key = jax.random.key(seed)
    ks = jax.random.split(key, 24)

    def nrm(k, shape, scale):
        return jax.random.normal(k, shape, jnp.float32) * scale

    def gain(k, shape):
        return 1.0 + nrm(k, shape, 0.05)

    offsets = jax.random.randint(ks[2], (BATCH, 1), 0, 4096, dtype=jnp.int32)
    positions = offsets + jnp.arange(SEQ, dtype=jnp.int32)[None, :]
    return {
        'x': nrm(ks[0], (BATCH, SEQ, D_MODEL), 1.0),
        'p': nrm(ks[1], (DEPTH, BATCH, SEQ, PLE_DIM), 1.0),
        'positions': positions,
        'norm_g': gain(ks[3], (DEPTH, D_MODEL)),
        'ab_w_in': nrm(ks[4], (N_AB, D_MODEL, AB_IN), D_MODEL ** -0.5),
        'mla_q_norm': gain(ks[5], (N_AB, MLA_Q_LORA)),
        'mla_w_uq': nrm(ks[6], (N_AB, MLA_Q_LORA, MLA_HEADS * (MLA_NOPE + MLA_ROPE)), MLA_Q_LORA ** -0.5),
        'mla_kv_norm': gain(ks[7], (N_AB, MLA_KV_LORA)),
        'mla_w_ukv': nrm(ks[8], (N_AB, MLA_KV_LORA, MLA_HEADS * (MLA_NOPE + MLA_V)), MLA_KV_LORA ** -0.5),
        'mla_q_gain': gain(ks[9], (N_AB, MLA_NOPE + MLA_ROPE)),
        'mla_k_gain': gain(ks[10], (N_AB, MLA_NOPE + MLA_ROPE)),
        'chk_q_gain': gain(ks[11], (N_AB, CHK_DIM)),
        'chk_k_gain': gain(ks[12], (N_AB, CHK_DIM)),
        'chk_rel_bias': nrm(ks[13], (N_AB, CHK_HEADS, 2 * REL_CLIP + 1), 0.1),
        'ab_w_out': nrm(ks[14], (N_AB, MLA_WIDTH + CHK_WIDTH, D_MODEL), (MLA_WIDTH + CHK_WIDTH) ** -0.5),
        'fox_w_in': nrm(ks[15], (N_FOX, D_MODEL, FOX_IN), D_MODEL ** -0.5),
        'fox_b_f': 2.0 + nrm(ks[16], (N_FOX, FOX_HEADS), 0.1),
        'fox_q_gain': gain(ks[17], (N_FOX, FOX_DIM)),
        'fox_k_gain': gain(ks[18], (N_FOX, FOX_DIM)),
        'fox_w_out': nrm(ks[19], (N_FOX, FOX_WIDTH, D_MODEL), FOX_WIDTH ** -0.5),
        'pe_w': nrm(ks[20], (DEPTH, PLE_DIM, D_MODEL), PLE_DIM ** -0.5),
        'pe_gate_norm': gain(ks[21], (DEPTH, D_MODEL)),
        'pe_gate_w': nrm(ks[22], (DEPTH, D_MODEL, D_MODEL), D_MODEL ** -0.5),
    }

def reference(x, p, positions, norm_g, ab_w_in, mla_q_norm, mla_w_uq, mla_kv_norm, mla_w_ukv,
              mla_q_gain, mla_k_gain, chk_q_gain, chk_k_gain, chk_rel_bias, ab_w_out,
              fox_w_in, fox_b_f, fox_q_gain, fox_k_gain, fox_w_out, pe_w, pe_gate_norm, pe_gate_w):
    B, S, _ = x.shape
    h = x
    for i in range(DEPTH):
        u = rms_norm(h, norm_g[i])
        l = i // 2
        if i % 2 == 0:
            cq, ckv, kr, g_a, q_b, k_b, v_b, g_b = split_cols(u @ ab_w_in[l], AB_SIZES)
            o_a = mla_attention(cq, ckv, kr, positions, mla_q_norm[l], mla_w_uq[l],
                                mla_kv_norm[l], mla_w_ukv[l], mla_q_gain[l], mla_k_gain[l])
            q_b = rms_norm(q_b.reshape(B, S, CHK_HEADS, CHK_DIM), chk_q_gain[l])
            k_b = rms_norm(k_b.reshape(B, S, CHK_HEADS, CHK_DIM), chk_k_gain[l])
            v_b = v_b.reshape(B, S, CHK_HEADS, CHK_DIM)
            o_b = chunk_rel_attention(q_b, k_b, v_b, chk_rel_bias[l])
            mixed = jnp.concatenate([o_a * jax.nn.silu(g_a), o_b * jax.nn.silu(g_b)], axis=-1) @ ab_w_out[l]
        else:
            q_c, k_c, v_c, g_c, f_c = split_cols(u @ fox_w_in[l], FOX_SIZES)
            q_c = rms_norm(q_c.reshape(B, S, FOX_HEADS, FOX_DIM), fox_q_gain[l])
            k_c = rms_norm(k_c.reshape(B, S, FOX_HEADS, FOX_DIM), fox_k_gain[l])
            v_c = v_c.reshape(B, S, FOX_HEADS, FOX_DIM)
            o_c = forgetting_attention(q_c, k_c, v_c, f_c, fox_b_f[l])
            mixed = (o_c * jax.nn.silu(g_c)) @ fox_w_out[l]
        h = h + mixed
        ple_gate = jax.nn.sigmoid(rms_norm(h, pe_gate_norm[i]) @ pe_gate_w[i])
        h = h + (p[i] @ pe_w[i]) * ple_gate
    return h


_drawn_inputs = setup_inputs


def setup_inputs(seed=0):
    import zlib

    import numpy as np

    out = dict(_drawn_inputs(seed))
    spreads = {}
    factors = {'norm_g': 3.229,
     'mla_q_norm': 8.0,
     'mla_kv_norm': 8.0,
     'mla_q_gain': 8.0,
     'mla_k_gain': 8.0,
     'chk_q_gain': 8.0,
     'chk_k_gain': 8.0,
     'chk_rel_bias': 8.0,
     'fox_b_f': 16.186,
     'fox_q_gain': 7.658,
     'fox_k_gain': 7.649,
     'pe_gate_norm': 23.195}
    for name, (base, spread) in spreads.items():
        noise = np.random.default_rng([zlib.crc32(name.encode()), seed]).standard_normal(out[name].shape)
        drawn = base * np.exp(spread * noise) if base else spread * noise
        out[name] = __import__('jax').numpy.asarray(drawn.astype(out[name].dtype))
    for name, factor in factors.items():
        out[name] = (out[name] * factor).astype(out[name].dtype)
    return out
```

```python
from contextlib import ExitStack

import numpy as np

import concourse.bass as bass
from concourse import mybir

F32 = mybir.dt.float32
F32R = mybir.dt.float32r
BF16 = mybir.dt.bfloat16
I32 = mybir.dt.int32
ALU = mybir.AluOpType
ACT = mybir.ActivationFunctionType
AX_X = mybir.AxisListType.X

P = 128
D = 1024
S = 1024
KD = D // P
ST = S // P
HALF = 512
NH = S // HALF
PLE = 256
EPS = 1e-6
NEG = -1e30
BIG = 3.0e38

HEADS = 8
NOPE, ROPE, VDIM = 64, 32, 64
QK = NOPE + ROPE
QLORA, KVLORA = 384, 256
CHK = 64
LEFT = 8
BAND = 640
CHUNK = 64
CLIP = 256
FH = 16
FD = 64

C_KR = QLORA + KVLORA
C_GA = C_KR + ROPE
C_QB = C_GA + HEADS * VDIM

LAT_Q, LAT_KV, KR = 0, 3, 5
QB0, QB1 = 6, 14
VB1 = 18
GB1 = 22
GA1 = 26
MQ1 = 34
MK1 = 42


def wait(eng, sem, value):
    if isinstance(value, int) and value <= 0:
        return
    eng.wait_ge(sem, value)


def pairs(eng, lo, hi, body):
    body(lo)
    if hi - lo == 2:
        body(lo + 1)
    elif hi > lo + 1:
        with eng.Fori(lo + 1, hi) as i:
            body(i)


def build(nc, x, p, positions, norm_g, ab_w_in, mla_q_norm, mla_w_uq, mla_kv_norm, mla_w_ukv,
          mla_q_gain, mla_k_gain, chk_q_gain, chk_k_gain, chk_rel_bias, ab_w_out,
          fox_w_in, fox_b_f, fox_q_gain, fox_k_gain, fox_w_out, pe_w, pe_gate_norm, pe_gate_w,
          rope_freq, out):
    top = ExitStack()

    def dram(name, shape):
        return nc.dram_tensor(name, shape, F32, kind="Internal").ap()

    s_h = dram("s_h", [P, KD, S])
    s_ab = dram("s_ab", [GA1 - QB0, P, S])
    s_mq = dram("s_mq", [HEADS, QK, S])
    s_mk = dram("s_mk", [HEADS, QK, S])
    s_mv = dram("s_mv", [HEADS, VDIM, S])
    s_fox = dram("s_fox", [4 * FH // 2, P, S])
    s_cum = dram("s_cum", [FH, S])
    s_rel = dram("s_rel", [HEADS, 768])
    s_rep = dram("s_rep", [HEADS, P, 768])
    s_bias = dram("s_bias", [HEADS, P, BAND])

    class Space:

        def __init__(self, stack, tag):
            self.stack, self.tag, self.numbers = stack, tag, []

        def sb(self, name, shape, dt=F32):
            return self.stack.enter_context(nc.sbuf_tensor(f"{self.tag}_{name}", shape, dt))

        def ps(self, name, shape, dt=F32):
            return self.stack.enter_context(nc.psum_tensor(f"{self.tag}_{name}", shape, dt))

        def sem(self, name):
            handle = self.stack.enter_context(nc.semaphore(f"{self.tag}_{name}"))
            self.numbers.append(handle.num)
            return handle

        def end(self):
            numbers = sorted(self.numbers)
            while numbers:
                n = next((k for k in range(1, len(numbers)) if numbers[k] != numbers[0] + k), len(numbers))
                nc.all_engine_barrier(sems_to_clear=range(numbers[0], numbers[0] + n))
                numbers = numbers[n:]

    G = Space(top, "g")
    hT = G.sb("hT", [P, KD, S])
    a_hi = G.sb("a_hi", [P, KD, S], F32R)
    a_lo = G.sb("a_lo", [P, KD, S], F32R)
    ident = G.sb("ident", [P, P])
    ident_r = G.sb("ident_r", [P, P], F32R)
    ident_b = G.sb("ident_b", [P, P], BF16)
    causal = G.sb("causal", [P, P], BF16)
    blockc = G.sb("blockc", [P, P], BF16)
    low_q = G.sb("low_q", [P, CHUNK], BF16)
    high_q = G.sb("high_q", [P, CHUNK], BF16)
    ind_all = G.sb("ind_all", [P, 2])
    ind_lat = G.sb("ind_lat", [P, 4])
    ind_head = G.sb("ind_head", [P, 2])
    ind_mla = G.sb("ind_mla", [P, 2])
    g_norm = G.sb("g_norm", [P, 2, KD])
    g_gate = G.sb("g_gate", [P, 2, KD])
    g_lat = G.sb("g_lat", [P, 5])
    g_mla = G.sb("g_mla", [P, 2])
    g_chk = G.sb("g_chk", [P, 8])
    g_fox = G.sb("g_fox", [P, 16])
    b_f = G.sb("b_f", [FH, 1])

    class Norm:

        def __init__(self, sp):
            self.ss = sp.ps("ss", [P, ST, 2])
            self.bc = sp.ps("bc", [P, S])
            self.r1 = sp.sb("r1", [P, ST, 2])
            self.r2 = sp.sb("r2", [P, ST, 2])
            self.r3 = sp.sb("r3", [P, ST, 2])
            self.e_hi = sp.sb("e_hi", [P, ST, 2, 64], F32R)
            self.e_lo = sp.sb("e_lo", [P, ST, 2, 64], F32R)
            self.summed = sp.sem("summed")
            self.eps_in = sp.sem("eps_in")
            self.inverted = sp.sem("inverted")
            self.rooted = sp.sem("rooted")
            self.spread_hi = sp.sem("spread_hi")
            self.spread = sp.sem("spread")
            self.on_rows = sp.sem("on_rows")
            self.applied = sp.sem("applied")

        def pe_sum(self, pe, n, squares, indicator):
            wait(pe, self.eps_in, n)
            for t in range(ST):
                last = nc.tensor.matmul(self.ss[:, t, :], squares[:, t * P:(t + 1) * P], indicator,
                                        start=True, stop=True)
            last.then_inc(self.summed, 1)

        def dve_invert(self, dve, n):
            wait(dve, self.summed, n + 1)
            nc.vector.tensor_scalar(self.r1[:], self.ss[:], EPS, None, ALU.add).then_inc(self.eps_in, 1)
            wait(dve, self.eps_in, n + 1)
            nc.vector.reciprocal(self.r2[:], self.r1[:]).then_inc(self.inverted, 1)

        def act_root(self, act, n):
            wait(act, self.inverted, n + 1)
            nc.scalar.activation(self.r3[:], self.r2[:], ACT.Sqrt).then_inc(self.rooted, 1)

        def dve_spread(self, dve, n):
            wait(dve, self.rooted, n + 1)
            wait(dve, self.on_rows, n)
            r3 = self.r3[:].unsqueeze(3).to_broadcast([P, ST, 2, 64])
            nc.vector.tensor_copy(self.e_hi[:], r3).then_inc(self.spread_hi, 1)
            wait(dve, self.spread_hi, n + 1)
            nc.vector.tensor_tensor(self.e_lo[:], r3, self.e_hi[:].bitcast(F32), ALU.subtract)\
                .then_inc(self.spread, 1)

        def pe_rows(self, pe, n):
            wait(pe, self.spread, n + 1)
            wait(pe, self.applied, n)
            for t in range(ST):
                for e, part in enumerate((self.e_hi, self.e_lo)):
                    last = nc.tensor.matmul(self.bc[:, t * P:(t + 1) * P],
                                            part[:, t].rearrange("p h f -> p (h f)"), ident_r[:],
                                            start=(e == 0), stop=(e == 1))
            last.then_inc(self.on_rows, 1)

    def stage_entry(rot):
        with ExitStack() as st:
            sp = Space(st, "en")
            xr = sp.sb("xr", [P, 2, D])
            xt = sp.ps("xt", [P, 2, KD, P])
            posi = sp.sb("posi", [P, S], I32)
            ang = sp.sb("ang", [P, S])
            turns = sp.sb("turns", [P, S])
            freq = sp.sb("freq", [P, 1])
            two_pi = sp.sb("two_pi", [P, S])
            rel = sp.sb("rel", [HEADS, 2 * CLIP + 1])
            rel_ext = sp.sb("rel_ext", [HEADS, 768])
            loaded = [sp.sem("loaded0"), sp.sem("loaded1")]
            small = sp.sem("small")
            pos_in = sp.sem("pos_in")
            rel_in = sp.sem("rel_in")
            rel_out = sp.sem("rel_out")
            turned = sp.sem("turned")
            from_act = sp.sem("from_act")
            from_dve = sp.sem("from_dve")
            made = sp.sem("made")
            chain = sp.sem("chain")
            angled = sp.sem("angled")
            widened = sp.sem("widened")
            sined = sp.sem("sined")
            with nc.Block() as block:

                @block.sync
                def _(sync):
                    def load(t, b):
                        wait(sync, turned, t - 1)
                        sync.dma_start(xr[:, b, :], x[0, bass.ds(t * P, P), :]).then_inc(loaded[b], 16)

                    def body(i):
                        for b in range(2):
                            load(2 * i + b, b)
                    pairs(sync, 0, ST // 2, body)

                @block.scalar
                def _(act):
                    n = 0
                    act.dma_start(posi[64:128, :], positions[0:1, :].to_broadcast([64, S])).then_inc(pos_in, 16)
                    act.dma_start(freq[64:128, :], rope_freq).then_inc(pos_in, 16)
                    act.dma_start(rel[:], chk_rel_bias[0]).then_inc(rel_in, 16)

                    def col(dst, src):
                        nonlocal n
                        act.dma_start(dst, src).then_inc(small, 16)
                        n += 1

                    for layer in range(2):
                        col(g_norm[:, layer, :], norm_g[layer].rearrange("(k q) -> q k", q=P))
                        col(g_gate[:, layer, :], pe_gate_norm[layer].rearrange("(k q) -> q k", q=P))
                    col(g_lat[:, 0:3], mla_q_norm[0].rearrange("(k q) -> q k", q=P))
                    col(g_lat[:, 3:5], mla_kv_norm[0].rearrange("(k q) -> q k", q=P))
                    half = ROPE // 2
                    for j, g in enumerate((mla_q_gain, mla_k_gain)):
                        g = g[0].rearrange("(f o) -> f o", o=1)
                        col(g_mla[0:QK, j:j + 1], g)
                        col(g_mla[QK:QK + half, j:j + 1], g[NOPE + half:QK])
                        col(g_mla[QK + half:P, j:j + 1], g[NOPE:NOPE + half])
                    for dst, width, gains in ((g_chk, 4, (chk_q_gain, chk_k_gain)),
                                              (g_fox, 8, (fox_q_gain, fox_k_gain))):
                        for j, g in enumerate(gains):
                            for base in (0, 64):
                                col(dst[base:base + 64, j * width:j * width + 1],
                                    g[0].rearrange("(f o) -> f o", o=1))
                    col(b_f[:], fox_b_f[0].rearrange("(f o) -> f o", o=1))
                    act.wait_ge(small, 16 * n)
                    nc.scalar.activation(g_mla[:, 0:1], g_mla[:, 0:1], ACT.Copy, scale=float(QK) ** -0.5)
                    for t, width in ((g_chk, 4), (g_fox, 8)):
                        nc.scalar.activation(t[:, 1:width], t[:, 0:1].to_broadcast([P, width - 1]), ACT.Copy,
                                             scale=float(CHK) ** -0.5)
                        nc.scalar.activation(t[:, width + 1:2 * width],
                                             t[:, width:width + 1].to_broadcast([P, width - 1]), ACT.Copy)\
                            .then_inc(widened, 1)
                    act.wait_ge(widened, 2)
                    for k, t in enumerate((g_chk, g_fox)):
                        nc.scalar.activation(t[:, 0:1], t[:, 0:1], ACT.Copy, scale=float(CHK) ** -0.5)

                    def body(i):
                        for b in range(2):
                            t = 2 * i + b
                            act.wait_ge(turned, t + 1)
                            nc.scalar.activation(hT[:, 0:4, bass.ds(t * P, P)], xt[:, b, 0:4, :], ACT.Copy)\
                                .then_inc(from_act, 1)
                    pairs(act, 0, ST // 2, body)
                    act.wait_ge(angled, 1)
                    nc.scalar.activation(rot[64:128, :], ang[64:128, :], ACT.Sin).then_inc(sined, 1)

                @block.gpsimd
                def _(pool):
                    pool.memset(ident[:], 0.0).then_inc(made, 1)
                    pool.memset(causal[:], 0.0).then_inc(made, 1)
                    pool.wait_ge(made, 2)
                    pool.affine_select(out=ident[:], in_=ident[:], compare_op=ALU.not_equal, fill=1.0, base=0,
                                       pattern=[[-1, P]], channel_multiplier=1).then_inc(made, 1)
                    pool.affine_select(out=causal[:], in_=causal[:], compare_op=ALU.is_ge, fill=NEG, base=0,
                                       pattern=[[-1, P]], channel_multiplier=1).then_inc(made, 1)

                @block.tensor
                def _(pe):
                    pe.wait_ge(made, 3)

                    def body(i):
                        for b in range(2):
                            t = 2 * i + b
                            pe.wait_ge(loaded[b], 16 * i + 16)
                            wait(pe, from_act, t - 1)
                            wait(pe, from_dve, t - 1)
                            for k in range(KD):
                                last = nc.tensor.transpose(xt[:, b, k, :], xr[:, b, k * P:(k + 1) * P], ident[:])
                            last.then_inc(turned, 1)
                    pairs(pe, 0, ST // 2, body)

                @block.vector
                def _(dve):
                    count = [0]

                    def link(ins):
                        count[0] += 1
                        ins.then_inc(chain, 1)
                        dve.wait_ge(chain, count[0])

                    for m in (blockc, low_q):
                        nc.vector.memset(m[:], 0.0)
                    link(nc.vector.memset(high_q[:], 0.0))
                    nc.vector.memset(blockc[0:CHUNK, CHUNK:P], NEG)
                    nc.vector.memset(low_q[0:CHUNK, :], NEG)
                    nc.vector.memset(high_q[CHUNK:P, :], NEG)
                    nc.vector.memset(ind_all[:], 1.0 / D)
                    nc.vector.memset(ind_lat[:, 0:2], 1.0 / QLORA)
                    nc.vector.memset(ind_lat[:, 2:4], 1.0 / KVLORA)
                    link(nc.vector.memset(ind_head[:], 0.0))
                    nc.vector.memset(ind_head[0:64, 0:1], 1.0 / CHK)
                    nc.vector.memset(ind_head[64:128, 1:2], 1.0 / CHK)
                    link(nc.vector.memset(ind_mla[:], 1.0 / QK))
                    nc.vector.memset(ind_mla[QK:P, :], 0.0)
                    dve.wait_ge(made, 3)
                    nc.vector.tensor_copy(ident_r[:], ident[:])
                    nc.vector.tensor_copy(ident_b[:], ident[:])

                    def body(i):
                        for b in range(2):
                            t = 2 * i + b
                            dve.wait_ge(turned, t + 1)
                            nc.vector.tensor_copy(hT[:, 4:8, bass.ds(t * P, P)], xt[:, b, 4:8, :])\
                                .then_inc(from_dve, 1)
                    pairs(dve, 0, ST // 2, body)

                    dve.wait_ge(rel_in, 16)
                    far = 639 - CLIP
                    nc.vector.tensor_copy(rel_ext[:, 0:far], rel[:, 2 * CLIP:2 * CLIP + 1].to_broadcast([HEADS, far]))
                    near = 768 - far
                    nc.vector.tensor_copy(rel_ext[:, far:768], rel[:, 2 * CLIP + 1 - near:2 * CLIP + 1][:, ::-1])\
                        .then_inc(rel_out, 1)

                    r = slice(64, 128)
                    rc = slice(64, 96)
                    dve.wait_ge(pos_in, 32)
                    link(nc.vector.tensor_copy(ang[r, :], posi[r, :]))
                    link(nc.vector.tensor_scalar(ang[r, :], ang[r, :], freq[r, 0:1], None, ALU.mult))
                    magic = 1.5 * 2.0 ** 23
                    link(nc.vector.tensor_scalar(turns[r, :], ang[r, :], 1.0 / (2 * np.pi), magic, ALU.mult, ALU.add))
                    link(nc.vector.tensor_scalar(turns[r, :], turns[r, :], magic, None, ALU.subtract))
                    parts, rest = [], 2 * np.pi
                    for bits in (5, 16):
                        part = float(np.floor(rest * 2.0 ** bits) / 2.0 ** bits)
                        parts.append(part)
                        rest -= part
                    parts.append(float(rest))
                    for part in parts:
                        link(nc.vector.scalar_tensor_tensor(out=ang[r, :], in0=turns[r, :], scalar=-part,
                                                            in1=ang[r, :], op0=ALU.mult, op1=ALU.add))
                    link(nc.vector.tensor_scalar(ang[rc, :], ang[rc, :], float(np.pi / 2), None, ALU.add))
                    link(nc.vector.tensor_scalar(two_pi[rc, :], ang[rc, :], float(np.pi), 2 * float(np.pi),
                                                 ALU.is_gt, ALU.mult))
                    link(nc.vector.tensor_tensor(ang[rc, :], ang[rc, :], two_pi[rc, :], ALU.subtract))
                    nc.vector.tensor_scalar(ang[r, :], ang[r, :], float(np.float32(3.1415925)),
                                            -float(np.float32(3.1415925)), ALU.min, ALU.max).then_inc(angled, 1)

            with nc.Block() as block:
                wrote = sp.sem("wrote")

                @block.sync
                def _(sync):
                    sync.dma_start(s_rel, rel_ext[:]).then_inc(wrote, 16)
                    sync.wait_ge(wrote, 16)
                    repeated = bass.AP(tensor=s_rel.tensor, offset=0, ap=[[768, HEADS], [0, P], [1, 768]])
                    sync.dma_start(s_rep, repeated).then_inc(wrote, 16)
                    sync.wait_ge(wrote, 32)
                    for h in range(HEADS):
                        rows = bass.AP(tensor=s_rep.tensor, offset=h * P * 768 + P - 1, ap=[[767, P], [1, BAND]])
                        sync.dma_start(s_bias[h], rows).then_inc(wrote, 16)
                    sync.wait_ge(wrote, 16 * (HEADS + 2))
            sp.end()


    h_parked = G.sem("h_parked")

    def stage_norm(tag, gain, park=False):
        with ExitStack() as st:
            sp = Space(st, tag)
            norm = Norm(sp)
            sq = sp.sb("sq", [P, 2, S])
            acc = sp.sb("acc", [P, S])
            u = sp.sb("u", [P, 2, S])
            squared = sp.sem("squared")
            added = sp.sem("added")
            scaled = sp.sem("scaled")
            hi_done = sp.sem("hi_done")
            lo_pool = sp.sem("lo_pool")
            lo_dve = sp.sem("lo_dve")
            with nc.Block() as block:

                @block.sync
                def _(sync):
                    if park:
                        sync.dma_start(s_h, hT[:]).then_inc(h_parked, 16)

                @block.scalar
                def _(act):
                    for k in range(KD):
                        if k >= 3:
                            act.wait_ge(added, k - 2)
                        dst = acc[:] if k == 0 else sq[:, k % 2, :]
                        nc.scalar.activation(dst, hT[:, k, :], ACT.Square).then_inc(squared, 1)
                    norm.act_root(act, 0)
                    for k in range(KD):
                        act.wait_ge(scaled, k + 1)
                        nc.scalar.activation(a_hi[:, k, :], u[:, k % 2, :], ACT.Copy).then_inc(hi_done, 1)

                @block.tensor
                def _(pe):
                    pe.wait_ge(added, KD - 1)
                    norm.pe_sum(pe, 0, acc, ind_all[:])
                    norm.pe_rows(pe, 0)

                @block.gpsimd
                def _(pool):
                    for k in range(0, KD, 2):
                        pool.wait_ge(hi_done, k + 1)
                        nc.gpsimd.tensor_tensor(a_lo[:, k, :], u[:, k % 2, :], a_hi[:, k, :].bitcast(F32),
                                                ALU.subtract).then_inc(lo_pool, 1)

                @block.vector
                def _(dve):
                    for k in range(1, KD):
                        dve.wait_ge(squared, k + 1)
                        if k > 1:
                            dve.wait_ge(added, k - 1)
                        nc.vector.tensor_tensor(acc[:], acc[:], sq[:, k % 2, :], ALU.add).then_inc(added, 1)
                    norm.dve_invert(dve, 0)
                    norm.dve_spread(dve, 0)
                    dve.wait_ge(norm.on_rows, 1)
                    for k in range(KD):
                        if k >= 2:
                            dve.wait_ge(lo_dve if k % 2 else lo_pool, k // 2)
                        nc.vector.scalar_tensor_tensor(out=u[:, k % 2, :], in0=norm.bc[:], scalar=gain[:, k:k + 1],
                                                       in1=hT[:, k, :], op0=ALU.mult, op1=ALU.mult)\
                            .then_inc(scaled, 1)
                        if k % 2:
                            dve.wait_ge(hi_done, k + 1)
                            nc.vector.tensor_tensor(a_lo[:, k, :], u[:, k % 2, :], a_hi[:, k, :].bitcast(F32),
                                                    ALU.subtract).then_inc(lo_dve, 1)
            sp.end()

    class Weights:

        def __init__(self, sp, kt):
            self.raw = sp.sb("w_raw", [P, 2, kt, P])
            self.hi = sp.sb("w_hi", [P, 2, kt, P], F32R)
            self.lo = sp.sb("w_lo", [P, 2, kt, P], F32R)
            self.loaded = [sp.sem("w_loaded0"), sp.sem("w_loaded1")]
            self.hi_done = sp.sem("w_hi_done")
            self.lo_done = sp.sem("w_lo_done")
            self.used = sp.sem("w_used")

        def load(self, sync, c, b, pieces):
            wait(sync, self.lo_done, c - 1)
            for at, k0, src in pieces:
                n, kt = src.shape[1], src.shape[0] // P
                sync.dma_start(self.raw[:, b, k0:k0 + kt, at:at + n], src.rearrange("(k q) n -> q k n", q=P))\
                    .then_inc(self.loaded[b], 16)

        def act_hi(self, act, c, b, loaded, kt):
            act.wait_ge(self.loaded[b], loaded)
            wait(act, self.used, c - 1)
            nc.scalar.activation(self.hi[:, b, 0:kt, :], self.raw[:, b, 0:kt, :], ACT.Copy).then_inc(self.hi_done, 1)

        def dve_lo(self, dve, c, b, kt):
            dve.wait_ge(self.hi_done, c + 1)
            nc.vector.tensor_tensor(self.lo[:, b, 0:kt, :], self.raw[:, b, 0:kt, :],
                                    self.hi[:, b, 0:kt, :].bitcast(F32), ALU.subtract).then_inc(self.lo_done, 1)

        def pe_multiply(self, pe, dst, b, kts, first, last, m_hi, m_lo, k0=0):
            for k in kts:
                for w, m in ((self.hi, m_hi), (self.hi, m_lo), (self.lo, m_hi)):
                    for h in range(NH):
                        ins = nc.tensor.matmul(dst[:, h * HALF:(h + 1) * HALF], w[:, b, k0 + k, :],
                                               m[:, k, h * HALF:(h + 1) * HALF],
                                               start=(k == first and w is self.hi and m is m_hi),
                                               stop=(k == last and w is self.lo))
            return ins

    def stage_project_ab(rot):
        with ExitStack() as st:
            sp = Space(st, "pa")
            wt = Weights(sp, KD)
            norm = Norm(sp)
            acc = sp.ps("acc", [P, 2, S])
            lat = hT[:, 0:5, :]
            kr = hT[:, 5, :]
            vout = hT[:, 6:8, :]
            l_hi = sp.sb("l_hi", [P, 5, S], F32R)
            l_lo = sp.sb("l_lo", [P, 5, S], F32R)
            y = sp.sb("y", [P, 2, S])
            sq = sp.sb("sq", [P, 2, S])
            lsq = sp.sb("lsq", [P, 2, S])
            rope_t = sp.sb("rope_t", [P, S])
            acc_free = sp.sem("acc_free")
            squares = sp.sem("squares")
            copied = sp.sem("copied")
            lat_sq = sp.sem("lat_sq")
            lat_added = sp.sem("lat_added")
            lat_scaled = sp.sem("lat_scaled")
            lat_hi = sp.sem("lat_hi")
            lat_lo = sp.sem("lat_lo")
            mq_ready = sp.sem("mq_ready")
            mk_ready = sp.sem("mk_ready")
            roped = sp.sem("roped")
            stored = [sp.sem("stored0"), sp.sem("stored1")]
            v_stored = [sp.sem("v_stored0"), sp.sem("v_stored1")]
            w_in, w_uq, w_ukv = ab_w_in[0], mla_w_uq[0], mla_w_ukv[0]
            half = ROPE // 2

            def pieces(c):
                c, seg = c
                if seg == "lat":
                    return [(0, 0, w_in[:, c * P:(c + 1) * P])]
                if seg == "kr":
                    return [(0, 0, w_in[:, C_KR - 64:C_KR + ROPE]), (96, 0, w_in[:, C_KR + half:C_KR + ROPE]),
                            (96 + half, 0, w_in[:, C_KR:C_KR + half])]
                if seg == "b":
                    return [(0, 0, w_in[:, bass.ds((c - QB0) * P + C_QB, P)])]
                if seg == "ga":
                    return [(0, 0, w_in[:, bass.ds((c - GB1) * P + C_GA, P)])]
                if seg == "mq":
                    o = (c - GA1) * QK
                    return [(0, 0, w_uq[:, bass.ds(o, QK)]), (QK, 0, w_uq[:, bass.ds(o + NOPE + half, half)]),
                            (QK + half, 0, w_uq[:, bass.ds(o + NOPE, half)])]
                return [(0, 0, w_ukv[:, bass.ds((c - MQ1) * P, P)])]

            SEGS = [("lat", 0, KR), ("kr", KR, QB0), ("b", QB0, GB1), ("ga", GB1, GA1), ("mq", GA1, MQ1),
                    ("mk", MQ1, MK1)]

            def seg_at(c):
                return next(s for s, a, z in SEGS if a <= c < z)

            def kt_of(seg):
                return {"mq": QLORA // P, "mk": KVLORA // P}.get(seg, KD)

            def loaded(c, b, seg):
                i = (c - b) // 2 if isinstance(c, int) else c[1]
                c = c if isinstance(c, int) else c[0]
                extra = 0
                if seg in ("kr", "b", "ga", "mq", "mk") and b == 1:
                    extra += 32
                if seg == "mq":
                    return 16 + 16 * i + extra + 32 * (i + 1) - 32 * (GA1 // 2)
                if seg == "mk":
                    extra += 32 * (MQ1 - GA1) // 2
                return 16 + 16 * i + extra

            LOOPS = [("qk", QB0 // 2, QB1 // 2), ("v", QB1 // 2, VB1 // 2), ("g", VB1 // 2, GA1 // 2),
                     ("mq", GA1 // 2, MQ1 // 2), ("mk", MQ1 // 2, MK1 // 2)]

            def loop(eng, lo, hi, body, edges):
                i = lo
                while i < hi:
                    if i in edges:
                        body(i)
                        i += 1
                        continue
                    end = i
                    while end < hi and end not in edges:
                        end += 1
                    if end - i == 1:
                        body(i)
                    else:
                        with eng.Fori(i, end) as r:
                            body(r)
                    i = end

            EDGES = {QB0 // 2, QB1 // 2, VB1 // 2, GB1 // 2, GA1 // 2, MQ1 // 2,
                     GB1 // 2 - 1, GA1 // 2 - 1, MQ1 // 2 - 1, MK1 // 2 - 1}

            def seg_for(kind, i, ahead):
                if isinstance(i, int):
                    c = 2 * (i + ahead)
                    return seg_at(c) if c < MK1 else None
                return {"qk": "b", "v": "b", "g": "ga" if kind == "g" else "b", "mq": "mq", "mk": "mk"}[kind]

            with nc.Block() as block:

                @block.sync
                def _(sync):
                    def load(c, i, b, seg):
                        wt.load(sync, c, b, pieces((c, seg)))

                    def load_ahead(kind, i, b):
                        seg = seg_for(kind, i, 1)
                        if isinstance(i, int) and 2 * i + 2 + b == KR:
                            seg = "kr"
                        if seg:
                            load(2 * i + 2 + b, i, b, seg)

                    load(0, 0, 0, "lat")
                    load(1, 0, 1, "lat")
                    for i in range(QB0 // 2):
                        for b in range(2):
                            load_ahead("lat", i, b)

                    def segment(kind, lo, hi):
                        def body(i):
                            for b in range(2):
                                c = 2 * i + b
                                load_ahead(kind, i, b)
                                if kind == "qk":
                                    sync.wait_ge(norm.applied, c - 4 + 1)
                                    sync.dma_start(s_ab[bass.ds(c - QB0, 1)].rearrange("o q n -> (o q) n"), y[:, b, :])\
                                        .then_inc(stored[b], 16)
                                elif kind in ("v", "g"):
                                    sync.wait_ge(acc_free, c + 1)
                                    sync.dma_start(s_ab[bass.ds(c - QB0, 1)].rearrange("o q n -> (o q) n"), y[:, b, :])\
                                        .then_inc(stored[b], 16)
                                elif kind == "mq":
                                    sync.wait_ge(mq_ready, c - GA1 + 1)
                                    sync.dma_start(s_mq[bass.ds(c - GA1, 1)].rearrange("o q n -> (o q) n"), y[0:QK, b, :])\
                                        .then_inc(stored[b], 16)
                                else:
                                    sync.wait_ge(acc_free, c + 1)
                                    sync.dma_start(s_mv[bass.ds(c - MQ1, 1)].rearrange("o q n -> (o q) n"), vout[64:128, b, :])\
                                        .then_inc(v_stored[b], 16)
                                    sync.wait_ge(mk_ready, c - MQ1 + 1)
                                    sync.dma_start(s_mk[bass.ds(c - MQ1, 1)].rearrange("o q n -> (o q) n"), y[0:QK, b, :])\
                                        .then_inc(stored[b], 16)
                        loop(sync, lo, hi, body, EDGES)

                    for kind, lo, hi in LOOPS:
                        segment(kind, lo, hi)
                    for b in range(2):
                        sync.wait_ge(stored[b], 16 * (MK1 - QB0) // 2)
                        sync.wait_ge(v_stored[b], 16 * (MK1 - MQ1) // 2)

                @block.scalar
                def _(act):
                    def split(i, b, kind):
                        seg = seg_for(kind, i, 1)
                        if isinstance(i, int) and 2 * i + 2 + b == KR:
                            seg = "kr"
                        if seg:
                            c = 2 * i + 2 + b
                            wt.act_hi(act, c, b, loaded(c, b, seg) if isinstance(i, int)
                                      else loaded((c, i + 1), b, seg), kt_of(seg))

                    def to_y(i, b):
                        wait(act, stored[b], 16 * i - 16 * (QB0 // 2))

                    wt.act_hi(act, 0, 0, 16, KD)
                    wt.act_hi(act, 1, 1, 16, KD)
                    act.wait_ge(h_parked, 16)
                    for c in range(QB0):
                        act.wait_ge(wt.used, c + 1)
                        if c < KR:
                            j = 0 if c < LAT_KV else 1
                            first = c in (LAT_Q, LAT_KV)
                            if not first:
                                wait(act, lat_added, {1: 0, 2: 1, 4: 2}[c])
                            dst = lsq[:, j, :] if first else sq[:, 0, :]
                            nc.scalar.activation(dst, acc[:, c % 2, :], ACT.Square).then_inc(lat_sq, 1)
                            nc.scalar.activation(lat[:, c, :], acc[:, c % 2, :], ACT.Copy).then_inc(acc_free, 1)
                        else:
                            nc.scalar.activation(kr[64:128, :], acc[64:128, c % 2, :], ACT.Copy).then_inc(acc_free, 1)
                        split(c // 2, c % 2, "lat")
                        if c == LAT_KV:
                            norm.act_root(act, 0)

                    def lat_split(k):
                        act.wait_ge(lat_scaled, k + 1)
                        nc.scalar.activation(l_hi[:, k, :], lat[:, k, :], ACT.Copy).then_inc(lat_hi, 1)

                    for k in range(LAT_KV):
                        lat_split(k)

                    def segment(kind, lo, hi):
                        def body(i):
                            for b in range(2):
                                c = 2 * i + b
                                if kind in ("qk", "mq"):
                                    act.wait_ge(wt.used, c + 1)
                                    to_y(i, b)
                                    if isinstance(i, int) and c == QB0:
                                        act.wait_ge(lat_added, 3)
                                    wait(act, norm.summed, c - (4 if kind == "qk" else 16) - 1)
                                    nc.scalar.activation(sq[:, b, :], acc[:, b, :], ACT.Square).then_inc(squares, 1)
                                    nc.scalar.activation(y[:, b, :], acc[:, b, :], ACT.Copy).then_inc(acc_free, 1)
                                    if isinstance(i, int) and c == QB0:
                                        norm.act_root(act, 1)
                                        for k in range(LAT_KV, 5):
                                            lat_split(k)
                                    norm.act_root(act, c - (4 if kind == "qk" else 16))
                                elif kind in ("v", "g"):
                                    act.wait_ge(wt.used, c + 1)
                                    to_y(i, b)
                                    nc.scalar.activation(y[:, b, :], acc[:, b, :], ACT.Copy if kind == "v" else ACT.Silu)\
                                        .then_inc(acc_free, 1)
                                else:
                                    to_y(i, b)
                                    nc.scalar.activation(y[64:128, b, :], kr[64:128, :], ACT.Copy).then_inc(copied, 1)
                                    act.wait_ge(wt.used, c + 1)
                                    nc.scalar.activation(y[0:64, b, :], acc[0:64, b, :], ACT.Copy).then_inc(copied, 1)
                                    wait(act, v_stored[b], 16 * i - 16 * (MQ1 // 2))
                                    nc.scalar.activation(vout[64:128, b, :], acc[64:128, b, :], ACT.Copy)\
                                        .then_inc(acc_free, 1)
                                    act.wait_ge(copied, 2 * (c - MQ1) + 2)
                                    wait(act, norm.summed, c - 16 - 1)
                                    nc.scalar.activation(sq[:, b, :], y[:, b, :], ACT.Square).then_inc(squares, 1)
                                    norm.act_root(act, c - 16)
                                split(i, b, kind)
                        loop(act, lo, hi, body, EDGES)

                    for kind, lo, hi in LOOPS:
                        segment(kind, lo, hi)

                @block.tensor
                def _(pe):
                    def main(c, b, seg, mid=None, end=None):
                        kt = kt_of(seg)
                        m_hi, m_lo = (a_hi, a_lo)
                        if seg == "mq":
                            m_hi, m_lo = l_hi[:, 0:3], l_lo[:, 0:3]
                        if seg == "mk":
                            m_hi, m_lo = l_hi[:, 3:5], l_lo[:, 3:5]
                        pe.wait_ge(wt.lo_done, c + 1)
                        wait(pe, acc_free, c - 1)
                        cut = (kt + 1) // 2
                        wt.pe_multiply(pe, acc[:, b, :], b, range(cut), 0, kt - 1, m_hi, m_lo)
                        if mid:
                            mid()
                        wt.pe_multiply(pe, acc[:, b, :], b, range(cut, kt), 0, kt - 1, m_hi, m_lo)\
                            .then_inc(wt.used, 1)
                        if end:
                            end()

                    def ss_lat(n):
                        pe.wait_ge(lat_added, 2 + n)
                        norm.pe_sum(pe, n, lsq[:, n, :], ind_lat[:, 2 * n:2 * n + 2])

                    for c in range(QB0):
                        if c == LAT_KV + 1:
                            main(c, c % 2, seg_at(c), lambda: ss_lat(0), lambda: norm.pe_rows(pe, 0))
                        else:
                            main(c, c % 2, seg_at(c))

                    def hooks(kind, c, b):
                        n = c - (4 if kind == "qk" else 16)
                        ind = ind_head if kind == "qk" else ind_mla
                        done = c - (QB0 if kind == "qk" else GA1 - 8) + 1

                        def mid():
                            pe.wait_ge(squares, done)
                            norm.pe_sum(pe, n, sq[:, b, :], ind[:])
                        return mid, lambda: norm.pe_rows(pe, n)

                    def segment(kind, lo, hi):
                        def body(i):
                            for b in range(2):
                                c = 2 * i + b
                                mid = end = None
                                if isinstance(i, int) and c == QB0:
                                    mid, end = (lambda: ss_lat(1)), (lambda: norm.pe_rows(pe, 1))
                                elif isinstance(i, int) and c == QB1:
                                    mid, end = hooks("qk", c - 1, 1 - b)
                                elif isinstance(i, int) and c == GA1:
                                    pe.wait_ge(lat_lo, 5)
                                elif kind in ("qk", "mq", "mk"):
                                    mid, end = hooks(kind, c - 1, 1 - b)
                                main(c, b, seg_for(kind, i, 0), mid, end)
                        loop(pe, lo, hi, body, EDGES)

                    for kind, lo, hi in LOOPS:
                        segment(kind, lo, hi)
                    mid, end = hooks("mk", MK1 - 1, 1)
                    mid()
                    end()

                @block.vector
                def _(dve):
                    def split(i, b, kind):
                        seg = seg_for(kind, i, 1)
                        if isinstance(i, int) and 2 * i + 2 + b == KR:
                            seg = "kr"
                        if seg:
                            wt.dve_lo(dve, 2 * i + 2 + b, b, kt_of(seg))

                    def lat_norm(n, ks):
                        dve.wait_ge(norm.on_rows, n + 1)
                        for k in ks:
                            nc.vector.scalar_tensor_tensor(out=lat[:, k, :], in0=norm.bc[:], scalar=g_lat[:, k:k + 1],
                                                           in1=lat[:, k, :], op0=ALU.mult, op1=ALU.mult)\
                                .then_inc(lat_scaled, 1)
                        dve.wait_ge(lat_scaled, ks[-1] + 1)
                        dve.sem_inc(norm.applied, 1)
                        for k in ks:
                            dve.wait_ge(lat_hi, k + 1)
                            nc.vector.tensor_tensor(l_lo[:, k, :], lat[:, k, :], l_hi[:, k, :].bitcast(F32),
                                                    ALU.subtract).then_inc(lat_lo, 1)

                    wt.dve_lo(dve, 0, 0, KD)
                    wt.dve_lo(dve, 1, 1, KD)
                    added = 0
                    for c in range(QB0):
                        if c < KR and c not in (LAT_Q, LAT_KV):
                            j = 0 if c < LAT_KV else 1
                            dve.wait_ge(lat_sq, c + 1)
                            wait(dve, lat_added, added)
                            nc.vector.tensor_tensor(lsq[:, j, :], lsq[:, j, :], sq[:, 0, :], ALU.add)\
                                .then_inc(lat_added, 1)
                            added += 1
                        split(c // 2, c % 2, "lat")
                        if c == LAT_KV:
                            norm.dve_invert(dve, 0)
                            norm.dve_spread(dve, 0)
                    lat_norm(0, [0, 1, 2])

                    def segment(kind, lo, hi):
                        def body(i):
                            for b in range(2):
                                c = 2 * i + b
                                if kind not in ("qk", "mq", "mk"):
                                    split(i, b, kind)
                                    continue
                                if isinstance(i, int) and c == QB0:
                                    norm.dve_invert(dve, 1)
                                    norm.dve_spread(dve, 1)
                                    lat_norm(1, [3, 4])
                                n = c - (4 if kind == "qk" else 16)
                                norm.dve_invert(dve, n)
                                norm.dve_spread(dve, n)
                                split(i, b, kind)
                                dve.wait_ge(norm.on_rows, n + 1)
                                gain = g_chk[:, bass.ds(c - QB0, 1)] if kind == "qk" else \
                                    g_mla[:, 0:1] if kind == "mq" else g_mla[:, 1:2]
                                ins = nc.vector.scalar_tensor_tensor(out=y[:, b, :], in0=norm.bc[:], scalar=gain,
                                                                     in1=y[:, b, :], op0=ALU.mult, op1=ALU.mult)
                                ins.then_inc(norm.applied, 1)
                                if kind == "qk":
                                    continue
                                dve.wait_ge(norm.applied, n + 1)
                                nc.vector.tensor_tensor(rope_t[64:96, :], y[96:128, b, :], rot[96:128, :], ALU.mult)\
                                    .then_inc(roped, 1)
                                nc.vector.tensor_tensor(y[64:96, b, :], y[64:96, b, :], rot[64:96, :], ALU.mult)\
                                    .then_inc(roped, 1)
                                dve.wait_ge(roped, 2 * (c - GA1) + 2)
                                nc.vector.tensor_tensor(y[64:96, b, :], y[64:96, b, :], rope_t[64:96, :], ALU.add)\
                                    .then_inc(mq_ready if kind == "mq" else mk_ready, 1)
                        loop(dve, lo, hi, body, EDGES)

                    for kind, lo, hi in LOOPS:
                        segment(kind, lo, hi)
            sp.end()

    def stage_project_fox():
        with ExitStack() as st:
            sp = Space(st, "pf")
            NQK, NALL = 2 * FH // 2, 4 * FH // 2
            wt = Weights(sp, KD)
            norm = Norm(sp)
            acc = sp.ps("acc", [P, 2, S])
            y = sp.sb("y", [P, 2, S])
            sq = sp.sb("sq", [P, 2, S])
            z = sp.sb("z", [FH, S])
            e = sp.sb("e", [FH, S])
            ones = sp.sb("ones", [FH, S])
            neg_cum = sp.sb("neg_cum", [FH, S])
            acc_free = sp.sem("acc_free")
            squares = sp.sem("squares")
            gate_act = sp.sem("gate_act")
            gate_dve = sp.sem("gate_dve")
            stored = [sp.sem("stored0"), sp.sem("stored1")]
            cum_stored = sp.sem("cum_stored")
            w = fox_w_in[0]
            with nc.Block() as block:

                def run(eng, lo, hi, body):
                    body(lo)
                    if hi - lo > 3:
                        with eng.Fori(lo + 1, hi - 1) as i:
                            body(i)
                    else:
                        for i in range(lo + 1, hi - 1):
                            body(i)
                    body(hi - 1)

                @block.sync
                def _(sync):
                    def load(c, b):
                        wt.load(sync, c, b, [(0, 0, w[:, bass.ds(c * P, P)])])

                    load(0, 0)
                    load(1, 1)

                    def segment(lo, hi):
                        def body(i):
                            for b in range(2):
                                c = 2 * i + b
                                if isinstance(i, int) and c + 2 >= NALL:
                                    if c + 2 == NALL:
                                        wt.load(sync, c + 2, b, [(0, 0, w[:, NALL * P:NALL * P + FH])])
                                else:
                                    load(c + 2, b)
                                sync.wait_ge(norm.applied if hi <= NQK // 2 else acc_free, c + 1)
                                sync.dma_start(s_fox[bass.ds(c, 1)].rearrange("o q n -> (o q) n"), y[:, b, :])\
                                    .then_inc(stored[b], 16)
                        run(sync, lo, hi, body)
                    segment(0, NQK // 2)
                    segment(NQK // 2, NALL // 2)
                    sync.wait_ge(gate_dve, 3)
                    sync.dma_start(s_cum, neg_cum[:]).then_inc(cum_stored, 16)
                    sync.wait_ge(cum_stored, 16)
                    for b in range(2):
                        sync.wait_ge(stored[b], 16 * NALL // 2)

                @block.scalar
                def _(act):
                    def hi_of(i, b):
                        c = 2 * i + b
                        if not isinstance(i, int) or c <= NALL:
                            wt.act_hi(act, c, b, 16 * i + 16, KD)

                    hi_of(0, 0)
                    hi_of(0, 1)

                    def segment(kind, lo, hi):
                        def body(i):
                            for b in range(2):
                                c = 2 * i + b
                                act.wait_ge(wt.used, c + 1)
                                if kind == "qk":
                                    wait(act, norm.summed, c - 1)
                                    nc.scalar.activation(sq[:, b, :], acc[:, b, :], ACT.Square).then_inc(squares, 1)
                                wait(act, stored[b], 16 * i)
                                nc.scalar.activation(y[:, b, :], acc[:, b, :], ACT.Silu if kind == "g" else ACT.Copy)\
                                    .then_inc(acc_free, 1)
                                if kind == "qk":
                                    norm.act_root(act, c)
                                hi_of(i + 1, b)
                        run(act, lo, hi, body)
                    segment("qk", 0, NQK // 2)
                    segment("v", NQK // 2, 3 * NALL // 8)
                    segment("g", 3 * NALL // 8, NALL // 2)
                    act.wait_ge(wt.used, NALL + 1)
                    nc.scalar.activation(z[:], acc[0:FH, 0, :], ACT.Identity, bias=b_f[:]).then_inc(gate_act, 1)
                    act.wait_ge(gate_act, 1)
                    nc.scalar.activation(e[:], z[:], ACT.Abs).then_inc(gate_act, 1)
                    act.wait_ge(gate_act, 2)
                    nc.scalar.activation(e[:], e[:], ACT.Exp, scale=-1.0).then_inc(gate_act, 1)
                    act.wait_ge(gate_act, 3)
                    nc.scalar.activation(e[:], e[:], ACT.Ln, bias=1.0).then_inc(gate_act, 1)

                @block.tensor
                def _(pe):
                    def main(c, b, mid, end):
                        pe.wait_ge(wt.lo_done, c + 1)
                        wait(pe, acc_free, c - 1)
                        wt.pe_multiply(pe, acc[:, b, :], b, range(KD // 2), 0, KD - 1, a_hi, a_lo)
                        if mid:
                            mid()
                        wt.pe_multiply(pe, acc[:, b, :], b, range(KD // 2, KD), 0, KD - 1, a_hi, a_lo)\
                            .then_inc(wt.used, 1)
                        if end:
                            end()

                    def segment(kind, lo, hi):
                        def body(i):
                            for b in range(2):
                                c = 2 * i + b
                                mid = end = None
                                first = isinstance(i, int) and i == lo and b == 0
                                if (kind == "qk") != first:

                                    def mid():
                                        pe.wait_ge(squares, c)
                                        norm.pe_sum(pe, c - 1, sq[:, 1 - b, :], ind_head[:])

                                    def end():
                                        norm.pe_rows(pe, c - 1)
                                main(c, b, mid, end)
                        run(pe, lo, hi, body)
                    segment("qk", 0, NQK // 2)
                    segment("vg", NQK // 2, NALL // 2)
                    main(NALL, 0, None, None)

                @block.vector
                def _(dve):
                    def lo_of(i, b):
                        c = 2 * i + b
                        if not isinstance(i, int) or c <= NALL:
                            wt.dve_lo(dve, c, b, KD)

                    nc.vector.memset(ones[:], 1.0)
                    lo_of(0, 0)
                    lo_of(0, 1)

                    def segment(kind, lo, hi):
                        def body(i):
                            for b in range(2):
                                c = 2 * i + b
                                if kind == "qk":
                                    norm.dve_invert(dve, c)
                                    norm.dve_spread(dve, c)
                                lo_of(i + 1, b)
                                if kind == "qk":
                                    dve.wait_ge(norm.on_rows, c + 1)
                                    nc.vector.scalar_tensor_tensor(out=y[:, b, :], in0=norm.bc[:],
                                                                   scalar=g_fox[:, bass.ds(c, 1)], in1=y[:, b, :],
                                                                   op0=ALU.mult, op1=ALU.mult)\
                                        .then_inc(norm.applied, 1)
                        run(dve, lo, hi, body)
                    segment("qk", 0, NQK // 2)
                    segment("vg", NQK // 2, NALL // 2)
                    dve.wait_ge(gate_act, 4)
                    nc.vector.tensor_scalar(z[:], z[:], 0.0, None, ALU.min).then_inc(gate_dve, 1)
                    dve.wait_ge(gate_dve, 1)
                    nc.vector.tensor_tensor(e[:], e[:], z[:], ALU.subtract).then_inc(gate_dve, 1)
                    dve.wait_ge(gate_dve, 2)
                    nc.vector.tensor_tensor_scan(neg_cum[:], ones[:], e[:], 0.0, ALU.mult, ALU.add)\
                        .then_inc(gate_dve, 1)
            sp.end()

    def stage_attention(kind, heads, first_pair, q_of, k_of, v_of, g_of, extra_of):
        mla, chk, fox = (kind == k for k in ("mla", "chk", "fox"))
        NT = ST
        NP2 = heads // 2

        def lowest(t):
            return max(0, t - BAND // P + 1) if chk else 0

        def turned(t):
            js = list(range(lowest(t), t + 1))
            return [js[n:n + 4] for n in range(0, len(js), 4)]

        PIECES = [len(turned(t)) for t in range(NT)]
        BEFORE = [sum(PIECES[:t]) for t in range(NT + 1)]
        NPC = BEFORE[NT]
        assert NPC % 2 == 0

        with ExitStack() as st:
            sp = Space(st, kind)
            raw = sp.sb("raw", [P, 2, S])
            q_hi = sp.sb("q_hi", [P, 2, S], F32R)
            k_hi = sp.sb("k_hi", [P, 2, S], F32R)
            k_lo = sp.sb("k_lo", [P, 2, S], F32R)
            q_lo = sp.sb("q_lo", [P, 2, S], F32R) if mla else None
            extra = None if mla else sp.sb("extra", [P, 2, BAND if chk else S])
            v_raw = sp.sb("v_raw", [64, S])
            v = sp.sb("v", [P, 2, ST, P], F32R)
            gate = sp.sb("gate", [P, S])
            o = sp.sb("o", [P, S])
            o_low = sp.sb("o_low", [64, 2 * P])
            WIDE = BAND if chk else S
            prob = sp.sb("prob", [P, 4, WIDE])
            pt_hi = sp.sb("pt_hi", [P, 2, WIDE // P + chk, 2 * P], F32R)
            pt_lo = sp.sb("pt_lo", [P, 2, WIDE // P + chk, 2 * P], F32R)
            neg_max = sp.sb("neg_max", [P, 4])
            total = sp.sb("total", [P, 4])
            inverse = sp.sb("inverse", [P, 4])
            spare = sp.sb("spare", [P, 1])
            scores = sp.ps("scores", [P, 2, S])
            turn = sp.ps("turn", [P, 2, 4, P])
            pv = sp.ps("pv", [P, 2 * P])
            vt = sp.ps("vt", [P, ST, 64])

            in_q, in_k, in_v = sp.sem("in_q"), sp.sem("in_k"), sp.sem("in_v")
            in_g = [sp.sem("in_g0"), sp.sem("in_g1")]
            in_x = [sp.sem("in_x0"), sp.sem("in_x1")]
            q_hi_done, q_lo_done = sp.sem("q_hi_done"), sp.sem("q_lo_done")
            k_hi_done, k_lo_done = sp.sem("k_hi_done"), sp.sem("k_lo_done")
            v_turned, v_hi_done, v_lo_done = sp.sem("v_turned"), sp.sem("v_hi_done"), sp.sem("v_lo_done")
            scored = sp.sem("scored")
            maxed = sp.sem("maxed")
            exped = sp.sem("exped")
            inverted = sp.sem("inverted")
            normed = sp.sem("normed")
            pieces_turned = sp.sem("pieces_turned")
            pt_hi_done, pt_lo_done = sp.sem("pt_hi_done"), sp.sem("pt_lo_done")
            pv_done = sp.sem("pv_done")
            o_low_done, o_done = sp.sem("o_low_done"), sp.sem("o_done")
            gated, out_hi, out_lo = sp.sem("gated"), sp.sem("out_hi"), sp.sem("out_lo")
            NDMA = 1 if mla else 2
            KROWS = QK if mla else P

            def over_heads(eng, head, tail=None):
                def body(i, final=False):
                    for b in range(2):
                        head(i, b, 2 * i + b, final and b == 1)
                body(0)
                if NP2 > 3:
                    with eng.Fori(1, NP2 - 1) as i:
                        body(i)
                else:
                    for i in range(1, NP2 - 1):
                        body(i)
                body(NP2 - 1, True)

            with nc.Block() as block:

                @block.sync
                def _(sync):
                    def load(hd, b, m):
                        for dst, src, sem, done in ((0, q_of(hd), in_q, q_lo_done), (1, k_of(hd), in_k, k_lo_done)):
                            wait(sync, done, hd)
                            rows = src.shape[0]
                            for n in range(NDMA):
                                sync.dma_start(raw[n * rows:(n + 1) * rows, dst, :], src).then_inc(sem, 16)
                        wait(sync, v_turned, hd)
                        sync.dma_start(v_raw[:], v_of(hd)).then_inc(in_v, 16)
                        if extra is not None:
                            wait(sync, maxed, NT * (hd - 1))
                            sync.dma_start(extra[:, b, :], extra_of(hd)).then_inc(in_x[b], 16)
                        wait(sync, gated, hd - 1)
                        sync.dma_start(gate[64 * b:64 * b + 64, :], g_of(hd)).then_inc(in_g[b], 16)

                    load(0, 0, 0)

                    def head(i, b, hd, last):
                        if not last:
                            load(hd + 1, 1 - b, i + b)
                    over_heads(sync, head)

                def lo_slices():
                    return (q_lo, slice(0, QK)) if mla else (q_hi, slice(64, P))

                @block.scalar
                def _(act):
                    def split_q(hd, b):
                        act.wait_ge(in_q, 16 * NDMA * (hd + 1))
                        wait(act, scored, NT * (hd - 1))
                        nc.scalar.activation(q_hi[0:KROWS, b, :], raw[0:KROWS, 0, :], ACT.Copy).then_inc(q_hi_done, 1)

                    def split_k(hd, b):
                        act.wait_ge(in_k, 16 * NDMA * (hd + 1))
                        nc.scalar.activation(k_hi[0:KROWS, b, :], raw[0:KROWS, 1, :], ACT.Copy).then_inc(k_hi_done, 1)

                    def split_v(hd, b):
                        act.wait_ge(v_turned, hd + 1)
                        wait(act, pv_done, NT // 2 * (hd - 1))
                        nc.scalar.activation(v[:, b, :, 0:64], vt[:], ACT.Copy).then_inc(v_hi_done, 1)

                    def evacuate(hd, t):
                        for n, js in enumerate(turned(t)):
                            g = BEFORE[t] + n
                            u = t // 2
                            act.wait_ge(pieces_turned, NPC * hd + g + 1)
                            wait(act, pv_done, NT // 2 * hd + u - 1)
                            at = js[0] - lowest(2 * u)
                            nc.scalar.activation(pt_hi[:, u % 2, at:at + len(js), (t % 2) * P:(t % 2 + 1) * P],
                                                 turn[:, g % 2, 0:len(js), :], ACT.Copy).then_inc(pt_hi_done, 1)

                    def low_half(hd, u):
                        act.wait_ge(pv_done, NT // 2 * hd + u + 1)
                        wait(act, o_done, NT // 2 * hd + u)
                        nc.scalar.activation(o_low[:], pv[64:P, :], ACT.Copy).then_inc(o_low_done, 1)

                    def give(m, b, hd):
                        act.wait_ge(gated, hd + 1)
                        r = slice(64 * b, 64 * b + 64)
                        nc.scalar.activation(a_hi[r, bass.ds(m + first_pair, 1), :].rearrange("q o n -> q (o n)"), o[r, :],
                                             ACT.Copy).then_inc(out_hi, 1)

                    split_q(0, 0)
                    split_k(0, 0)
                    split_v(0, 0)

                    def head(i, b, hd, last):
                        for t in range(NT):
                            before = hd if t >= 2 else hd - 1
                            if not (isinstance(hd, int) and before < 0):
                                evacuate(before, (t - 2) % NT)
                            s = NT * hd + t
                            act.wait_ge(maxed, s + 1)
                            n = (t + 1 - lowest(t)) * P
                            src = scores[:, t % 2, 0:n] if mla else prob[:, t % 4, 0:n]
                            if mla:
                                wait(act, pieces_turned, NPC * hd + BEFORE[t - 4] + PIECES[t - 4] if t >= 4 else
                                     NPC * (hd - 1) + BEFORE[t + NT - 4] + PIECES[t + NT - 4])
                            nc.scalar.activation(prob[:, t % 4, 0:n], src, ACT.Exp, bias=neg_max[:, t % 4:t % 4 + 1],
                                                 scale=1.0 if mla else -1.0,
                                                 accum_out=total[:, t % 4:t % 4 + 1]).then_inc(exped, 1)
                            if t % 2 == 0:
                                if t >= 4:
                                    low_half(hd, (t - 4) // 2)
                                elif not (isinstance(hd, int) and hd == 0):
                                    low_half(hd - 1, (t + NT - 4) // 2)
                            if t == 3 and not (isinstance(hd, int) and hd == 0):
                                give(i - 1 + b, 1 - b, hd - 1)
                            if not last:
                                if t == 1:
                                    split_q(hd + 1, 1 - b)
                                if t == 3:
                                    split_k(hd + 1, 1 - b)
                                if t == 5:
                                    split_v(hd + 1, 1 - b)
                    over_heads(act, head)
                    hd = heads - 1
                    evacuate(hd, NT - 2)
                    low_half(hd, NT // 2 - 2)
                    evacuate(hd, NT - 1)
                    low_half(hd, NT // 2 - 1)
                    give(NP2 - 1, 1, hd)

                @block.gpsimd
                def _(pool):
                    def split(hd, b):
                        dst, r = lo_slices()
                        wait(pool, out_lo, hd - 1)
                        pool.wait_ge(q_hi_done, hd + 1)
                        nc.gpsimd.tensor_tensor(dst[r, b, :], raw[r, 0, :], q_hi[r, b, :].bitcast(F32), ALU.subtract)\
                            .then_inc(q_lo_done, 1)
                        pool.wait_ge(q_lo_done, hd + 1)
                        pool.wait_ge(k_hi_done, hd + 1)
                        nc.gpsimd.tensor_tensor(k_lo[0:KROWS, b, :], raw[0:KROWS, 1, :],
                                                k_hi[0:KROWS, b, :].bitcast(F32), ALU.subtract).then_inc(k_lo_done, 1)

                    def give(m, b, hd):
                        r = slice(64 * b, 64 * b + 64)
                        pool.wait_ge(k_lo_done, hd + 1)
                        pool.wait_ge(o_done, NT // 2 * (hd + 1))
                        pool.wait_ge(in_g[b], 16 * (m + 1))
                        nc.gpsimd.tensor_tensor(o[r, :], o[r, :], gate[r, :], ALU.mult).then_inc(gated, 1)
                        pool.wait_ge(gated, hd + 1)
                        pool.wait_ge(out_hi, hd + 1)
                        at = bass.ds(m + first_pair, 1)
                        nc.gpsimd.tensor_tensor(a_lo[r, at, :].rearrange("q o n -> q (o n)"), o[r, :],
                                                a_hi[r, at, :].rearrange("q o n -> q (o n)").bitcast(F32),
                                                ALU.subtract).then_inc(out_lo, 1)

                    split(0, 0)

                    def head(i, b, hd, last):
                        if not (isinstance(hd, int) and hd == 0):
                            give(i - 1 + b, 1 - b, hd - 1)
                        if not last:
                            split(hd + 1, 1 - b)
                    over_heads(pool, head)
                    give(NP2 - 1, 1, heads - 1)

                @block.tensor
                def _(pe):
                    def before_turn_v(hd):
                        pe.wait_ge(in_v, 16 * (hd + 1))
                        wait(pe, v_lo_done, hd)

                    def turn_v(hd):
                        for j in range(ST):
                            last = nc.tensor.transpose(vt[:, j, :], v_raw[:, j * P:(j + 1) * P], ident[0:64, 0:64])
                        last.then_inc(v_turned, 1)

                    def score(hd, b, t):
                        s = NT * hd + t
                        if t == 0:
                            pe.wait_ge(q_lo_done, hd + 1)
                            pe.wait_ge(k_lo_done, hd + 1)
                        wait(pe, exped if mla else maxed, s - 1)
                        lo = lowest(t)
                        n = (t + 1 - lo) * P
                        q = slice(t * P, (t + 1) * P)
                        for c in range(0, n, HALF):
                            w = min(HALF, n - c)
                            dst = scores[:, t % 2, c:c + w]
                            keys = slice(lo * P + c, lo * P + c + w)
                            R = slice(0, KROWS)
                            terms = [(q_hi, k_hi), (q_lo, k_hi), (q_hi, k_lo)] if mla else [(q_hi, k_hi), (q_hi, k_lo)]
                            masks = []
                            if c + w == n:
                                if chk:
                                    masks.append((slice(w - CHUNK, w), low_q))
                                else:
                                    masks.append((slice(w - P, w), causal if fox else blockc))
                            if chk and c == 0 and t >= BAND // P - 1:
                                masks.append((slice(0, CHUNK), high_q))
                            for m, (a, k) in enumerate(terms):
                                ins = nc.tensor.matmul(dst, a[R, b, q], k[R, b, keys], start=(m == 0),
                                                       stop=(m == len(terms) - 1))
                                if m == 0:
                                    for cols, mask in masks:
                                        nc.tensor.matmul(dst[:, cols], ident_b[:], mask[:], start=False, stop=False)
                        ins.then_inc(scored, 1)

                    def turn_p(hd, t):
                        pe.wait_ge(normed, NT * hd + t + 1)
                        lo = lowest(t)
                        for n, js in enumerate(turned(t)):
                            g = BEFORE[t] + n
                            wait(pe, pt_lo_done, NPC * hd + g - 1)
                            for m, j in enumerate(js):
                                last = nc.tensor.transpose(turn[:, g % 2, m, :], prob[:, t % 4, (j - lo) * P:(j - lo + 1) * P],
                                                           ident[:])
                            last.then_inc(pieces_turned, 1)

                    def times_v(hd, b, u):
                        pe.wait_ge(pt_lo_done, NPC * hd + BEFORE[2 * u + 2])
                        wait(pe, o_done, NT // 2 * hd + u)
                        if u == 0:
                            pe.wait_ge(v_lo_done, hd + 1)
                        lo0, lo1 = lowest(2 * u), lowest(2 * u + 1)
                        js = [j for j in range(lo1, 2 * u + 1)] + [2 * u + 1] + list(range(lo0, lo1))
                        terms = [(j, part) for j in js for part in (pt_hi, pt_lo)]
                        for m, (j, part) in enumerate(terms):
                            cols = slice(P, 2 * P) if j == 2 * u + 1 else slice(0, P) if j < lo1 else slice(0, 2 * P)
                            ins = nc.tensor.matmul(pv[:, cols], v[:, b, j, :], part[:, u % 2, j - lo0, cols],
                                                   start=(m == 0), stop=(m == len(terms) - 1))
                        ins.then_inc(pv_done, 1)

                    before_turn_v(0)
                    turn_v(0)

                    def head(i, b, hd, last):
                        first = isinstance(hd, int) and hd == 0
                        for t in range(NT):
                            score(hd, b, t)
                            if t >= 4 and t % 2 == 0:
                                times_v(hd, b, t // 2 - 2)
                            if t in (0, 2) and not first:
                                times_v(hd - 1, 1 - b, (t + NT) // 2 - 2)
                            if t == 4 and not last:
                                before_turn_v(hd + 1)
                            if t >= 2:
                                turn_p(hd, t - 2)
                            elif not first:
                                turn_p(hd - 1, t - 2 + NT)
                            if t == 4 and not last:
                                turn_v(hd + 1)
                    over_heads(pe, head)
                    hd = heads - 1
                    times_v(hd, 1, NT // 2 - 2)
                    turn_p(hd, NT - 2)
                    turn_p(hd, NT - 1)
                    times_v(hd, 1, NT // 2 - 1)

                @block.vector
                def _(dve):
                    def split_v(hd, b):
                        dve.wait_ge(v_hi_done, hd + 1)
                        nc.vector.tensor_tensor(v[:, b, :, 64:128], vt[:], v[:, b, :, 0:64].bitcast(F32), ALU.subtract)\
                            .then_inc(v_lo_done, 1)

                    def normalise(hd, t):
                        s = NT * hd + t
                        lo = lowest(t)
                        n = (t + 1 - lo) * P
                        r = slice(t % 4, t % 4 + 1)
                        dve.wait_ge(exped, s + 1)
                        nc.vector.reciprocal(inverse[:, r], total[:, r]).then_inc(inverted, 1)
                        dve.wait_ge(inverted, s + 1)
                        nc.vector.tensor_scalar(prob[:, t % 4, 0:n], prob[:, t % 4, 0:n], inverse[:, r], None, ALU.mult)\
                            .then_inc(normed, 1)

                    def row_max(hd, b, t):
                        s = NT * hd + t
                        lo = lowest(t)
                        n = (t + 1 - lo) * P
                        r = slice(t % 4, t % 4 + 1)
                        if mla:
                            dve.wait_ge(scored, s + 1)
                            nc.vector.tensor_reduce(neg_max[:, r], scores[:, t % 2, 0:n], AX_X, ALU.max, negate=True)\
                                .then_inc(maxed, 1)
                            return
                        x = extra[:, b, BAND - n:BAND] if chk else extra[:, b, 0:n]
                        nc.vector.tensor_tensor_reduce(out=prob[:, t % 4, 0:n], in0=scores[:, t % 2, 0:n], in1=x,
                                                       scale=-1.0, scalar=BIG, op0=ALU.add, op1=ALU.min,
                                                       accum_out=neg_max[:, r]).then_inc(maxed, 1)

                    def before_max(i, hd, b, t):
                        s = NT * hd + t
                        if mla:
                            return
                        dve.wait_ge(scored, s + 1)
                        wait(dve, pieces_turned, NPC * hd + BEFORE[t - 4] + PIECES[t - 4] if t >= 4 else
                             NPC * (hd - 1) + BEFORE[t + NT - 4] + PIECES[t + NT - 4])
                        if t == 0:
                            dve.wait_ge(in_x[b], 16 * i + 16)

                    def evacuate(hd, t):
                        for n, js in enumerate(turned(t)):
                            g = BEFORE[t] + n
                            u = t // 2
                            dve.wait_ge(pt_hi_done, NPC * hd + g + 1)
                            at = js[0] - lowest(2 * u)
                            where = (slice(None), u % 2, slice(at, at + len(js)), slice((t % 2) * P, (t % 2 + 1) * P))
                            nc.vector.tensor_tensor(pt_lo[where], turn[:, g % 2, 0:len(js), :], pt_hi[where].bitcast(F32),
                                                    ALU.subtract).then_inc(pt_lo_done, 1)

                    def add_halves(hd, b, u):
                        dve.wait_ge(o_low_done, NT // 2 * hd + u + 1)
                        if u == 0:
                            wait(dve, out_lo, hd - 1)
                        nc.vector.tensor_tensor(o[64 * b:64 * b + 64, 2 * u * P:2 * (u + 1) * P], pv[0:64, :], o_low[:],
                                                ALU.add).then_inc(o_done, 1)

                    split_v(0, 0)

                    def head(i, b, hd, last):
                        first = isinstance(hd, int) and hd == 0
                        for t in range(NT):
                            before_max(i, hd, b, t)
                            if mla:
                                row_max(hd, b, t)
                            if t >= 1:
                                normalise(hd, t - 1)
                            elif not first:
                                normalise(hd - 1, NT - 1)
                            elif not mla:
                                nc.vector.memset(spare[:], 0.0)
                            if not mla:
                                row_max(hd, b, t)
                            if t >= 2:
                                evacuate(hd, t - 2)
                            elif not first:
                                evacuate(hd - 1, t - 2 + NT)
                            if t % 2 == 0:
                                if t >= 4:
                                    add_halves(hd, b, t // 2 - 2)
                                elif not first:
                                    add_halves(hd - 1, 1 - b, (t + NT) // 2 - 2)
                            if t == 5 and not last:
                                split_v(hd + 1, 1 - b)
                    over_heads(dve, head)
                    hd = heads - 1
                    normalise(hd, NT - 1)
                    evacuate(hd, NT - 2)
                    add_halves(hd, 1, NT // 2 - 2)
                    evacuate(hd, NT - 1)
                    add_halves(hd, 1, NT // 2 - 1)
            sp.end()

    def stage_output(tag, weights, parked=False):
        with ExitStack() as st:
            sp = Space(st, tag)
            wt = Weights(sp, KD)
            acc = sp.ps("acc", [P, 2, S])
            added = sp.sem("added")
            h_back = sp.sem("h_back")
            with nc.Block() as block:

                @block.sync
                def _(sync):
                    def body(i):
                        for b in range(2):
                            c = 2 * i + b
                            wt.load(sync, c, b, [(0, 0, weights[:, bass.ds(c * P, P)])])
                            if parked and isinstance(i, int) and c == 1:
                                sync.dma_start(hT[:], s_h).then_inc(h_back, 16)
                    pairs(sync, 0, KD // 2, body)

                @block.scalar
                def _(act):
                    def body(i):
                        for b in range(2):
                            wt.act_hi(act, 2 * i + b, b, 16 * i + 16, KD)
                    pairs(act, 0, KD // 2, body)

                @block.tensor
                def _(pe):
                    def body(i):
                        for b in range(2):
                            c = 2 * i + b
                            pe.wait_ge(wt.lo_done, c + 1)
                            wait(pe, added, c - 1)
                            wt.pe_multiply(pe, acc[:, b, :], b, range(KD), 0, KD - 1, a_hi, a_lo).then_inc(wt.used, 1)
                    pairs(pe, 0, KD // 2, body)

                @block.vector
                def _(dve):
                    def add(c, b):
                        dve.wait_ge(wt.used, c + 1)
                        at = bass.ds(c, 1)
                        rows = hT[:, at, :].rearrange("q o n -> q (o n)")
                        nc.vector.tensor_tensor(rows, acc[:, b, :], rows, ALU.add).then_inc(added, 1)

                    def body(i):
                        for b in range(2):
                            c = 2 * i + b
                            wt.dve_lo(dve, c, b, KD)
                            if parked and isinstance(i, int) and c == 1:
                                dve.wait_ge(h_back, 16)
                            if not (isinstance(i, int) and c == 0):
                                add(c - 1, 1 - b)
                    pairs(dve, 0, KD // 2, body)
                    add(KD - 1, 1)
            sp.end()

    def stage_ple(tag, layer):
        with ExitStack() as st:
            sp = Space(st, tag)
            KP = PLE // P
            wt = Weights(sp, KD + KP)
            acc = sp.ps("acc", [P, 2, S])
            pt = sp.ps("pt", [P, KP, ST, P])
            pr = sp.sb("pr", [P, ST, PLE])
            p_hi = sp.sb("p_hi", [P, KP, S], F32R)
            p_lo = sp.sb("p_lo", [P, KP, S], F32R)
            gate = sp.sb("gate", [P, 2, S])
            p_in = sp.sem("p_in")
            p_turned = sp.sem("p_turned")
            p_hi_done, p_lo_done = sp.sem("p_hi_done"), sp.sem("p_lo_done")
            gates_summed = sp.sem("gates_summed")
            gate_done = sp.sem("gate_done")
            gated = sp.sem("gated")
            added = sp.sem("added")
            with nc.Block() as block:

                @block.sync
                def _(sync):
                    sync.dma_start(pr[:], p[layer, 0].rearrange("(t q) n -> q t n", q=P)).then_inc(p_in, 16)

                    def body(i):
                        for b in range(2):
                            c = 2 * i + b
                            cols = bass.ds(c * P, P)
                            wt.load(sync, c, b, [(0, 0, pe_gate_w[layer][:, cols]), (0, KD, pe_w[layer][:, cols])])
                    pairs(sync, 0, KD // 2, body)

                @block.scalar
                def _(act):
                    act.wait_ge(p_turned, 1)
                    for k in range(KP):
                        nc.scalar.activation(p_hi[:, k, :].rearrange("q (t n) -> q t n", t=ST), pt[:, k, :, :], ACT.Copy)\
                            .then_inc(p_hi_done, 1)

                    def gates(c, b):
                        act.wait_ge(gates_summed, c + 1)
                        wait(act, gated, c - 1)
                        nc.scalar.activation(gate[:, b, :], acc[:, 0, :], ACT.Sigmoid).then_inc(gate_done, 1)

                    def body(i):
                        for b in range(2):
                            c = 2 * i + b
                            wt.act_hi(act, c, b, 32 * i + 32, KD + KP)
                            if not (isinstance(i, int) and c == 0):
                                gates(c - 1, 1 - b)
                    pairs(act, 0, KD // 2, body)
                    gates(KD - 1, 1)

                @block.tensor
                def _(pe):
                    pe.wait_ge(p_in, 16)
                    for t in range(ST):
                        for k in range(KP):
                            last = nc.tensor.transpose(pt[:, k, t, :], pr[:, t, k * P:(k + 1) * P], ident[:])
                    last.then_inc(p_turned, 1)

                    def body(i):
                        for b in range(2):
                            c = 2 * i + b
                            pe.wait_ge(wt.lo_done, c + 1)
                            wait(pe, gate_done, c)
                            wt.pe_multiply(pe, acc[:, 0, :], b, range(KD), 0, KD - 1, a_hi, a_lo)\
                                .then_inc(gates_summed, 1)
                            if isinstance(i, int) and c == 0:
                                pe.wait_ge(p_lo_done, KP)
                            wait(pe, gated, c)
                            wt.pe_multiply(pe, acc[:, 1, :], b, range(KP), 0, KP - 1, p_hi, p_lo, k0=KD)\
                                .then_inc(wt.used, 1)
                    pairs(pe, 0, KD // 2, body)

                @block.vector
                def _(dve):
                    for k in range(KP):
                        dve.wait_ge(p_hi_done, k + 1)
                        nc.vector.tensor_tensor(p_lo[:, k, :].rearrange("q (t n) -> q t n", t=ST), pt[:, k, :, :],
                                                p_hi[:, k, :].rearrange("q (t n) -> q t n", t=ST).bitcast(F32),
                                                ALU.subtract).then_inc(p_lo_done, 1)

                    def add(c, b):
                        dve.wait_ge(wt.used, c + 1)
                        dve.wait_ge(gate_done, c + 1)
                        nc.vector.tensor_tensor(gate[:, b, :], acc[:, 1, :], gate[:, b, :], ALU.mult).then_inc(gated, 1)
                        dve.wait_ge(gated, c + 1)
                        rows = hT[:, bass.ds(c, 1), :].rearrange("q o n -> q (o n)")
                        nc.vector.tensor_tensor(rows, rows, gate[:, b, :], ALU.add).then_inc(added, 1)

                    def body(i):
                        for b in range(2):
                            c = 2 * i + b
                            wt.dve_lo(dve, c, b, KD + KP)
                            if not (isinstance(i, int) and c == 0):
                                add(c - 1, 1 - b)
                    pairs(dve, 0, KD // 2, body)
                    add(KD - 1, 1)
            sp.end()

    def stage_result():
        with ExitStack() as st:
            sp = Space(st, "re")
            ht = sp.ps("ht", [P, 2, KD, P])
            row = sp.sb("row", [P, 2, D])
            turned = sp.sem("turned")
            from_act, from_dve = sp.sem("from_act"), sp.sem("from_dve")
            stored = [sp.sem("stored0"), sp.sem("stored1")]
            H2 = KD // 2 * P
            with nc.Block() as block:

                @block.sync
                def _(sync):
                    for t in range(ST):
                        sync.wait_ge(from_act, t + 1)
                        sync.wait_ge(from_dve, t + 1)
                        sync.dma_start(out[0, t * P:(t + 1) * P, :], row[:, t % 2, :]).then_inc(stored[t % 2], 16)
                    for b in range(2):
                        sync.wait_ge(stored[b], 16 * ST // 2)

                @block.tensor
                def _(pe):
                    for t in range(ST):
                        wait(pe, from_act, t - 1)
                        wait(pe, from_dve, t - 1)
                        for k in range(KD):
                            last = nc.tensor.transpose(ht[:, t % 2, k, :], hT[:, k, t * P:(t + 1) * P], ident[:])
                        last.then_inc(turned, 1)

                @block.scalar
                def _(act):
                    for t in range(ST):
                        act.wait_ge(turned, t + 1)
                        wait(act, stored[t % 2], 16 * (t // 2))
                        nc.scalar.activation(row[:, t % 2, 0:H2], ht[:, t % 2, 0:KD // 2, :].rearrange("q k n -> q (k n)"),
                                             ACT.Copy).then_inc(from_act, 1)

                @block.vector
                def _(dve):
                    for t in range(ST):
                        dve.wait_ge(turned, t + 1)
                        wait(dve, stored[t % 2], 16 * (t // 2))
                        nc.vector.tensor_copy(row[:, t % 2, H2:D], ht[:, t % 2, KD // 2:KD, :].rearrange("q k n -> q (k n)"))\
                            .then_inc(from_dve, 1)
            sp.end()

    with top, nc.allow_non_contiguous_dma(reason="gains, a column each"):
        with ExitStack() as first:
            rot = Space(first, "r").sb("rot", [P, S])
            stage_entry(rot)
            stage_norm("n0", g_norm[:, 0, :], park=True)
            stage_project_ab(rot)

        def slab(src, rows, at=0):
            return lambda hd: src[bass.ds(hd + at, 1)].rearrange("o q n -> (o q) n")

        ab = s_ab.rearrange("c (h q) n -> (c h) q n", h=2)
        fx = s_fox.rearrange("c (h q) n -> (c h) q n", h=2)
        stage_attention("mla", HEADS, 0, slab(s_mq, QK), slab(s_mk, QK), slab(s_mv, VDIM),
                        slab(ab, 64, 4 * HEADS), None)
        stage_attention("chk", HEADS, HEADS // 2, slab(ab, 64), slab(ab, 64, HEADS), slab(ab, 64, 2 * HEADS),
                        slab(ab, 64, 3 * HEADS), slab(s_bias, P))
        stage_output("o0", ab_w_out[0], parked=True)
        stage_norm("n1", g_gate[:, 0, :])
        stage_ple("e0", 0)
        stage_norm("n2", g_norm[:, 1, :])
        stage_project_fox()
        stage_attention("fox", FH, 0, slab(fx, 64), slab(fx, 64, FH), slab(fx, 64, 2 * FH), slab(fx, 64, 3 * FH),
                        lambda hd: s_cum[bass.ds(hd, 1), :].to_broadcast([P, S]))
        stage_output("o1", fox_w_out[0])
        stage_norm("n3", g_gate[:, 1, :])
        stage_ple("e1", 1)
        stage_result()


_INS = ["x", "p", "positions", "norm_g", "ab_w_in", "mla_q_norm", "mla_w_uq", "mla_kv_norm", "mla_w_ukv",
        "mla_q_gain", "mla_k_gain", "chk_q_gain", "chk_k_gain", "chk_rel_bias", "ab_w_out",
        "fox_w_in", "fox_b_f", "fox_q_gain", "fox_k_gain", "fox_w_out", "pe_w", "pe_gate_norm", "pe_gate_w"]


def kernel(**inputs):
    import concourse.bacc as bacc
    from concourse.bass_utils import run_bass_kernel_spmd

    nc = bacc.Bacc("TRN2", target_bir_lowering=False, num_devices=1)
    arrays = {name: np.ascontiguousarray(inputs[name]) for name in _INS}
    half = ROPE // 2
    freq = (np.float32(1.0) / (np.float32(10000.0) ** (np.arange(half, dtype=np.float32) / np.float32(half))))
    arrays["rope_freq"] = np.concatenate([freq, freq, -freq, freq]).astype(np.float32)[:, None]
    args = {name: nc.dram_tensor(f"in_{name}", a.shape, mybir.dt.from_np(a.dtype), kind="ExternalInput").ap()
            for name, a in arrays.items()}
    out = nc.dram_tensor("out_0", (1, S, D), F32, kind="ExternalOutput").ap()
    build(nc, **args, out=out)
    r = run_bass_kernel_spmd(nc, [{f"in_{name}": a for name, a in arrays.items()}], core_ids=[0])
    return r.results[0]["out_0"]
```

```python
from contextlib import ExitStack

import numpy as np

import concourse.bass as bass
from concourse import mybir

F32 = mybir.dt.float32
F32R = mybir.dt.float32r
BF16 = mybir.dt.bfloat16
I32 = mybir.dt.int32
ALU = mybir.AluOpType
ACT = mybir.ActivationFunctionType
AX_X = mybir.AxisListType.X

P = 128
D = 1024
S = 1024
KD = D // P
ST = S // P
HALF = 512
NH = S // HALF
PLE = 256
EPS = 1e-6
NEG = -1e30
BIG = 3.0e38

HEADS = 8
NOPE, ROPE, VDIM = 64, 32, 64
QK = NOPE + ROPE
QLORA, KVLORA = 384, 256
CHK = 64
LEFT = 8
BAND = 640
CHUNK = 64
CLIP = 256
FH = 16
FD = 64

C_KR = QLORA + KVLORA
C_GA = C_KR + ROPE
C_QB = C_GA + HEADS * VDIM

LAT_Q, LAT_KV, KR = 0, 3, 5
QB0, QB1 = 6, 14
VB1 = 18
GB1 = 22
GA1 = 26
MQ1 = 34
MK1 = 42


def wait(eng, sem, value):
    if isinstance(value, int) and value <= 0:
        return
    eng.wait_ge(sem, value)


def pairs(eng, lo, hi, body):
    body(lo)
    body(lo + 1)
    with eng.Fori(lo + 2, hi) as i:
        body(i)


def build(nc, x, p, positions, norm_g, ab_w_in, mla_q_norm, mla_w_uq, mla_kv_norm, mla_w_ukv,
          mla_q_gain, mla_k_gain, chk_q_gain, chk_k_gain, chk_rel_bias, ab_w_out,
          fox_w_in, fox_b_f, fox_q_gain, fox_k_gain, fox_w_out, pe_w, pe_gate_norm, pe_gate_w,
          rope_freq, out):
    top = ExitStack()

    def dram(name, shape):
        return nc.dram_tensor(name, shape, F32, kind="Internal").ap()

    s_h = dram("s_h", [P, KD, S])
    s_ab = dram("s_ab", [GA1 - QB0, P, S])
    s_mq = dram("s_mq", [HEADS, QK, S])
    s_mk = dram("s_mk", [HEADS, QK, S])
    s_mv = dram("s_mv", [HEADS, VDIM, S])
    s_fox = dram("s_fox", [4 * FH // 2, P, S])
    s_cum = dram("s_cum", [FH, S])
    s_rel = dram("s_rel", [HEADS, 768])
    s_rep = dram("s_rep", [HEADS, P, 768])
    s_bias = dram("s_bias", [HEADS, P, BAND])

    class Space:

        def __init__(self, stack, tag):
            self.stack, self.tag, self.numbers = stack, tag, []

        def sb(self, name, shape, dt=F32):
            return self.stack.enter_context(nc.sbuf_tensor(f"{self.tag}_{name}", shape, dt))

        def ps(self, name, shape, dt=F32):
            return self.stack.enter_context(nc.psum_tensor(f"{self.tag}_{name}", shape, dt))

        def sem(self, name):
            handle = self.stack.enter_context(nc.semaphore(f"{self.tag}_{name}"))
            self.numbers.append(handle.num)
            return handle

        def end(self):
            numbers = sorted(self.numbers)
            while numbers:
                n = next((k for k in range(1, len(numbers)) if numbers[k] != numbers[0] + k), len(numbers))
                nc.all_engine_barrier(sems_to_clear=range(numbers[0], numbers[0] + n))
                numbers = numbers[n:]

    G = Space(top, "g")
    hT = G.sb("hT", [P, KD, S])
    a_hi = G.sb("a_hi", [P, KD, S], F32R)
    a_lo = G.sb("a_lo", [P, KD, S], F32R)
    ident = G.sb("ident", [P, P])
    ident_r = G.sb("ident_r", [P, P], F32R)
    ident_b = G.sb("ident_b", [P, P], BF16)
    causal = G.sb("causal", [P, P], BF16)
    blockc = G.sb("blockc", [P, P], BF16)
    low_q = G.sb("low_q", [P, CHUNK], BF16)
    high_q = G.sb("high_q", [P, CHUNK], BF16)
    ind_all = G.sb("ind_all", [P, 2])
    ind_lat = G.sb("ind_lat", [P, 4])
    ind_head = G.sb("ind_head", [P, 2])
    ind_mla = G.sb("ind_mla", [P, 2])
    g_norm = G.sb("g_norm", [P, 2, KD])
    g_gate = G.sb("g_gate", [P, 2, KD])
    g_lat = G.sb("g_lat", [P, 5])
    g_mla = G.sb("g_mla", [P, 2])
    g_chk = G.sb("g_chk", [P, 8])
    g_fox = G.sb("g_fox", [P, 16])
    b_f = G.sb("b_f", [FH, 1])
    x_ss = G.sb("x_ss", [P, ST])

    class Norm:

        def __init__(self, sp, front=None):
            self.front = front
            if front:
                self.ss, self.bc, self.r1, self.r2, self.r3, self.e_hi, self.e_lo = \
                    front.ss, front.bc, front.r1, front.r2, front.r3, front.e_hi, front.e_lo
            else:
                self.ss = sp.ps("ss", [P, ST, 2])
                self.bc = sp.ps("bc", [P, S])
                self.r1 = sp.sb("r1", [P, ST, 2])
                self.r2 = sp.sb("r2", [P, ST, 2])
                self.r3 = sp.sb("r3", [P, ST, 2])
                self.e_hi = sp.sb("e_hi", [P, ST, 2, 64], F32R)
                self.e_lo = sp.sb("e_lo", [P, ST, 2, 64], F32R)
            def name(what):
                return what if front else f"f_{what}"

            self.summed = sp.sem(name("summed"))
            self.eps_in = sp.sem(name("eps_in"))
            self.inverted = sp.sem(name("inverted"))
            self.rooted = sp.sem(name("rooted"))
            self.spread_hi = sp.sem(name("spread_hi"))
            self.spread = sp.sem(name("spread"))
            self.on_rows = sp.sem(name("on_rows"))
            self.applied = sp.sem(name("applied"))

        def pe_sum(self, pe, n, squares, indicator):
            wait(pe, self.eps_in, n)
            if self.front and isinstance(n, int) and n == 0:
                pe.wait_ge(self.front.eps_in, 1)
            for t in range(ST):
                last = nc.tensor.matmul(self.ss[:, t, :], squares[:, t * P:(t + 1) * P], indicator,
                                        start=True, stop=True)
            last.then_inc(self.summed, 1)

        def dve_invert(self, dve, n):
            wait(dve, self.summed, n + 1)
            nc.vector.tensor_scalar(self.r1[:], self.ss[:], EPS, None, ALU.add).then_inc(self.eps_in, 1)
            wait(dve, self.eps_in, n + 1)
            nc.vector.reciprocal(self.r2[:], self.r1[:]).then_inc(self.inverted, 1)

        def act_root(self, act, n):
            wait(act, self.inverted, n + 1)
            nc.scalar.activation(self.r3[:], self.r2[:], ACT.Sqrt).then_inc(self.rooted, 1)

        def dve_spread(self, dve, n):
            wait(dve, self.rooted, n + 1)
            wait(dve, self.on_rows, n)
            if self.front and isinstance(n, int) and n == 0:
                dve.wait_ge(self.front.on_rows, 1)
            r3 = self.r3[:].unsqueeze(3).to_broadcast([P, ST, 2, 64])
            nc.vector.tensor_copy(self.e_hi[:], r3).then_inc(self.spread_hi, 1)
            wait(dve, self.spread_hi, n + 1)
            nc.vector.tensor_tensor(self.e_lo[:], r3, self.e_hi[:].bitcast(F32), ALU.subtract)\
                .then_inc(self.spread, 1)

        def pe_rows(self, pe, n):
            wait(pe, self.spread, n + 1)
            wait(pe, self.applied, n)
            if self.front and isinstance(n, int) and n == 0:
                pe.wait_ge(self.front.scaled, KD)
            for t in range(ST):
                for e, part in enumerate((self.e_hi, self.e_lo)):
                    last = nc.tensor.matmul(self.bc[:, t * P:(t + 1) * P],
                                            part[:, t].rearrange("p h f -> p (h f)"), ident_r[:],
                                            start=(e == 0), stop=(e == 1))
            last.then_inc(self.on_rows, 1)

    bias_wrote = G.sem("bias_wrote")

    def stage_entry(rot):
        with ExitStack() as st:
            sp = Space(st, "en")
            xr = sp.sb("xr", [P, ST, D])
            x_sq = sp.sb("x_sq", [P, 2, D])
            xt = sp.ps("xt", [P, 2, KD, P])
            posi = sp.sb("posi", [P, S], I32)
            ang = sp.sb("ang", [P, S])
            turns = sp.sb("turns", [P, S])
            freq = sp.sb("freq", [P, 1])
            two_pi = sp.sb("two_pi", [P, S])
            rel = sp.sb("rel", [HEADS, 2 * CLIP + 1])
            rel_ext = sp.sb("rel_ext", [HEADS, 768])
            loaded = [sp.sem(f"loaded{t}") for t in range(ST)]
            small = sp.sem("small")
            pos_in = sp.sem("pos_in")
            rel_in = sp.sem("rel_in")
            rel_out = sp.sem("rel_out")
            turned = sp.sem("turned")
            from_act = sp.sem("from_act")
            from_dve = sp.sem("from_dve")
            made = sp.sem("made")
            chain = sp.sem("chain")
            angled = sp.sem("angled")
            widened = sp.sem("widened")
            sined = sp.sem("sined")
            x_squared = sp.sem("x_squared")
            with nc.Block() as block:

                @block.sync
                def _(sync):
                    for t in range(ST):
                        sync.dma_start(xr[:, t, :], x[0, t * P:(t + 1) * P, :]).then_inc(loaded[t], 16)
                    sync.wait_ge(rel_out, 1)
                    sync.dma_start(s_rel, rel_ext[:]).then_inc(bias_wrote, 16)
                    sync.wait_ge(bias_wrote, 16)
                    repeated = bass.AP(tensor=s_rel.tensor, offset=0, ap=[[768, HEADS], [0, P], [1, 768]])
                    sync.dma_start(s_rep, repeated).then_inc(bias_wrote, 16)

                @block.scalar
                def _(act):
                    n = 0
                    act.dma_start(posi[64:128, :], positions[0:1, :].to_broadcast([64, S])).then_inc(pos_in, 16)
                    act.dma_start(freq[64:128, :], rope_freq).then_inc(pos_in, 16)
                    act.dma_start(rel[:], chk_rel_bias[0]).then_inc(rel_in, 16)

                    def col(dst, src):
                        nonlocal n
                        act.dma_start(dst, src).then_inc(small, 16)
                        n += 1

                    for layer in range(2):
                        col(g_norm[:, layer, :], norm_g[layer].rearrange("(k q) -> q k", q=P))
                        col(g_gate[:, layer, :], pe_gate_norm[layer].rearrange("(k q) -> q k", q=P))
                    col(g_lat[:, 0:3], mla_q_norm[0].rearrange("(k q) -> q k", q=P))
                    col(g_lat[:, 3:5], mla_kv_norm[0].rearrange("(k q) -> q k", q=P))
                    half = ROPE // 2
                    for j, g in enumerate((mla_q_gain, mla_k_gain)):
                        g = g[0].rearrange("(f o) -> f o", o=1)
                        col(g_mla[0:QK, j:j + 1], g)
                        col(g_mla[QK:QK + half, j:j + 1], g[NOPE + half:QK])
                        col(g_mla[QK + half:P, j:j + 1], g[NOPE:NOPE + half])
                    for dst, width, gains in ((g_chk, 4, (chk_q_gain, chk_k_gain)),
                                              (g_fox, 8, (fox_q_gain, fox_k_gain))):
                        for j, g in enumerate(gains):
                            for base in (0, 64):
                                col(dst[base:base + 64, j * width:j * width + 1],
                                    g[0].rearrange("(f o) -> f o", o=1))
                    col(b_f[:], fox_b_f[0].rearrange("(f o) -> f o", o=1))
                    for t in range(ST):
                        act.wait_ge(loaded[t], 16)
                        nc.scalar.activation(x_sq[:, t % 2, :], xr[:, t, :], ACT.Square, accum_out=x_ss[:, t:t + 1])\
                            .then_inc(x_squared, 1)
                        act.wait_ge(turned, t + 1)
                        nc.scalar.activation(hT[:, 0:4, t * P:(t + 1) * P], xt[:, t % 2, 0:4, :], ACT.Copy)\
                            .then_inc(from_act, 1)
                        wait(act, x_squared, t)
                    act.wait_ge(angled, 1)
                    nc.scalar.activation(rot[64:128, :], ang[64:128, :], ACT.Sin).then_inc(sined, 1)
                    act.wait_ge(small, 16 * n)
                    nc.scalar.activation(g_mla[:, 0:1], g_mla[:, 0:1], ACT.Copy, scale=float(QK) ** -0.5)
                    for t, width in ((g_chk, 4), (g_fox, 8)):
                        nc.scalar.activation(t[:, 1:width], t[:, 0:1].to_broadcast([P, width - 1]), ACT.Copy,
                                             scale=float(CHK) ** -0.5)
                        nc.scalar.activation(t[:, width + 1:2 * width],
                                             t[:, width:width + 1].to_broadcast([P, width - 1]), ACT.Copy)\
                            .then_inc(widened, 1)
                    act.wait_ge(widened, 2)
                    for k, t in enumerate((g_chk, g_fox)):
                        nc.scalar.activation(t[:, 0:1], t[:, 0:1], ACT.Copy, scale=float(CHK) ** -0.5)

                @block.gpsimd
                def _(pool):
                    pool.memset(ident[:], 0.0).then_inc(made, 1)
                    pool.memset(causal[:], 0.0).then_inc(made, 1)
                    pool.wait_ge(made, 2)
                    pool.affine_select(out=ident[:], in_=ident[:], compare_op=ALU.not_equal, fill=1.0, base=0,
                                       pattern=[[-1, P]], channel_multiplier=1).then_inc(made, 1)
                    pool.affine_select(out=causal[:], in_=causal[:], compare_op=ALU.is_ge, fill=NEG, base=0,
                                       pattern=[[-1, P]], channel_multiplier=1).then_inc(made, 1)

                @block.tensor
                def _(pe):
                    pe.wait_ge(made, 3)
                    for t in range(ST):
                        pe.wait_ge(loaded[t], 16)
                        wait(pe, from_act, t - 1)
                        wait(pe, from_dve, t - 1)
                        for k in range(KD):
                            last = nc.tensor.transpose(xt[:, t % 2, k, :], xr[:, t, k * P:(k + 1) * P], ident[:])
                        last.then_inc(turned, 1)

                @block.vector
                def _(dve):
                    count = [0]

                    def link(ins):
                        count[0] += 1
                        ins.then_inc(chain, 1)
                        dve.wait_ge(chain, count[0])

                    for m in (blockc, low_q):
                        nc.vector.memset(m[:], 0.0)
                    link(nc.vector.memset(high_q[:], 0.0))
                    nc.vector.memset(blockc[0:CHUNK, CHUNK:P], NEG)
                    nc.vector.memset(low_q[0:CHUNK, :], NEG)
                    nc.vector.memset(high_q[CHUNK:P, :], NEG)
                    nc.vector.memset(ind_all[:], 1.0 / D)
                    nc.vector.memset(ind_lat[:, 0:2], 1.0 / QLORA)
                    nc.vector.memset(ind_lat[:, 2:4], 1.0 / KVLORA)
                    link(nc.vector.memset(ind_head[:], 0.0))
                    nc.vector.memset(ind_head[0:64, 0:1], 1.0 / CHK)
                    nc.vector.memset(ind_head[64:128, 1:2], 1.0 / CHK)
                    link(nc.vector.memset(ind_mla[:], 1.0 / QK))
                    nc.vector.memset(ind_mla[QK:P, :], 0.0)
                    dve.wait_ge(made, 3)
                    nc.vector.tensor_copy(ident_r[:], ident[:])
                    nc.vector.tensor_copy(ident_b[:], ident[:])

                    dve.wait_ge(rel_in, 16)
                    far = 639 - CLIP
                    nc.vector.tensor_copy(rel_ext[:, 0:far], rel[:, 2 * CLIP:2 * CLIP + 1].to_broadcast([HEADS, far]))
                    near = 768 - far
                    nc.vector.tensor_copy(rel_ext[:, far:768], rel[:, 2 * CLIP + 1 - near:2 * CLIP + 1][:, ::-1])\
                        .then_inc(rel_out, 1)

                    r = slice(64, 128)
                    rc = slice(64, 96)
                    dve.wait_ge(pos_in, 32)
                    link(nc.vector.tensor_copy(ang[r, :], posi[r, :]))
                    link(nc.vector.tensor_scalar(ang[r, :], ang[r, :], freq[r, 0:1], None, ALU.mult))
                    magic = 1.5 * 2.0 ** 23
                    link(nc.vector.tensor_scalar(turns[r, :], ang[r, :], 1.0 / (2 * np.pi), magic, ALU.mult, ALU.add))
                    link(nc.vector.tensor_scalar(turns[r, :], turns[r, :], magic, None, ALU.subtract))
                    parts, rest = [], 2 * np.pi
                    for bits in (5, 16):
                        part = float(np.floor(rest * 2.0 ** bits) / 2.0 ** bits)
                        parts.append(part)
                        rest -= part
                    parts.append(float(rest))
                    for part in parts:
                        link(nc.vector.scalar_tensor_tensor(out=ang[r, :], in0=turns[r, :], scalar=-part,
                                                            in1=ang[r, :], op0=ALU.mult, op1=ALU.add))
                    link(nc.vector.tensor_scalar(ang[rc, :], ang[rc, :], float(np.pi / 2), None, ALU.add))
                    link(nc.vector.tensor_scalar(two_pi[rc, :], ang[rc, :], float(np.pi), 2 * float(np.pi),
                                                 ALU.is_gt, ALU.mult))
                    link(nc.vector.tensor_tensor(ang[rc, :], ang[rc, :], two_pi[rc, :], ALU.subtract))
                    nc.vector.tensor_scalar(ang[r, :], ang[r, :], float(np.float32(3.1415925)),
                                            -float(np.float32(3.1415925)), ALU.min, ALU.max).then_inc(angled, 1)
                    for t in range(ST):
                        dve.wait_ge(turned, t + 1)
                        nc.vector.tensor_copy(hT[:, 4:8, t * P:(t + 1) * P], xt[:, t % 2, 4:8, :]).then_inc(from_dve, 1)

            sp.end()


    h_parked = G.sem("h_parked")
    h_sq = [None]

    class Front(Norm):

        def __init__(self, sp, gain, u, from_x=False):
            super().__init__(sp)
            self.gain, self.u, self.from_x = gain, u, from_x
            self.scaled = sp.sem("f_scaled")
            self.hi_done = sp.sem("f_hi_done")
            self.lo_pool = sp.sem("f_lo_pool")
            self.lo_dve = sp.sem("f_lo_dve")

        def pe_norm(self, pe):
            if not self.from_x:
                self.pe_sum(pe, 0, h_sq[0], ind_all[:])
            self.pe_rows(pe, 0)

        def act_split(self, act):
            for k in range(KD):
                act.wait_ge(self.scaled, k + 1)
                nc.scalar.activation(a_hi[:, k, :], self.u[:, k % 2, :], ACT.Copy).then_inc(self.hi_done, 1)

        def pool_split(self, pool):
            for k in range(0, KD, 2):
                pool.wait_ge(self.hi_done, k + 1)
                nc.gpsimd.tensor_tensor(a_lo[:, k, :], self.u[:, k % 2, :], a_hi[:, k, :].bitcast(F32),
                                        ALU.subtract).then_inc(self.lo_pool, 1)

        def dve_norm(self, dve):
            if self.from_x:
                sums = x_ss[:].unsqueeze(2).to_broadcast([P, ST, 2])
                nc.vector.tensor_scalar(self.r1[:], sums, 1.0 / D, EPS, ALU.mult, ALU.add).then_inc(self.eps_in, 1)
                dve.wait_ge(self.eps_in, 1)
                nc.vector.reciprocal(self.r2[:], self.r1[:]).then_inc(self.inverted, 1)
            else:
                self.dve_invert(dve, 0)
            self.dve_spread(dve, 0)

        def dve_apply(self, dve):
            dve.wait_ge(self.on_rows, 1)
            for k in range(KD):
                if k >= 2:
                    dve.wait_ge(self.lo_dve if k % 2 else self.lo_pool, k // 2)
                nc.vector.scalar_tensor_tensor(out=self.u[:, k % 2, :], in0=self.bc[:], scalar=self.gain[:, k:k + 1],
                                               in1=hT[:, k, :], op0=ALU.mult, op1=ALU.mult)\
                    .then_inc(self.scaled, 1)
                if k % 2:
                    dve.wait_ge(self.hi_done, k + 1)
                    nc.vector.tensor_tensor(a_lo[:, k, :], self.u[:, k % 2, :], a_hi[:, k, :].bitcast(F32),
                                            ALU.subtract).then_inc(self.lo_dve, 1)

        def pe_tile(self, pe, k):
            pe.wait_ge(self.lo_dve if k % 2 else self.lo_pool, k // 2 + 1)

        def all_split(self, eng):
            eng.wait_ge(self.lo_pool, KD // 2)
            eng.wait_ge(self.lo_dve, KD // 2)

    class Squares:

        def __init__(self, sp, added):
            self.sq = sp.sb("sq", [P, 2, S])
            self.added = added
            self.squared = sp.sem("squared")
            self.gathered = sp.sem("gathered")

        def act_square(self, act, c, b):
            act.wait_ge(self.added, c + 1)
            first = isinstance(c, int) and c == 0
            wait(act, self.gathered, c - 2)
            nc.scalar.activation(h_sq[0][:] if first else self.sq[:, b, :],
                                 hT[:, bass.ds(c, 1), :].rearrange("q o n -> q (o n)"), ACT.Square)\
                .then_inc(self.squared, 1)

        def dve_gather(self, dve, c, b):
            if isinstance(c, int) and c == 0:
                return
            dve.wait_ge(self.squared, c + 1)
            wait(dve, self.gathered, c - 1)
            nc.vector.tensor_tensor(h_sq[0][:], h_sq[0][:], self.sq[:, b, :], ALU.add).then_inc(self.gathered, 1)

    class Weights:

        def __init__(self, sp, kt):
            self.raw = sp.sb("w_raw", [P, 2, kt, P])
            self.hi = sp.sb("w_hi", [P, 2, kt, P], F32R)
            self.lo = sp.sb("w_lo", [P, 2, kt, P], F32R)
            self.loaded = [sp.sem("w_loaded0"), sp.sem("w_loaded1")]
            self.hi_done = sp.sem("w_hi_done")
            self.lo_done = sp.sem("w_lo_done")
            self.used = sp.sem("w_used")

        def load(self, sync, c, b, pieces):
            wait(sync, self.lo_done, c - 1)
            for at, k0, src in pieces:
                n, kt = src.shape[1], src.shape[0] // P
                sync.dma_start(self.raw[:, b, k0:k0 + kt, at:at + n], src.rearrange("(k q) n -> q k n", q=P))\
                    .then_inc(self.loaded[b], 16)

        def act_hi(self, act, c, b, loaded, kt):
            act.wait_ge(self.loaded[b], loaded)
            wait(act, self.used, c - 1)
            nc.scalar.activation(self.hi[:, b, 0:kt, :], self.raw[:, b, 0:kt, :], ACT.Copy).then_inc(self.hi_done, 1)

        def dve_lo(self, dve, c, b, kt):
            dve.wait_ge(self.hi_done, c + 1)
            nc.vector.tensor_tensor(self.lo[:, b, 0:kt, :], self.raw[:, b, 0:kt, :],
                                    self.hi[:, b, 0:kt, :].bitcast(F32), ALU.subtract).then_inc(self.lo_done, 1)

        def pe_multiply(self, pe, dst, b, kts, first, last, m_hi, m_lo, k0=0, tile=None):
            for k in kts:
                if tile:
                    tile(pe, k)
                for w, m in ((self.hi, m_hi), (self.hi, m_lo), (self.lo, m_hi)):
                    for h in range(NH):
                        ins = nc.tensor.matmul(dst[:, h * HALF:(h + 1) * HALF], w[:, b, k0 + k, :],
                                               m[:, k, h * HALF:(h + 1) * HALF],
                                               start=(k == first and w is self.hi and m is m_hi),
                                               stop=(k == last and w is self.lo))
            return ins

    def stage_project_ab(rot):
        with ExitStack() as st:
            sp = Space(st, "pa")
            wt = Weights(sp, KD)
            y = sp.sb("y", [P, 2, S])
            front = Front(sp, g_norm[:, 0, :], y, from_x=True)
            norm = Norm(sp, front)
            acc = sp.ps("acc", [P, 2, S])
            lat = hT[:, 0:5, :]
            kr = hT[:, 5, :]
            vout = hT[:, 6:8, :]
            l_hi = sp.sb("l_hi", [P, 5, S], F32R)
            l_lo = sp.sb("l_lo", [P, 5, S], F32R)
            sq = sp.sb("sq", [P, 2, S])
            lsq = sp.sb("lsq", [P, 2, S])
            rope_t = sp.sb("rope_t", [P, S])
            acc_free = sp.sem("acc_free")
            squares = sp.sem("squares")
            copied = sp.sem("copied")
            lat_sq = sp.sem("lat_sq")
            lat_added = sp.sem("lat_added")
            lat_scaled = sp.sem("lat_scaled")
            lat_hi = sp.sem("lat_hi")
            lat_lo = sp.sem("lat_lo")
            mq_ready = sp.sem("mq_ready")
            mk_ready = sp.sem("mk_ready")
            roped = sp.sem("roped")
            stored = [sp.sem("stored0"), sp.sem("stored1")]
            v_stored = [sp.sem("v_stored0"), sp.sem("v_stored1")]
            w_in, w_uq, w_ukv = ab_w_in[0], mla_w_uq[0], mla_w_ukv[0]
            half = ROPE // 2

            def pieces(c):
                c, seg = c
                if seg == "lat":
                    return [(0, 0, w_in[:, c * P:(c + 1) * P])]
                if seg == "kr":
                    return [(0, 0, w_in[:, C_KR - 64:C_KR + ROPE]), (96, 0, w_in[:, C_KR + half:C_KR + ROPE]),
                            (96 + half, 0, w_in[:, C_KR:C_KR + half])]
                if seg == "b":
                    return [(0, 0, w_in[:, bass.ds((c - QB0) * P + C_QB, P)])]
                if seg == "ga":
                    return [(0, 0, w_in[:, bass.ds((c - GB1) * P + C_GA, P)])]
                if seg == "mq":
                    o = (c - GA1) * QK
                    return [(0, 0, w_uq[:, bass.ds(o, QK)]), (QK, 0, w_uq[:, bass.ds(o + NOPE + half, half)]),
                            (QK + half, 0, w_uq[:, bass.ds(o + NOPE, half)])]
                return [(0, 0, w_ukv[:, bass.ds((c - MQ1) * P, P)])]

            SEGS = [("lat", 0, KR), ("kr", KR, QB0), ("b", QB0, GB1), ("ga", GB1, GA1), ("mq", GA1, MQ1),
                    ("mk", MQ1, MK1)]

            def seg_at(c):
                return next(s for s, a, z in SEGS if a <= c < z)

            def kt_of(seg):
                return {"mq": QLORA // P, "mk": KVLORA // P}.get(seg, KD)

            def loaded(c, b, seg):
                i = (c - b) // 2 if isinstance(c, int) else c[1]
                c = c if isinstance(c, int) else c[0]
                extra = 0
                if seg in ("kr", "b", "ga", "mq", "mk") and b == 1:
                    extra += 32
                if seg == "mq":
                    return 16 + 16 * i + extra + 32 * (i + 1) - 32 * (GA1 // 2)
                if seg == "mk":
                    extra += 32 * (MQ1 - GA1) // 2
                return 16 + 16 * i + extra

            LOOPS = [("qk", QB0 // 2, QB1 // 2), ("v", QB1 // 2, VB1 // 2), ("g", VB1 // 2, GA1 // 2),
                     ("mq", GA1 // 2, MQ1 // 2), ("mk", MQ1 // 2, MK1 // 2)]

            def loop(eng, lo, hi, body, edges):
                i = lo
                while i < hi:
                    if i in edges:
                        body(i)
                        i += 1
                        continue
                    end = i
                    while end < hi and end not in edges:
                        end += 1
                    if end - i == 1:
                        body(i)
                    else:
                        with eng.Fori(i, end) as r:
                            body(r)
                    i = end

            EDGES = {QB0 // 2, QB1 // 2, VB1 // 2, GB1 // 2, GA1 // 2, MQ1 // 2,
                     GB1 // 2 - 1, GA1 // 2 - 1, MQ1 // 2 - 1, MK1 // 2 - 1}

            def seg_for(kind, i, ahead):
                if isinstance(i, int):
                    c = 2 * (i + ahead)
                    return seg_at(c) if c < MK1 else None
                return {"qk": "b", "v": "b", "g": "ga" if kind == "g" else "b", "mq": "mq", "mk": "mk"}[kind]

            with nc.Block() as block:

                @block.gpsimd
                def _(pool):
                    front.pool_split(pool)

                @block.sync
                def _(sync):
                    def load(c, i, b, seg):
                        wt.load(sync, c, b, pieces((c, seg)))

                    def load_ahead(kind, i, b):
                        seg = seg_for(kind, i, 1)
                        if isinstance(i, int) and 2 * i + 2 + b == KR:
                            seg = "kr"
                        if seg:
                            load(2 * i + 2 + b, i, b, seg)

                    load(0, 0, 0, "lat")
                    sync.dma_start(s_h, hT[:]).then_inc(h_parked, 16)
                    load(1, 0, 1, "lat")
                    for i in range(QB0 // 2):
                        for b in range(2):
                            load_ahead("lat", i, b)
                    sync.wait_ge(bias_wrote, 32)
                    for h in range(HEADS):
                        rows = bass.AP(tensor=s_rep.tensor, offset=h * P * 768 + P - 1, ap=[[767, P], [1, BAND]])
                        sync.dma_start(s_bias[h], rows).then_inc(bias_wrote, 16)

                    def segment(kind, lo, hi):
                        def body(i):
                            for b in range(2):
                                c = 2 * i + b
                                load_ahead(kind, i, b)
                                if kind == "qk":
                                    sync.wait_ge(norm.applied, c - 4 + 1)
                                    sync.dma_start(s_ab[bass.ds(c - QB0, 1)].rearrange("o q n -> (o q) n"), y[:, b, :])\
                                        .then_inc(stored[b], 16)
                                elif kind in ("v", "g"):
                                    sync.wait_ge(acc_free, c + 1)
                                    sync.dma_start(s_ab[bass.ds(c - QB0, 1)].rearrange("o q n -> (o q) n"), y[:, b, :])\
                                        .then_inc(stored[b], 16)
                                elif kind == "mq":
                                    sync.wait_ge(mq_ready, c - GA1 + 1)
                                    sync.dma_start(s_mq[bass.ds(c - GA1, 1)].rearrange("o q n -> (o q) n"), y[0:QK, b, :])\
                                        .then_inc(stored[b], 16)
                                else:
                                    sync.wait_ge(acc_free, c + 1)
                                    sync.dma_start(s_mv[bass.ds(c - MQ1, 1)].rearrange("o q n -> (o q) n"), vout[64:128, b, :])\
                                        .then_inc(v_stored[b], 16)
                                    sync.wait_ge(mk_ready, c - MQ1 + 1)
                                    sync.dma_start(s_mk[bass.ds(c - MQ1, 1)].rearrange("o q n -> (o q) n"), y[0:QK, b, :])\
                                        .then_inc(stored[b], 16)
                        loop(sync, lo, hi, body, EDGES)

                    for kind, lo, hi in LOOPS:
                        segment(kind, lo, hi)
                    sync.wait_ge(bias_wrote, 16 * (HEADS + 2))
                    for b in range(2):
                        sync.wait_ge(stored[b], 16 * (MK1 - QB0) // 2)
                        sync.wait_ge(v_stored[b], 16 * (MK1 - MQ1) // 2)

                @block.scalar
                def _(act):
                    def split(i, b, kind):
                        seg = seg_for(kind, i, 1)
                        if isinstance(i, int) and 2 * i + 2 + b == KR:
                            seg = "kr"
                        if seg:
                            c = 2 * i + 2 + b
                            wt.act_hi(act, c, b, loaded(c, b, seg) if isinstance(i, int)
                                      else loaded((c, i + 1), b, seg), kt_of(seg))

                    def to_y(i, b):
                        wait(act, stored[b], 16 * i - 16 * (QB0 // 2))

                    front.act_root(act, 0)
                    wt.act_hi(act, 0, 0, 16, KD)
                    front.act_split(act)
                    wt.act_hi(act, 1, 1, 16, KD)
                    act.wait_ge(h_parked, 16)
                    for c in range(QB0):
                        act.wait_ge(wt.used, c + 1)
                        if c < KR:
                            j = 0 if c < LAT_KV else 1
                            first = c in (LAT_Q, LAT_KV)
                            if not first:
                                wait(act, lat_added, {1: 0, 2: 1, 4: 2}[c])
                            dst = lsq[:, j, :] if first else sq[:, 0, :]
                            nc.scalar.activation(dst, acc[:, c % 2, :], ACT.Square).then_inc(lat_sq, 1)
                            nc.scalar.activation(lat[:, c, :], acc[:, c % 2, :], ACT.Copy).then_inc(acc_free, 1)
                        else:
                            nc.scalar.activation(kr[64:128, :], acc[64:128, c % 2, :], ACT.Copy).then_inc(acc_free, 1)
                        split(c // 2, c % 2, "lat")
                        if c == LAT_KV:
                            norm.act_root(act, 0)

                    def lat_split(k):
                        act.wait_ge(lat_scaled, k + 1)
                        nc.scalar.activation(l_hi[:, k, :], lat[:, k, :], ACT.Copy).then_inc(lat_hi, 1)

                    for k in range(LAT_KV):
                        lat_split(k)

                    def segment(kind, lo, hi):
                        def body(i):
                            for b in range(2):
                                c = 2 * i + b
                                if kind in ("qk", "mq"):
                                    act.wait_ge(wt.used, c + 1)
                                    to_y(i, b)
                                    if isinstance(i, int) and c == QB0:
                                        act.wait_ge(lat_added, 3)
                                        front.all_split(act)
                                    wait(act, norm.summed, c - (4 if kind == "qk" else 16) - 1)
                                    nc.scalar.activation(sq[:, b, :], acc[:, b, :], ACT.Square).then_inc(squares, 1)
                                    nc.scalar.activation(y[:, b, :], acc[:, b, :], ACT.Copy).then_inc(acc_free, 1)
                                    if isinstance(i, int) and c == QB0:
                                        norm.act_root(act, 1)
                                        for k in range(LAT_KV, 5):
                                            lat_split(k)
                                    norm.act_root(act, c - (4 if kind == "qk" else 16))
                                elif kind in ("v", "g"):
                                    act.wait_ge(wt.used, c + 1)
                                    to_y(i, b)
                                    nc.scalar.activation(y[:, b, :], acc[:, b, :], ACT.Copy if kind == "v" else ACT.Silu)\
                                        .then_inc(acc_free, 1)
                                else:
                                    to_y(i, b)
                                    nc.scalar.activation(y[64:128, b, :], kr[64:128, :], ACT.Copy).then_inc(copied, 1)
                                    act.wait_ge(wt.used, c + 1)
                                    nc.scalar.activation(y[0:64, b, :], acc[0:64, b, :], ACT.Copy).then_inc(copied, 1)
                                    wait(act, v_stored[b], 16 * i - 16 * (MQ1 // 2))
                                    nc.scalar.activation(vout[64:128, b, :], acc[64:128, b, :], ACT.Copy)\
                                        .then_inc(acc_free, 1)
                                    act.wait_ge(copied, 2 * (c - MQ1) + 2)
                                    wait(act, norm.summed, c - 16 - 1)
                                    nc.scalar.activation(sq[:, b, :], y[:, b, :], ACT.Square).then_inc(squares, 1)
                                    norm.act_root(act, c - 16)
                                split(i, b, kind)
                        loop(act, lo, hi, body, EDGES)

                    for kind, lo, hi in LOOPS:
                        segment(kind, lo, hi)

                @block.tensor
                def _(pe):
                    def main(c, b, seg, mid=None, end=None):
                        kt = kt_of(seg)
                        m_hi, m_lo = (a_hi, a_lo)
                        if seg == "mq":
                            m_hi, m_lo = l_hi[:, 0:3], l_lo[:, 0:3]
                        if seg == "mk":
                            m_hi, m_lo = l_hi[:, 3:5], l_lo[:, 3:5]
                        pe.wait_ge(wt.lo_done, c + 1)
                        wait(pe, acc_free, c - 1)
                        cut = (kt + 1) // 2
                        tile = front.pe_tile if isinstance(c, int) and c == 0 else None
                        wt.pe_multiply(pe, acc[:, b, :], b, range(cut), 0, kt - 1, m_hi, m_lo, tile=tile)
                        if mid:
                            mid()
                        wt.pe_multiply(pe, acc[:, b, :], b, range(cut, kt), 0, kt - 1, m_hi, m_lo, tile=tile)\
                            .then_inc(wt.used, 1)
                        if end:
                            end()

                    def ss_lat(n):
                        pe.wait_ge(lat_added, 2 + n)
                        norm.pe_sum(pe, n, lsq[:, n, :], ind_lat[:, 2 * n:2 * n + 2])

                    front.pe_norm(pe)
                    for c in range(QB0):
                        if c == LAT_KV + 1:
                            main(c, c % 2, seg_at(c), lambda: ss_lat(0), lambda: norm.pe_rows(pe, 0))
                        else:
                            main(c, c % 2, seg_at(c))

                    def hooks(kind, c, b):
                        n = c - (4 if kind == "qk" else 16)
                        ind = ind_head if kind == "qk" else ind_mla
                        done = c - (QB0 if kind == "qk" else GA1 - 8) + 1

                        def mid():
                            pe.wait_ge(squares, done)
                            norm.pe_sum(pe, n, sq[:, b, :], ind[:])
                        return mid, lambda: norm.pe_rows(pe, n)

                    def segment(kind, lo, hi):
                        def body(i):
                            for b in range(2):
                                c = 2 * i + b
                                mid = end = None
                                if isinstance(i, int) and c == QB0:
                                    mid, end = (lambda: ss_lat(1)), (lambda: norm.pe_rows(pe, 1))
                                elif isinstance(i, int) and c == QB1:
                                    mid, end = hooks("qk", c - 1, 1 - b)
                                elif isinstance(i, int) and c == GA1:
                                    pe.wait_ge(lat_lo, 5)
                                elif kind in ("qk", "mq", "mk"):
                                    mid, end = hooks(kind, c - 1, 1 - b)
                                main(c, b, seg_for(kind, i, 0), mid, end)
                        loop(pe, lo, hi, body, EDGES)

                    for kind, lo, hi in LOOPS:
                        segment(kind, lo, hi)
                    mid, end = hooks("mk", MK1 - 1, 1)
                    mid()
                    end()

                @block.vector
                def _(dve):
                    def split(i, b, kind):
                        seg = seg_for(kind, i, 1)
                        if isinstance(i, int) and 2 * i + 2 + b == KR:
                            seg = "kr"
                        if seg:
                            wt.dve_lo(dve, 2 * i + 2 + b, b, kt_of(seg))

                    def lat_norm(n, ks):
                        dve.wait_ge(norm.on_rows, n + 1)
                        for k in ks:
                            nc.vector.scalar_tensor_tensor(out=lat[:, k, :], in0=norm.bc[:], scalar=g_lat[:, k:k + 1],
                                                           in1=lat[:, k, :], op0=ALU.mult, op1=ALU.mult)\
                                .then_inc(lat_scaled, 1)
                        dve.wait_ge(lat_scaled, ks[-1] + 1)
                        dve.sem_inc(norm.applied, 1)
                        for k in ks:
                            dve.wait_ge(lat_hi, k + 1)
                            nc.vector.tensor_tensor(l_lo[:, k, :], lat[:, k, :], l_hi[:, k, :].bitcast(F32),
                                                    ALU.subtract).then_inc(lat_lo, 1)

                    front.dve_norm(dve)
                    wt.dve_lo(dve, 0, 0, KD)
                    front.dve_apply(dve)
                    wt.dve_lo(dve, 1, 1, KD)
                    added = 0
                    for c in range(QB0):
                        if c < KR and c not in (LAT_Q, LAT_KV):
                            j = 0 if c < LAT_KV else 1
                            dve.wait_ge(lat_sq, c + 1)
                            wait(dve, lat_added, added)
                            nc.vector.tensor_tensor(lsq[:, j, :], lsq[:, j, :], sq[:, 0, :], ALU.add)\
                                .then_inc(lat_added, 1)
                            added += 1
                        split(c // 2, c % 2, "lat")
                        if c == LAT_KV:
                            norm.dve_invert(dve, 0)
                            norm.dve_spread(dve, 0)
                    lat_norm(0, [0, 1, 2])

                    def segment(kind, lo, hi):
                        def body(i):
                            for b in range(2):
                                c = 2 * i + b
                                if kind not in ("qk", "mq", "mk"):
                                    split(i, b, kind)
                                    continue
                                if isinstance(i, int) and c == QB0:
                                    norm.dve_invert(dve, 1)
                                    norm.dve_spread(dve, 1)
                                    lat_norm(1, [3, 4])
                                n = c - (4 if kind == "qk" else 16)
                                norm.dve_invert(dve, n)
                                norm.dve_spread(dve, n)
                                split(i, b, kind)
                                dve.wait_ge(norm.on_rows, n + 1)
                                gain = g_chk[:, bass.ds(c - QB0, 1)] if kind == "qk" else \
                                    g_mla[:, 0:1] if kind == "mq" else g_mla[:, 1:2]
                                ins = nc.vector.scalar_tensor_tensor(out=y[:, b, :], in0=norm.bc[:], scalar=gain,
                                                                     in1=y[:, b, :], op0=ALU.mult, op1=ALU.mult)
                                ins.then_inc(norm.applied, 1)
                                if kind == "qk":
                                    continue
                                dve.wait_ge(norm.applied, n + 1)
                                nc.vector.tensor_tensor(rope_t[64:96, :], y[96:128, b, :], rot[96:128, :], ALU.mult)\
                                    .then_inc(roped, 1)
                                nc.vector.tensor_tensor(y[64:96, b, :], y[64:96, b, :], rot[64:96, :], ALU.mult)\
                                    .then_inc(roped, 1)
                                dve.wait_ge(roped, 2 * (c - GA1) + 2)
                                nc.vector.tensor_tensor(y[64:96, b, :], y[64:96, b, :], rope_t[64:96, :], ALU.add)\
                                    .then_inc(mq_ready if kind == "mq" else mk_ready, 1)
                        loop(dve, lo, hi, body, EDGES)

                    for kind, lo, hi in LOOPS:
                        segment(kind, lo, hi)
            sp.end()

    def stage_project_fox():
        with ExitStack() as st:
            sp = Space(st, "pf")
            NQK, NALL = 2 * FH // 2, 4 * FH // 2
            wt = Weights(sp, KD)
            y = sp.sb("y", [P, 2, S])
            front = Front(sp, g_norm[:, 1, :], y)
            norm = Norm(sp, front)
            acc = sp.ps("acc", [P, 2, S])
            sq = sp.sb("sq", [P, 2, S])
            z = sp.sb("z", [FH, S])
            e = sp.sb("e", [FH, S])
            ones = sp.sb("ones", [FH, S])
            neg_cum = sp.sb("neg_cum", [FH, S])
            acc_free = sp.sem("acc_free")
            squares = sp.sem("squares")
            gate_act = sp.sem("gate_act")
            gate_dve = sp.sem("gate_dve")
            stored = [sp.sem("stored0"), sp.sem("stored1")]
            cum_stored = sp.sem("cum_stored")
            w = fox_w_in[0]
            with nc.Block() as block:

                def run(eng, lo, hi, body):
                    body(lo)
                    if hi - lo > 3:
                        with eng.Fori(lo + 1, hi - 1) as i:
                            body(i)
                    else:
                        for i in range(lo + 1, hi - 1):
                            body(i)
                    body(hi - 1)

                @block.gpsimd
                def _(pool):
                    front.pool_split(pool)

                @block.sync
                def _(sync):
                    def load(c, b):
                        wt.load(sync, c, b, [(0, 0, w[:, bass.ds(c * P, P)])])

                    load(0, 0)
                    load(1, 1)

                    def segment(lo, hi):
                        def body(i):
                            for b in range(2):
                                c = 2 * i + b
                                if isinstance(i, int) and c + 2 >= NALL:
                                    if c + 2 == NALL:
                                        wt.load(sync, c + 2, b, [(0, 0, w[:, NALL * P:NALL * P + FH])])
                                else:
                                    load(c + 2, b)
                                sync.wait_ge(norm.applied if hi <= NQK // 2 else acc_free, c + 1)
                                sync.dma_start(s_fox[bass.ds(c, 1)].rearrange("o q n -> (o q) n"), y[:, b, :])\
                                    .then_inc(stored[b], 16)
                        run(sync, lo, hi, body)
                    segment(0, NQK // 2)
                    segment(NQK // 2, NALL // 2)
                    sync.wait_ge(gate_dve, 3)
                    sync.dma_start(s_cum, neg_cum[:]).then_inc(cum_stored, 16)
                    sync.wait_ge(cum_stored, 16)
                    for b in range(2):
                        sync.wait_ge(stored[b], 16 * NALL // 2)

                @block.scalar
                def _(act):
                    def hi_of(i, b):
                        c = 2 * i + b
                        if not isinstance(i, int) or c <= NALL:
                            wt.act_hi(act, c, b, 16 * i + 16, KD)

                    front.act_root(act, 0)
                    hi_of(0, 0)
                    front.act_split(act)
                    hi_of(0, 1)

                    def segment(kind, lo, hi):
                        def body(i):
                            for b in range(2):
                                c = 2 * i + b
                                act.wait_ge(wt.used, c + 1)
                                if kind == "qk":
                                    wait(act, norm.summed, c - 1)
                                    nc.scalar.activation(sq[:, b, :], acc[:, b, :], ACT.Square).then_inc(squares, 1)
                                wait(act, stored[b], 16 * i)
                                if isinstance(i, int) and c == 0:
                                    front.all_split(act)
                                nc.scalar.activation(y[:, b, :], acc[:, b, :], ACT.Silu if kind == "g" else ACT.Copy)\
                                    .then_inc(acc_free, 1)
                                if kind == "qk":
                                    norm.act_root(act, c)
                                hi_of(i + 1, b)
                        run(act, lo, hi, body)
                    segment("qk", 0, NQK // 2)
                    segment("v", NQK // 2, 3 * NALL // 8)
                    segment("g", 3 * NALL // 8, NALL // 2)
                    act.wait_ge(wt.used, NALL + 1)
                    nc.scalar.activation(z[:], acc[0:FH, 0, :], ACT.Identity, bias=b_f[:]).then_inc(gate_act, 1)
                    act.wait_ge(gate_act, 1)
                    nc.scalar.activation(e[:], z[:], ACT.Abs).then_inc(gate_act, 1)
                    act.wait_ge(gate_act, 2)
                    nc.scalar.activation(e[:], e[:], ACT.Exp, scale=-1.0).then_inc(gate_act, 1)
                    act.wait_ge(gate_act, 3)
                    nc.scalar.activation(e[:], e[:], ACT.Ln, bias=1.0).then_inc(gate_act, 1)

                @block.tensor
                def _(pe):
                    front.pe_norm(pe)

                    def main(c, b, mid, end):
                        pe.wait_ge(wt.lo_done, c + 1)
                        wait(pe, acc_free, c - 1)
                        tile = front.pe_tile if isinstance(c, int) and c == 0 else None
                        wt.pe_multiply(pe, acc[:, b, :], b, range(KD // 2), 0, KD - 1, a_hi, a_lo, tile=tile)
                        if mid:
                            mid()
                        wt.pe_multiply(pe, acc[:, b, :], b, range(KD // 2, KD), 0, KD - 1, a_hi, a_lo, tile=tile)\
                            .then_inc(wt.used, 1)
                        if end:
                            end()

                    def segment(kind, lo, hi):
                        def body(i):
                            for b in range(2):
                                c = 2 * i + b
                                mid = end = None
                                first = isinstance(i, int) and i == lo and b == 0
                                if (kind == "qk") != first:

                                    def mid():
                                        pe.wait_ge(squares, c)
                                        norm.pe_sum(pe, c - 1, sq[:, 1 - b, :], ind_head[:])

                                    def end():
                                        norm.pe_rows(pe, c - 1)
                                main(c, b, mid, end)
                        run(pe, lo, hi, body)
                    segment("qk", 0, NQK // 2)
                    segment("vg", NQK // 2, NALL // 2)
                    main(NALL, 0, None, None)

                @block.vector
                def _(dve):
                    def lo_of(i, b):
                        c = 2 * i + b
                        if not isinstance(i, int) or c <= NALL:
                            wt.dve_lo(dve, c, b, KD)

                    front.dve_norm(dve)
                    nc.vector.memset(ones[:], 1.0)
                    lo_of(0, 0)
                    front.dve_apply(dve)
                    lo_of(0, 1)

                    def segment(kind, lo, hi):
                        def body(i):
                            for b in range(2):
                                c = 2 * i + b
                                if kind == "qk":
                                    norm.dve_invert(dve, c)
                                    norm.dve_spread(dve, c)
                                lo_of(i + 1, b)
                                if kind == "qk":
                                    dve.wait_ge(norm.on_rows, c + 1)
                                    nc.vector.scalar_tensor_tensor(out=y[:, b, :], in0=norm.bc[:],
                                                                   scalar=g_fox[:, bass.ds(c, 1)], in1=y[:, b, :],
                                                                   op0=ALU.mult, op1=ALU.mult)\
                                        .then_inc(norm.applied, 1)
                        run(dve, lo, hi, body)
                    segment("qk", 0, NQK // 2)
                    segment("vg", NQK // 2, NALL // 2)
                    dve.wait_ge(gate_act, 4)
                    nc.vector.tensor_scalar(z[:], z[:], 0.0, None, ALU.min).then_inc(gate_dve, 1)
                    dve.wait_ge(gate_dve, 1)
                    nc.vector.tensor_tensor(e[:], e[:], z[:], ALU.subtract).then_inc(gate_dve, 1)
                    dve.wait_ge(gate_dve, 2)
                    nc.vector.tensor_tensor_scan(neg_cum[:], ones[:], e[:], 0.0, ALU.mult, ALU.add)\
                        .then_inc(gate_dve, 1)
            sp.end()

    def stage_attention(kind, heads, first_pair, q_of, k_of, v_of, g_of, extra_of):
        mla, chk, fox = (kind == k for k in ("mla", "chk", "fox"))
        NT = ST
        NP2 = heads // 2

        def lowest(t):
            return max(0, t - BAND // P + 1) if chk else 0

        def turned(t):
            js = list(range(lowest(t), t + 1))
            return [js[n:n + 4] for n in range(0, len(js), 4)]

        PIECES = [len(turned(t)) for t in range(NT)]
        BEFORE = [sum(PIECES[:t]) for t in range(NT + 1)]
        NPC = BEFORE[NT]
        assert NPC % 2 == 0

        with ExitStack() as st:
            sp = Space(st, kind)
            raw = sp.sb("raw", [P, 2, S])
            q_hi = sp.sb("q_hi", [P, 2, S], F32R)
            k_hi = sp.sb("k_hi", [P, 2, S], F32R)
            k_lo = sp.sb("k_lo", [P, 2, S], F32R)
            q_lo = sp.sb("q_lo", [P, 2, S], F32R) if mla else None
            extra = None if mla else sp.sb("extra", [P, 2, BAND if chk else S])
            v_raw = sp.sb("v_raw", [64, S])
            v = sp.sb("v", [P, 2, ST, P], F32R)
            gate = sp.sb("gate", [P, S])
            o = sp.sb("o", [P, S])
            o_low = sp.sb("o_low", [64, 2 * P])
            WIDE = BAND if chk else S
            prob = sp.sb("prob", [P, 4, WIDE])
            pt_hi = sp.sb("pt_hi", [P, 2, WIDE // P + chk, 2 * P], F32R)
            pt_lo = sp.sb("pt_lo", [P, 2, WIDE // P + chk, 2 * P], F32R)
            neg_max = sp.sb("neg_max", [P, 4])
            total = sp.sb("total", [P, 4])
            inverse = sp.sb("inverse", [P, 4])
            spare = sp.sb("spare", [P, 2])
            scores = sp.ps("scores", [P, 2, S])
            turn = sp.ps("turn", [P, 2, 4, P])
            pv = sp.ps("pv", [P, 2 * P])
            vt = sp.ps("vt", [P, ST, 64])

            in_q, in_k, in_v = sp.sem("in_q"), sp.sem("in_k"), sp.sem("in_v")
            in_g = [sp.sem("in_g0"), sp.sem("in_g1")]
            in_x = [sp.sem("in_x0"), sp.sem("in_x1")]
            q_hi_done, q_lo_done = sp.sem("q_hi_done"), sp.sem("q_lo_done")
            k_hi_done, k_lo_done = sp.sem("k_hi_done"), sp.sem("k_lo_done")
            v_turned, v_hi_done, v_lo_done = sp.sem("v_turned"), sp.sem("v_hi_done"), sp.sem("v_lo_done")
            scored = sp.sem("scored")
            maxed = sp.sem("maxed")
            exped = sp.sem("exped")
            inverted = sp.sem("inverted")
            normed = sp.sem("normed")
            pieces_turned = sp.sem("pieces_turned")
            pt_hi_done, pt_lo_done = sp.sem("pt_hi_done"), sp.sem("pt_lo_done")
            pv_done = sp.sem("pv_done")
            o_low_done, o_done = sp.sem("o_low_done"), sp.sem("o_done")
            gated, out_hi, out_lo = sp.sem("gated"), sp.sem("out_hi"), sp.sem("out_lo")
            NDMA = 1 if mla else 2
            KROWS = QK if mla else P

            def over_heads(eng, head, tail=None):
                def body(i, final=False):
                    for b in range(2):
                        head(i, b, 2 * i + b, final and b == 1)
                body(0)
                if NP2 > 3:
                    with eng.Fori(1, NP2 - 1) as i:
                        body(i)
                else:
                    for i in range(1, NP2 - 1):
                        body(i)
                body(NP2 - 1, True)

            with nc.Block() as block:

                @block.sync
                def _(sync):
                    def load(hd, b, m):
                        for dst, src, sem, done in ((0, q_of(hd), in_q, q_lo_done), (1, k_of(hd), in_k, k_lo_done)):
                            wait(sync, done, hd)
                            rows = src.shape[0]
                            for n in range(NDMA):
                                sync.dma_start(raw[n * rows:(n + 1) * rows, dst, :], src).then_inc(sem, 16)
                        wait(sync, v_turned, hd)
                        sync.dma_start(v_raw[:], v_of(hd)).then_inc(in_v, 16)
                        if extra is not None:
                            wait(sync, maxed, NT * (hd - 1))
                            sync.dma_start(extra[:, b, :], extra_of(hd)).then_inc(in_x[b], 16)
                        wait(sync, gated, hd - 1)
                        sync.dma_start(gate[64 * b:64 * b + 64, :], g_of(hd)).then_inc(in_g[b], 16)

                    load(0, 0, 0)

                    def head(i, b, hd, last):
                        if not last:
                            load(hd + 1, 1 - b, i + b)
                    over_heads(sync, head)

                def lo_slices():
                    return (q_lo, slice(0, QK)) if mla else (q_hi, slice(64, P))

                @block.scalar
                def _(act):
                    def split_q(hd, b):
                        act.wait_ge(in_q, 16 * NDMA * (hd + 1))
                        wait(act, scored, NT * (hd - 1))
                        nc.scalar.activation(q_hi[0:KROWS, b, :], raw[0:KROWS, 0, :], ACT.Copy).then_inc(q_hi_done, 1)

                    def split_k(hd, b):
                        act.wait_ge(in_k, 16 * NDMA * (hd + 1))
                        nc.scalar.activation(k_hi[0:KROWS, b, :], raw[0:KROWS, 1, :], ACT.Copy).then_inc(k_hi_done, 1)

                    def split_v(hd, b):
                        act.wait_ge(v_turned, hd + 1)
                        wait(act, pv_done, NT // 2 * (hd - 1))
                        nc.scalar.activation(v[:, b, :, 0:64], vt[:], ACT.Copy).then_inc(v_hi_done, 1)

                    def evacuate(hd, t):
                        for n, js in enumerate(turned(t)):
                            g = BEFORE[t] + n
                            u = t // 2
                            act.wait_ge(pieces_turned, NPC * hd + g + 1)
                            wait(act, pv_done, NT // 2 * hd + u - 1)
                            at = js[0] - lowest(2 * u)
                            nc.scalar.activation(pt_hi[:, u % 2, at:at + len(js), (t % 2) * P:(t % 2 + 1) * P],
                                                 turn[:, g % 2, 0:len(js), :], ACT.Copy).then_inc(pt_hi_done, 1)

                    def low_half(hd, u):
                        act.wait_ge(pv_done, NT // 2 * hd + u + 1)
                        wait(act, o_done, NT // 2 * hd + u)
                        nc.scalar.activation(o_low[:], pv[64:P, :], ACT.Copy).then_inc(o_low_done, 1)

                    def give(m, b, hd):
                        act.wait_ge(gated, hd + 1)
                        r = slice(64 * b, 64 * b + 64)
                        nc.scalar.activation(a_hi[r, bass.ds(m + first_pair, 1), :].rearrange("q o n -> q (o n)"), o[r, :],
                                             ACT.Copy).then_inc(out_hi, 1)

                    split_q(0, 0)
                    split_k(0, 0)
                    split_v(0, 0)

                    def head(i, b, hd, last):
                        for t in range(NT):
                            before = hd if t >= 3 else hd - 1
                            if not (isinstance(hd, int) and before < 0):
                                evacuate(before, (t - 3) % NT)
                            if t % 2 == 0:
                                if t >= 6:
                                    low_half(hd, (t - 6) // 2)
                                elif not (isinstance(hd, int) and hd == 0):
                                    low_half(hd - 1, (t + NT - 6) // 2)
                            if t == 7 and not (isinstance(hd, int) and hd == 0):
                                give(i - 1 + b, 1 - b, hd - 1)
                            if not last:
                                if t == 1:
                                    split_q(hd + 1, 1 - b)
                                if t == 2:
                                    split_k(hd + 1, 1 - b)
                                if t == 5:
                                    split_v(hd + 1, 1 - b)
                            s = NT * hd + t
                            act.wait_ge(maxed, s + 1)
                            n = (t + 1 - lowest(t)) * P
                            src = scores[:, t % 2, 0:n] if mla else prob[:, t % 4, 0:n]
                            if mla:
                                wait(act, pieces_turned, NPC * hd + BEFORE[t - 4] + PIECES[t - 4] if t >= 4 else
                                     NPC * (hd - 1) + BEFORE[t + NT - 4] + PIECES[t + NT - 4])
                            nc.scalar.activation(prob[:, t % 4, 0:n], src, ACT.Exp, bias=neg_max[:, t % 4:t % 4 + 1],
                                                 scale=1.0 if mla else -1.0,
                                                 accum_out=total[:, t % 4:t % 4 + 1]).then_inc(exped, 1)
                    over_heads(act, head)
                    hd = heads - 1
                    evacuate(hd, NT - 3)
                    low_half(hd, NT // 2 - 3)
                    evacuate(hd, NT - 2)
                    evacuate(hd, NT - 1)
                    low_half(hd, NT // 2 - 2)
                    low_half(hd, NT // 2 - 1)
                    give(NP2 - 1, 1, hd)

                @block.gpsimd
                def _(pool):
                    def split(hd, b):
                        dst, r = lo_slices()
                        wait(pool, out_lo, hd - 2)
                        wait(pool, k_lo_done, hd)
                        pool.wait_ge(q_hi_done, hd + 1)
                        nc.gpsimd.tensor_tensor(dst[r, b, :], raw[r, 0, :], q_hi[r, b, :].bitcast(F32), ALU.subtract)\
                            .then_inc(q_lo_done, 1)
                        pool.wait_ge(q_lo_done, hd + 1)
                        pool.wait_ge(k_hi_done, hd + 1)
                        nc.gpsimd.tensor_tensor(k_lo[0:KROWS, b, :], raw[0:KROWS, 1, :],
                                                k_hi[0:KROWS, b, :].bitcast(F32), ALU.subtract).then_inc(k_lo_done, 1)

                    def give(m, b, hd, final):
                        r = slice(64 * b, 64 * b + 64)
                        pool.wait_ge(k_lo_done, heads if final else hd + 3)
                        wait(pool, out_lo, hd)
                        pool.wait_ge(o_done, NT // 2 * (hd + 1))
                        pool.wait_ge(in_g[b], 16 * (m + 1))
                        nc.gpsimd.tensor_tensor(o[r, :], o[r, :], gate[r, :], ALU.mult).then_inc(gated, 1)
                        pool.wait_ge(gated, hd + 1)
                        pool.wait_ge(out_hi, hd + 1)
                        at = bass.ds(m + first_pair, 1)
                        nc.gpsimd.tensor_tensor(a_lo[r, at, :].rearrange("q o n -> q (o n)"), o[r, :],
                                                a_hi[r, at, :].rearrange("q o n -> q (o n)").bitcast(F32),
                                                ALU.subtract).then_inc(out_lo, 1)

                    split(0, 0)

                    def head(i, b, hd, last):
                        if not last:
                            split(hd + 1, 1 - b)
                        if not (isinstance(hd, int) and hd == 0):
                            give(i - 1 + b, 1 - b, hd - 1, last)
                    over_heads(pool, head)
                    give(NP2 - 1, 1, heads - 1, True)

                @block.tensor
                def _(pe):
                    def before_turn_v(hd):
                        pe.wait_ge(in_v, 16 * (hd + 1))
                        wait(pe, v_lo_done, hd)

                    def turn_v(hd):
                        for j in range(ST):
                            last = nc.tensor.transpose(vt[:, j, :], v_raw[:, j * P:(j + 1) * P], ident[0:64, 0:64])
                        last.then_inc(v_turned, 1)

                    def score(hd, b, t):
                        s = NT * hd + t
                        if t == 0:
                            pe.wait_ge(q_lo_done, hd + 1)
                            pe.wait_ge(k_lo_done, hd + 1)
                        wait(pe, exped if mla else maxed, s - 1)
                        lo = lowest(t)
                        n = (t + 1 - lo) * P
                        q = slice(t * P, (t + 1) * P)
                        for c in range(0, n, HALF):
                            w = min(HALF, n - c)
                            dst = scores[:, t % 2, c:c + w]
                            keys = slice(lo * P + c, lo * P + c + w)
                            R = slice(0, KROWS)
                            terms = [(q_hi, k_hi), (q_lo, k_hi), (q_hi, k_lo)] if mla else [(q_hi, k_hi), (q_hi, k_lo)]
                            masks = []
                            if c + w == n:
                                if chk:
                                    masks.append((slice(w - CHUNK, w), low_q))
                                else:
                                    masks.append((slice(w - P, w), causal if fox else blockc))
                            if chk and c == 0 and t >= BAND // P - 1:
                                masks.append((slice(0, CHUNK), high_q))
                            for m, (a, k) in enumerate(terms):
                                ins = nc.tensor.matmul(dst, a[R, b, q], k[R, b, keys], start=(m == 0),
                                                       stop=(m == len(terms) - 1))
                                if m == 0:
                                    for cols, mask in masks:
                                        nc.tensor.matmul(dst[:, cols], ident_b[:], mask[:], start=False, stop=False)
                        ins.then_inc(scored, 1)

                    def turn_p(hd, t):
                        pe.wait_ge(normed, NT * hd + t + 1)
                        lo = lowest(t)
                        for n, js in enumerate(turned(t)):
                            g = BEFORE[t] + n
                            wait(pe, pt_lo_done, NPC * hd + g - 1)
                            for m, j in enumerate(js):
                                last = nc.tensor.transpose(turn[:, g % 2, m, :], prob[:, t % 4, (j - lo) * P:(j - lo + 1) * P],
                                                           ident[:])
                            last.then_inc(pieces_turned, 1)

                    def times_v(hd, b, u):
                        pe.wait_ge(pt_lo_done, NPC * hd + BEFORE[2 * u + 2])
                        wait(pe, o_done, NT // 2 * hd + u)
                        if u == 0:
                            pe.wait_ge(v_lo_done, hd + 1)
                        lo0, lo1 = lowest(2 * u), lowest(2 * u + 1)
                        js = [j for j in range(lo1, 2 * u + 1)] + [2 * u + 1] + list(range(lo0, lo1))
                        terms = [(j, part) for j in js for part in (pt_hi, pt_lo)]
                        for m, (j, part) in enumerate(terms):
                            cols = slice(P, 2 * P) if j == 2 * u + 1 else slice(0, P) if j < lo1 else slice(0, 2 * P)
                            ins = nc.tensor.matmul(pv[:, cols], v[:, b, j, :], part[:, u % 2, j - lo0, cols],
                                                   start=(m == 0), stop=(m == len(terms) - 1))
                        ins.then_inc(pv_done, 1)

                    before_turn_v(0)
                    turn_v(0)

                    def head(i, b, hd, last):
                        first = isinstance(hd, int) and hd == 0
                        for t in range(NT):
                            score(hd, b, t)
                            if t == 6:
                                times_v(hd, b, 0)
                            if t in (0, 2, 4) and not first:
                                times_v(hd - 1, 1 - b, (t + NT) // 2 - 3)
                            if t == 4 and not last:
                                before_turn_v(hd + 1)
                            if t >= 3:
                                turn_p(hd, t - 3)
                            elif not first:
                                turn_p(hd - 1, t - 3 + NT)
                            if t == 4 and not last:
                                turn_v(hd + 1)
                    over_heads(pe, head)
                    hd = heads - 1
                    times_v(hd, 1, NT // 2 - 3)
                    turn_p(hd, NT - 3)
                    turn_p(hd, NT - 2)
                    times_v(hd, 1, NT // 2 - 2)
                    turn_p(hd, NT - 1)
                    times_v(hd, 1, NT // 2 - 1)

                @block.vector
                def _(dve):
                    def split_v(hd, b):
                        dve.wait_ge(v_hi_done, hd + 1)
                        nc.vector.tensor_tensor(v[:, b, :, 64:128], vt[:], v[:, b, :, 0:64].bitcast(F32), ALU.subtract)\
                            .then_inc(v_lo_done, 1)

                    def normalise(hd, t):
                        s = NT * hd + t
                        lo = lowest(t)
                        n = (t + 1 - lo) * P
                        r = slice(t % 4, t % 4 + 1)
                        dve.wait_ge(exped, s + 1)
                        nc.vector.reciprocal(inverse[:, r], total[:, r]).then_inc(inverted, 1)
                        dve.wait_ge(inverted, s + 1)
                        nc.vector.tensor_scalar(prob[:, t % 4, 0:n], prob[:, t % 4, 0:n], inverse[:, r], None, ALU.mult)\
                            .then_inc(normed, 1)

                    def row_max(hd, b, t):
                        s = NT * hd + t
                        lo = lowest(t)
                        n = (t + 1 - lo) * P
                        r = slice(t % 4, t % 4 + 1)
                        if mla:
                            dve.wait_ge(scored, s + 1)
                            nc.vector.tensor_reduce(neg_max[:, r], scores[:, t % 2, 0:n], AX_X, ALU.max, negate=True)\
                                .then_inc(maxed, 1)
                            return
                        x = extra[:, b, BAND - n:BAND] if chk else extra[:, b, 0:n]
                        nc.vector.tensor_tensor_reduce(out=prob[:, t % 4, 0:n], in0=scores[:, t % 2, 0:n], in1=x,
                                                       scale=-1.0, scalar=BIG, op0=ALU.add, op1=ALU.min,
                                                       accum_out=neg_max[:, r]).then_inc(maxed, 1)

                    def before_max(i, hd, b, t):
                        s = NT * hd + t
                        if mla:
                            return
                        dve.wait_ge(scored, s + 1)
                        wait(dve, pieces_turned, NPC * hd + BEFORE[t - 4] + PIECES[t - 4] if t >= 4 else
                             NPC * (hd - 1) + BEFORE[t + NT - 4] + PIECES[t + NT - 4])
                        if t == 0:
                            dve.wait_ge(in_x[b], 16 * i + 16)

                    def evacuate(hd, t):
                        for n, js in enumerate(turned(t)):
                            g = BEFORE[t] + n
                            u = t // 2
                            dve.wait_ge(pt_hi_done, NPC * hd + g + 1)
                            at = js[0] - lowest(2 * u)
                            where = (slice(None), u % 2, slice(at, at + len(js)), slice((t % 2) * P, (t % 2 + 1) * P))
                            nc.vector.tensor_tensor(pt_lo[where], turn[:, g % 2, 0:len(js), :], pt_hi[where].bitcast(F32),
                                                    ALU.subtract).then_inc(pt_lo_done, 1)

                    def add_halves(hd, b, u):
                        dve.wait_ge(o_low_done, NT // 2 * hd + u + 1)
                        if u == 0:
                            wait(dve, out_lo, hd - 1)
                        nc.vector.tensor_tensor(o[64 * b:64 * b + 64, 2 * u * P:2 * (u + 1) * P], pv[0:64, :], o_low[:],
                                                ALU.add).then_inc(o_done, 1)

                    split_v(0, 0)

                    def head(i, b, hd, last):
                        first = isinstance(hd, int) and hd == 0
                        for t in range(NT):
                            before_max(i, hd, b, t)
                            if t >= 2:
                                normalise(hd, t - 2)
                            elif not first:
                                normalise(hd - 1, NT - 2 + t)
                            elif not mla:
                                nc.vector.memset(spare[:, t:t + 1], 0.0)
                            row_max(hd, b, t)
                            if t >= 3:
                                evacuate(hd, t - 3)
                            elif not first:
                                evacuate(hd - 1, t - 3 + NT)
                            if t % 2 == 0:
                                if t >= 6:
                                    add_halves(hd, b, t // 2 - 3)
                                elif not first:
                                    add_halves(hd - 1, 1 - b, (t + NT) // 2 - 3)
                            if t == 5 and not last:
                                split_v(hd + 1, 1 - b)
                    over_heads(dve, head)
                    hd = heads - 1
                    normalise(hd, NT - 2)
                    evacuate(hd, NT - 3)
                    add_halves(hd, 1, NT // 2 - 3)
                    normalise(hd, NT - 1)
                    evacuate(hd, NT - 2)
                    evacuate(hd, NT - 1)
                    add_halves(hd, 1, NT // 2 - 2)
                    add_halves(hd, 1, NT // 2 - 1)
            sp.end()

    def stage_output(tag, weights, parked=False):
        with ExitStack() as st:
            sp = Space(st, tag)
            wt = Weights(sp, KD)
            acc = sp.ps("acc", [P, 2, S])
            added = sp.sem("added")
            h_back = sp.sem("h_back")
            squares = Squares(sp, added)
            with nc.Block() as block:

                @block.sync
                def _(sync):
                    def body(i):
                        for b in range(2):
                            c = 2 * i + b
                            wt.load(sync, c, b, [(0, 0, weights[:, bass.ds(c * P, P)])])
                            if parked and isinstance(i, int) and c == 1:
                                sync.dma_start(hT[:], s_h).then_inc(h_back, 16)
                    pairs(sync, 0, KD // 2, body)

                @block.scalar
                def _(act):
                    def body(i):
                        for b in range(2):
                            wt.act_hi(act, 2 * i + b, b, 16 * i + 16, KD)
                            if not (isinstance(i, int) and i == 0 and b == 0):
                                squares.act_square(act, 2 * i + b - 1, 1 - b)
                    pairs(act, 0, KD // 2, body)
                    squares.act_square(act, KD - 1, 1)

                @block.tensor
                def _(pe):
                    def body(i):
                        for b in range(2):
                            c = 2 * i + b
                            pe.wait_ge(wt.lo_done, c + 1)
                            wait(pe, added, c - 1)
                            wt.pe_multiply(pe, acc[:, b, :], b, range(KD), 0, KD - 1, a_hi, a_lo).then_inc(wt.used, 1)
                    pairs(pe, 0, KD // 2, body)

                @block.vector
                def _(dve):
                    def add(c, b):
                        dve.wait_ge(wt.used, c + 1)
                        at = bass.ds(c, 1)
                        rows = hT[:, at, :].rearrange("q o n -> q (o n)")
                        nc.vector.tensor_tensor(rows, acc[:, b, :], rows, ALU.add).then_inc(added, 1)

                    def body(i):
                        for b in range(2):
                            c = 2 * i + b
                            wt.dve_lo(dve, c, b, KD)
                            if parked and isinstance(i, int) and c == 1:
                                dve.wait_ge(h_back, 16)
                            if not (isinstance(i, int) and c == 0):
                                add(c - 1, 1 - b)
                            if not (isinstance(i, int) and c < 2):
                                squares.dve_gather(dve, c - 2, b)
                    pairs(dve, 0, KD // 2, body)
                    add(KD - 1, 1)
                    squares.dve_gather(dve, KD - 2, 0)
                    squares.dve_gather(dve, KD - 1, 1)
            sp.end()

    def stage_ple(tag, layer):
        with ExitStack() as st:
            sp = Space(st, tag)
            KP = PLE // P
            wt = Weights(sp, KD + KP)
            acc = sp.ps("acc", [P, 2, S])
            pt = acc[:].rearrange("q k (t n) -> q k t n", t=ST)
            pr = sp.sb("pr", [P, ST, PLE])
            p_hi = sp.sb("p_hi", [P, KP, S], F32R)
            p_lo = sp.sb("p_lo", [P, KP, S], F32R)
            gate = sp.sb("gate", [P, 2, S])
            p_in = sp.sem("p_in")
            p_turned = sp.sem("p_turned")
            p_hi_done, p_lo_done = sp.sem("p_hi_done"), sp.sem("p_lo_done")
            gates_summed = sp.sem("gates_summed")
            gate_done = sp.sem("gate_done")
            gated = sp.sem("gated")
            added = sp.sem("added")
            front = Front(sp, g_gate[:, layer, :], gate)
            squares = None if layer == 1 else Squares(sp, added)
            with nc.Block() as block:

                @block.gpsimd
                def _(pool):
                    front.pool_split(pool)

                @block.sync
                def _(sync):
                    sync.dma_start(pr[:], p[layer, 0].rearrange("(t q) n -> q t n", q=P)).then_inc(p_in, 16)

                    def body(i):
                        for b in range(2):
                            c = 2 * i + b
                            cols = bass.ds(c * P, P)
                            wt.load(sync, c, b, [(0, 0, pe_gate_w[layer][:, cols]), (0, KD, pe_w[layer][:, cols])])
                    pairs(sync, 0, KD // 2, body)

                @block.scalar
                def _(act):
                    front.act_root(act, 0)
                    act.wait_ge(p_turned, 1)
                    for k in range(KP):
                        nc.scalar.activation(p_hi[:, k, :].rearrange("q (t n) -> q t n", t=ST), pt[:, k, :, :], ACT.Copy)\
                            .then_inc(p_hi_done, 1)

                    def gates(c, b):
                        act.wait_ge(gates_summed, c + 1)
                        wait(act, gated, c - 1)
                        nc.scalar.activation(gate[:, b, :], acc[:, 0, :], ACT.Sigmoid).then_inc(gate_done, 1)

                    def body(i):
                        for b in range(2):
                            c = 2 * i + b
                            wt.act_hi(act, c, b, 32 * i + 32, KD + KP)
                            if isinstance(i, int) and c == 0:
                                front.act_split(act)
                                front.all_split(act)
                            else:
                                gates(c - 1, 1 - b)
                            if squares and not (isinstance(i, int) and c < 2):
                                squares.act_square(act, c - 2, b)
                    pairs(act, 0, KD // 2, body)
                    gates(KD - 1, 1)
                    if squares:
                        squares.act_square(act, KD - 2, 0)
                        squares.act_square(act, KD - 1, 1)

                @block.tensor
                def _(pe):
                    pe.wait_ge(p_in, 16)
                    for t in range(ST):
                        for k in range(KP):
                            last = nc.tensor.transpose(pt[:, k, t, :], pr[:, t, k * P:(k + 1) * P], ident[:])
                    last.then_inc(p_turned, 1)
                    front.pe_norm(pe)

                    def body(i):
                        for b in range(2):
                            c = 2 * i + b
                            pe.wait_ge(wt.lo_done, c + 1)
                            wait(pe, gate_done, c)
                            if isinstance(i, int) and c == 0:
                                pe.wait_ge(p_lo_done, KP)
                            wt.pe_multiply(pe, acc[:, 0, :], b, range(KD), 0, KD - 1, a_hi, a_lo,
                                           tile=front.pe_tile if isinstance(i, int) and c == 0 else None)\
                                .then_inc(gates_summed, 1)
                            wait(pe, gated, c)
                            wt.pe_multiply(pe, acc[:, 1, :], b, range(KP), 0, KP - 1, p_hi, p_lo, k0=KD)\
                                .then_inc(wt.used, 1)
                    pairs(pe, 0, KD // 2, body)

                @block.vector
                def _(dve):
                    front.dve_norm(dve)
                    for k in range(KP):
                        dve.wait_ge(p_hi_done, k + 1)
                        nc.vector.tensor_tensor(p_lo[:, k, :].rearrange("q (t n) -> q t n", t=ST), pt[:, k, :, :],
                                                p_hi[:, k, :].rearrange("q (t n) -> q t n", t=ST).bitcast(F32),
                                                ALU.subtract).then_inc(p_lo_done, 1)

                    def add(c, b):
                        dve.wait_ge(wt.used, c + 1)
                        dve.wait_ge(gate_done, c + 1)
                        nc.vector.tensor_tensor(gate[:, b, :], acc[:, 1, :], gate[:, b, :], ALU.mult).then_inc(gated, 1)
                        dve.wait_ge(gated, c + 1)
                        rows = hT[:, bass.ds(c, 1), :].rearrange("q o n -> q (o n)")
                        nc.vector.tensor_tensor(rows, rows, gate[:, b, :], ALU.add).then_inc(added, 1)

                    def body(i):
                        for b in range(2):
                            c = 2 * i + b
                            wt.dve_lo(dve, c, b, KD + KP)
                            if isinstance(i, int) and c == 0:
                                front.dve_apply(dve)
                            else:
                                add(c - 1, 1 - b)
                            if squares and not (isinstance(i, int) and c < 3):
                                squares.dve_gather(dve, c - 3, 1 - b)
                    pairs(dve, 0, KD // 2, body)
                    add(KD - 1, 1)
                    if squares:
                        for c in range(KD - 3, KD):
                            squares.dve_gather(dve, c, c % 2)
            sp.end()

    def stage_result():
        with ExitStack() as st:
            sp = Space(st, "re")
            ht = sp.ps("ht", [P, 2, KD, P])
            row = sp.sb("row", [P, 2, D])
            turned = sp.sem("turned")
            from_act, from_dve = sp.sem("from_act"), sp.sem("from_dve")
            stored = [sp.sem("stored0"), sp.sem("stored1")]
            H2 = KD // 2 * P
            with nc.Block() as block:

                @block.sync
                def _(sync):
                    for t in range(ST):
                        sync.wait_ge(from_act, t + 1)
                        sync.wait_ge(from_dve, t + 1)
                        sync.dma_start(out[0, t * P:(t + 1) * P, :], row[:, t % 2, :]).then_inc(stored[t % 2], 16)
                    for b in range(2):
                        sync.wait_ge(stored[b], 16 * ST // 2)

                @block.tensor
                def _(pe):
                    for t in range(ST):
                        wait(pe, from_act, t - 1)
                        wait(pe, from_dve, t - 1)
                        for k in range(KD):
                            last = nc.tensor.transpose(ht[:, t % 2, k, :], hT[:, k, t * P:(t + 1) * P], ident[:])
                        last.then_inc(turned, 1)

                @block.scalar
                def _(act):
                    for t in range(ST):
                        act.wait_ge(turned, t + 1)
                        wait(act, stored[t % 2], 16 * (t // 2))
                        nc.scalar.activation(row[:, t % 2, 0:H2], ht[:, t % 2, 0:KD // 2, :].rearrange("q k n -> q (k n)"),
                                             ACT.Copy).then_inc(from_act, 1)

                @block.vector
                def _(dve):
                    for t in range(ST):
                        dve.wait_ge(turned, t + 1)
                        wait(dve, stored[t % 2], 16 * (t // 2))
                        nc.vector.tensor_copy(row[:, t % 2, H2:D], ht[:, t % 2, KD // 2:KD, :].rearrange("q k n -> q (k n)"))\
                            .then_inc(from_dve, 1)
            sp.end()

    with top, nc.allow_non_contiguous_dma(reason="gains, a column each"):
        with ExitStack() as first:
            rot = Space(first, "r").sb("rot", [P, S])
            stage_entry(rot)
            stage_project_ab(rot)

        def slab(src, rows, at=0):
            return lambda hd: src[bass.ds(hd + at, 1)].rearrange("o q n -> (o q) n")

        ab = s_ab.rearrange("c (h q) n -> (c h) q n", h=2)
        fx = s_fox.rearrange("c (h q) n -> (c h) q n", h=2)
        stage_attention("mla", HEADS, 0, slab(s_mq, QK), slab(s_mk, QK), slab(s_mv, VDIM),
                        slab(ab, 64, 4 * HEADS), None)
        stage_attention("chk", HEADS, HEADS // 2, slab(ab, 64), slab(ab, 64, HEADS), slab(ab, 64, 2 * HEADS),
                        slab(ab, 64, 3 * HEADS), slab(s_bias, P))
        with ExitStack() as between:
            h_sq[0] = Space(between, "b0").sb("h_sq", [P, S])
            stage_output("o0", ab_w_out[0], parked=True)
            stage_ple("e0", 0)
            stage_project_fox()
        stage_attention("fox", FH, 0, slab(fx, 64), slab(fx, 64, FH), slab(fx, 64, 2 * FH), slab(fx, 64, 3 * FH),
                        lambda hd: s_cum[bass.ds(hd, 1), :].to_broadcast([P, S]))
        with ExitStack() as between:
            h_sq[0] = Space(between, "b1").sb("h_sq", [P, S])
            stage_output("o1", fox_w_out[0])
            stage_ple("e1", 1)
        stage_result()


_INS = ["x", "p", "positions", "norm_g", "ab_w_in", "mla_q_norm", "mla_w_uq", "mla_kv_norm", "mla_w_ukv",
        "mla_q_gain", "mla_k_gain", "chk_q_gain", "chk_k_gain", "chk_rel_bias", "ab_w_out",
        "fox_w_in", "fox_b_f", "fox_q_gain", "fox_k_gain", "fox_w_out", "pe_w", "pe_gate_norm", "pe_gate_w"]


def kernel(**inputs):
    import concourse.bacc as bacc
    from concourse.bass_utils import run_bass_kernel_spmd

    nc = bacc.Bacc("TRN2", target_bir_lowering=False, num_devices=1)
    arrays = {name: np.ascontiguousarray(inputs[name]) for name in _INS}
    half = ROPE // 2
    freq = (np.float32(1.0) / (np.float32(10000.0) ** (np.arange(half, dtype=np.float32) / np.float32(half))))
    arrays["rope_freq"] = np.concatenate([freq, freq, -freq, freq]).astype(np.float32)[:, None]
    args = {name: nc.dram_tensor(f"in_{name}", a.shape, mybir.dt.from_np(a.dtype), kind="ExternalInput").ap()
            for name, a in arrays.items()}
    out = nc.dram_tensor("out_0", (1, S, D), F32, kind="ExternalOutput").ap()
    build(nc, **args, out=out)
    r = run_bass_kernel_spmd(nc, [{f"in_{name}": a for name, a in arrays.items()}], core_ids=[0])
    return r.results[0]["out_0"]
```

```python
from contextlib import ExitStack

import numpy as np

import concourse.bass as bass
from concourse import mybir

F32 = mybir.dt.float32
F32R = mybir.dt.float32r
BF16 = mybir.dt.bfloat16
I32 = mybir.dt.int32
ALU = mybir.AluOpType
ACT = mybir.ActivationFunctionType
AX_X = mybir.AxisListType.X

P = 128
D = 1024
S = 1024
KD = D // P
ST = S // P
HALF = 512
NH = S // HALF
PLE = 256
EPS = 1e-6
NEG = -1e30
BIG = 3.0e38

HEADS = 8
NOPE, ROPE, VDIM = 64, 32, 64
QK = NOPE + ROPE
QLORA, KVLORA = 384, 256
CHK = 64
LEFT = 8
BAND = 640
CHUNK = 64
CLIP = 256
FH = 16
FD = 64

C_KR = QLORA + KVLORA
C_GA = C_KR + ROPE
C_QB = C_GA + HEADS * VDIM

LAT_Q, LAT_KV, KR = 0, 3, 5
QB0, QB1 = 6, 14
VB1 = 18
GB1 = 22
GA1 = 26
MQ1 = 34
MK1 = 42


def wait(eng, sem, value):
    if isinstance(value, int) and value <= 0:
        return
    eng.wait_ge(sem, value)


def pairs(eng, lo, hi, body):
    body(lo)
    body(lo + 1)
    with eng.Fori(lo + 2, hi) as i:
        body(i)


def build(nc, x, p, positions, norm_g, ab_w_in, mla_q_norm, mla_w_uq, mla_kv_norm, mla_w_ukv,
          mla_q_gain, mla_k_gain, chk_q_gain, chk_k_gain, chk_rel_bias, ab_w_out,
          fox_w_in, fox_b_f, fox_q_gain, fox_k_gain, fox_w_out, pe_w, pe_gate_norm, pe_gate_w,
          rope_freq, out):
    top = ExitStack()

    def dram(name, shape):
        return nc.dram_tensor(name, shape, F32, kind="Internal").ap()

    s_h = dram("s_h", [P, KD, S])
    s_ab = dram("s_ab", [GA1 - QB0, P, S])
    s_mq = dram("s_mq", [HEADS, QK, S])
    s_mk = dram("s_mk", [HEADS, QK, S])
    s_mv = dram("s_mv", [HEADS, VDIM, S])
    s_fox = dram("s_fox", [4 * FH // 2, P, S])
    s_cum = dram("s_cum", [FH, S])
    s_rel = dram("s_rel", [HEADS, 768])
    s_rep = dram("s_rep", [HEADS, P, 768])
    s_bias = dram("s_bias", [HEADS, P, BAND])

    class Space:

        def __init__(self, stack, tag):
            self.stack, self.tag, self.numbers = stack, tag, []

        def sb(self, name, shape, dt=F32):
            return self.stack.enter_context(nc.sbuf_tensor(f"{self.tag}_{name}", shape, dt))

        def ps(self, name, shape, dt=F32):
            return self.stack.enter_context(nc.psum_tensor(f"{self.tag}_{name}", shape, dt))

        def sem(self, name):
            handle = self.stack.enter_context(nc.semaphore(f"{self.tag}_{name}"))
            self.numbers.append(handle.num)
            return handle

        def end(self):
            numbers = sorted(self.numbers)
            while numbers:
                n = next((k for k in range(1, len(numbers)) if numbers[k] != numbers[0] + k), len(numbers))
                nc.all_engine_barrier(sems_to_clear=range(numbers[0], numbers[0] + n))
                numbers = numbers[n:]

    G = Space(top, "g")
    hT = G.sb("hT", [P, KD, S])
    a_hi = G.sb("a_hi", [P, KD, S], F32R)
    a_lo = G.sb("a_lo", [P, KD, S], F32R)
    ident = G.sb("ident", [P, P])
    ident_r = G.sb("ident_r", [P, P], F32R)
    ident_b = G.sb("ident_b", [P, P], BF16)
    pick = G.sb("pick", [4 * ST, ST, P], F32R)
    causal = G.sb("causal", [P, P], BF16)
    blockc = G.sb("blockc", [P, P], BF16)
    low_q = G.sb("low_q", [P, CHUNK], BF16)
    high_q = G.sb("high_q", [P, CHUNK], BF16)
    ind_all = G.sb("ind_all", [P, 2])
    ind_lat = G.sb("ind_lat", [P, 4])
    ind_head = G.sb("ind_head", [P, 2])
    ind_mla = G.sb("ind_mla", [P, 2])
    g_norm = G.sb("g_norm", [P, 2, KD])
    g_gate = G.sb("g_gate", [P, 2, KD])
    g_lat = G.sb("g_lat", [P, 5])
    g_mla = G.sb("g_mla", [P, 2])
    g_chk = G.sb("g_chk", [P, 8])
    g_fox = G.sb("g_fox", [P, 16])
    b_f = G.sb("b_f", [FH, 1])
    x_ss = G.sb("x_ss", [P, ST])

    class Norm:

        def __init__(self, sp, front=None):
            self.front = front
            if front:
                self.ss, self.bc, self.r1, self.r2, self.r3, self.r4, self.flat, self.rows = \
                    front.ss, front.bc, front.r1, front.r2, front.r3, front.r4, front.flat, front.rows
            else:
                self.ss = sp.ps("ss", [P, ST, 2])
                self.bc = sp.ps("bc", [P, S])
                self.r1 = sp.sb("r1", [P, ST, 2])
                self.r2 = sp.sb("r2", [P, ST, 2])
                self.r3 = sp.sb("r3", [P, ST, 2])
                self.r4 = sp.sb("r4", [P, ST, 2, 2], F32R)
                self.flat = sp.ps("flat", [4 * ST, P])
                self.rows = sp.sb("rows", [4 * ST, P], F32R)
            def name(what):
                return what if front else f"f_{what}"

            self.summed = sp.sem(name("summed"))
            self.eps_in = sp.sem(name("eps_in"))
            self.inverted = sp.sem(name("inverted"))
            self.rooted = sp.sem(name("rooted"))
            self.spread_hi = sp.sem(name("spread_hi"))
            self.spread = sp.sem(name("spread"))
            self.flattened = sp.sem(name("flattened"))
            self.flat_out = sp.sem(name("flat_out"))
            self.on_rows = sp.sem(name("on_rows"))
            self.applied = sp.sem(name("applied"))

        def pe_sum(self, pe, n, squares, indicator):
            wait(pe, self.eps_in, n)
            if self.front and isinstance(n, int) and n == 0:
                pe.wait_ge(self.front.eps_in, 1)
            for t in range(ST):
                last = nc.tensor.matmul(self.ss[:, t, :], squares[:, t * P:(t + 1) * P], indicator,
                                        start=True, stop=True)
            last.then_inc(self.summed, 1)

        def dve_invert(self, dve, n):
            wait(dve, self.summed, n + 1)
            nc.vector.tensor_scalar(self.r1[:], self.ss[:], EPS, None, ALU.add).then_inc(self.eps_in, 1)
            wait(dve, self.eps_in, n + 1)
            nc.vector.reciprocal(self.r2[:], self.r1[:]).then_inc(self.inverted, 1)

        def act_root(self, act, n):
            wait(act, self.inverted, n + 1)
            nc.scalar.activation(self.r3[:], self.r2[:], ACT.Sqrt).then_inc(self.rooted, 1)

        def dve_spread(self, dve, n):
            wait(dve, self.rooted, n + 1)
            wait(dve, self.flattened, n)
            if self.front and isinstance(n, int) and n == 0:
                dve.wait_ge(self.front.flattened, 1)
            nc.vector.tensor_copy(self.r4[:, :, :, 0], self.r3[:]).then_inc(self.spread_hi, 1)
            wait(dve, self.spread_hi, n + 1)
            nc.vector.tensor_tensor(self.r4[:, :, :, 1], self.r3[:], self.r4[:, :, :, 0].bitcast(F32), ALU.subtract)\
                .then_inc(self.spread, 1)

        def pe_flatten(self, pe, n):
            wait(pe, self.spread, n + 1)
            wait(pe, self.flat_out, n)
            if self.front and isinstance(n, int) and n == 0:
                pe.wait_ge(self.front.flat_out, 1)
            nc.tensor.matmul(self.flat[:], self.r4[:].rearrange("p t h e -> p (t h e)"), ident_r[:],
                             start=True, stop=True).then_inc(self.flattened, 1)

        def act_rows(self, act, n):
            wait(act, self.flattened, n + 1)
            wait(act, self.on_rows, n)
            if self.front and isinstance(n, int) and n == 0:
                act.wait_ge(self.front.on_rows, 1)
            nc.scalar.activation(self.rows[:], self.flat[:], ACT.Copy).then_inc(self.flat_out, 1)

        def pe_rows(self, pe, n):
            wait(pe, self.flat_out, n + 1)
            wait(pe, self.applied, n)
            if self.front and isinstance(n, int) and n == 0:
                pe.wait_ge(self.front.scaled, KD)
            for t in range(ST):
                last = nc.tensor.matmul(self.bc[:, t * P:(t + 1) * P], pick[:, t, :], self.rows[:],
                                        start=True, stop=True)
            last.then_inc(self.on_rows, 1)

    bias_wrote = G.sem("bias_wrote")

    def stage_entry(rot):
        with ExitStack() as st:
            sp = Space(st, "en")
            xr = sp.sb("xr", [P, ST, D])
            x_sq = sp.sb("x_sq", [P, 2, D])
            xt = sp.ps("xt", [P, 2, KD, P])
            posi = sp.sb("posi", [P, S], I32)
            ang = sp.sb("ang", [P, S])
            turns = sp.sb("turns", [P, S])
            freq = sp.sb("freq", [P, 1])
            two_pi = sp.sb("two_pi", [P, S])
            pick_f = sp.sb("pick_f", [4 * ST, ST, 2, 64])
            rel = sp.sb("rel", [HEADS, 2 * CLIP + 1])
            rel_ext = sp.sb("rel_ext", [HEADS, 768])
            loaded = [sp.sem(f"loaded{t}") for t in range(ST)]
            small = sp.sem("small")
            pos_in = sp.sem("pos_in")
            rel_in = sp.sem("rel_in")
            rel_out = sp.sem("rel_out")
            turned = sp.sem("turned")
            from_act = sp.sem("from_act")
            from_dve = sp.sem("from_dve")
            made = sp.sem("made")
            chain = sp.sem("chain")
            angled = sp.sem("angled")
            widened = sp.sem("widened")
            sined = sp.sem("sined")
            x_squared = sp.sem("x_squared")
            with nc.Block() as block:

                @block.sync
                def _(sync):
                    for t in range(ST):
                        sync.dma_start(xr[:, t, :], x[0, t * P:(t + 1) * P, :]).then_inc(loaded[t], 16)
                    sync.wait_ge(rel_out, 1)
                    sync.dma_start(s_rel, rel_ext[:]).then_inc(bias_wrote, 16)
                    sync.wait_ge(bias_wrote, 16)
                    repeated = bass.AP(tensor=s_rel.tensor, offset=0, ap=[[768, HEADS], [0, P], [1, 768]])
                    sync.dma_start(s_rep, repeated).then_inc(bias_wrote, 16)

                @block.scalar
                def _(act):
                    n = 0
                    act.dma_start(posi[64:128, :], positions[0:1, :].to_broadcast([64, S])).then_inc(pos_in, 16)
                    act.dma_start(freq[64:128, :], rope_freq).then_inc(pos_in, 16)
                    act.dma_start(rel[:], chk_rel_bias[0]).then_inc(rel_in, 16)

                    def col(dst, src):
                        nonlocal n
                        act.dma_start(dst, src).then_inc(small, 16)
                        n += 1

                    for layer in range(2):
                        col(g_norm[:, layer, :], norm_g[layer].rearrange("(k q) -> q k", q=P))
                        col(g_gate[:, layer, :], pe_gate_norm[layer].rearrange("(k q) -> q k", q=P))
                    col(g_lat[:, 0:3], mla_q_norm[0].rearrange("(k q) -> q k", q=P))
                    col(g_lat[:, 3:5], mla_kv_norm[0].rearrange("(k q) -> q k", q=P))
                    half = ROPE // 2
                    for j, g in enumerate((mla_q_gain, mla_k_gain)):
                        g = g[0].rearrange("(f o) -> f o", o=1)
                        col(g_mla[0:QK, j:j + 1], g)
                        col(g_mla[QK:QK + half, j:j + 1], g[NOPE + half:QK])
                        col(g_mla[QK + half:P, j:j + 1], g[NOPE:NOPE + half])
                    for dst, width, gains in ((g_chk, 4, (chk_q_gain, chk_k_gain)),
                                              (g_fox, 8, (fox_q_gain, fox_k_gain))):
                        for j, g in enumerate(gains):
                            for base in (0, 64):
                                col(dst[base:base + 64, j * width:j * width + 1],
                                    g[0].rearrange("(f o) -> f o", o=1))
                    col(b_f[:], fox_b_f[0].rearrange("(f o) -> f o", o=1))
                    for t in range(ST):
                        act.wait_ge(loaded[t], 16)
                        nc.scalar.activation(x_sq[:, t % 2, :], xr[:, t, :], ACT.Square, accum_out=x_ss[:, t:t + 1])\
                            .then_inc(x_squared, 1)
                        act.wait_ge(turned, t + 1)
                        nc.scalar.activation(hT[:, 0:4, t * P:(t + 1) * P], xt[:, t % 2, 0:4, :], ACT.Copy)\
                            .then_inc(from_act, 1)
                        wait(act, x_squared, t)
                    act.wait_ge(angled, 1)
                    nc.scalar.activation(rot[64:128, :], ang[64:128, :], ACT.Sin).then_inc(sined, 1)
                    act.wait_ge(small, 16 * n)
                    nc.scalar.activation(g_mla[:, 0:1], g_mla[:, 0:1], ACT.Copy, scale=float(QK) ** -0.5)
                    for t, width in ((g_chk, 4), (g_fox, 8)):
                        nc.scalar.activation(t[:, 1:width], t[:, 0:1].to_broadcast([P, width - 1]), ACT.Copy,
                                             scale=float(CHK) ** -0.5)
                        nc.scalar.activation(t[:, width + 1:2 * width],
                                             t[:, width:width + 1].to_broadcast([P, width - 1]), ACT.Copy)\
                            .then_inc(widened, 1)
                    act.wait_ge(widened, 2)
                    for k, t in enumerate((g_chk, g_fox)):
                        nc.scalar.activation(t[:, 0:1], t[:, 0:1], ACT.Copy, scale=float(CHK) ** -0.5)

                @block.gpsimd
                def _(pool):
                    pool.memset(ident[:], 0.0).then_inc(made, 1)
                    pool.memset(causal[:], 0.0).then_inc(made, 1)
                    pool.wait_ge(made, 2)
                    pool.affine_select(out=ident[:], in_=ident[:], compare_op=ALU.not_equal, fill=1.0, base=0,
                                       pattern=[[-1, P]], channel_multiplier=1).then_inc(made, 1)
                    pool.affine_select(out=causal[:], in_=causal[:], compare_op=ALU.is_ge, fill=NEG, base=0,
                                       pattern=[[-1, P]], channel_multiplier=1).then_inc(made, 1)
                    pool.memset(pick_f[:], 1.0).then_inc(made, 1)
                    pool.wait_ge(made, 5)
                    pool.affine_select(out=pick_f[:], in_=pick_f[:], compare_op=ALU.is_ge, fill=0.0, base=0,
                                       pattern=[[-4, ST], [-2, 2], [0, 64]], channel_multiplier=1).then_inc(made, 1)
                    pool.wait_ge(made, 6)
                    pool.affine_select(out=pick_f[:], in_=pick_f[:], compare_op=ALU.is_ge, fill=0.0, base=1,
                                       pattern=[[4, ST], [2, 2], [0, 64]], channel_multiplier=-1).then_inc(made, 1)

                @block.tensor
                def _(pe):
                    pe.wait_ge(made, 3)
                    for t in range(ST):
                        pe.wait_ge(loaded[t], 16)
                        wait(pe, from_act, t - 1)
                        wait(pe, from_dve, t - 1)
                        for k in range(KD):
                            last = nc.tensor.transpose(xt[:, t % 2, k, :], xr[:, t, k * P:(k + 1) * P], ident[:])
                        last.then_inc(turned, 1)

                @block.vector
                def _(dve):
                    count = [0]

                    def link(ins):
                        count[0] += 1
                        ins.then_inc(chain, 1)
                        dve.wait_ge(chain, count[0])

                    for m in (blockc, low_q):
                        nc.vector.memset(m[:], 0.0)
                    link(nc.vector.memset(high_q[:], 0.0))
                    nc.vector.memset(blockc[0:CHUNK, CHUNK:P], NEG)
                    nc.vector.memset(low_q[0:CHUNK, :], NEG)
                    nc.vector.memset(high_q[CHUNK:P, :], NEG)
                    nc.vector.memset(ind_all[:], 1.0 / D)
                    nc.vector.memset(ind_lat[:, 0:2], 1.0 / QLORA)
                    nc.vector.memset(ind_lat[:, 2:4], 1.0 / KVLORA)
                    link(nc.vector.memset(ind_head[:], 0.0))
                    nc.vector.memset(ind_head[0:64, 0:1], 1.0 / CHK)
                    nc.vector.memset(ind_head[64:128, 1:2], 1.0 / CHK)
                    link(nc.vector.memset(ind_mla[:], 1.0 / QK))
                    nc.vector.memset(ind_mla[QK:P, :], 0.0)
                    dve.wait_ge(made, 3)
                    nc.vector.tensor_copy(ident_r[:], ident[:])
                    nc.vector.tensor_copy(ident_b[:], ident[:])

                    dve.wait_ge(rel_in, 16)
                    far = 639 - CLIP
                    nc.vector.tensor_copy(rel_ext[:, 0:far], rel[:, 2 * CLIP:2 * CLIP + 1].to_broadcast([HEADS, far]))
                    near = 768 - far
                    nc.vector.tensor_copy(rel_ext[:, far:768], rel[:, 2 * CLIP + 1 - near:2 * CLIP + 1][:, ::-1])\
                        .then_inc(rel_out, 1)

                    r = slice(64, 128)
                    rc = slice(64, 96)
                    dve.wait_ge(pos_in, 32)
                    link(nc.vector.tensor_copy(ang[r, :], posi[r, :]))
                    link(nc.vector.tensor_scalar(ang[r, :], ang[r, :], freq[r, 0:1], None, ALU.mult))
                    magic = 1.5 * 2.0 ** 23
                    link(nc.vector.tensor_scalar(turns[r, :], ang[r, :], 1.0 / (2 * np.pi), magic, ALU.mult, ALU.add))
                    link(nc.vector.tensor_scalar(turns[r, :], turns[r, :], magic, None, ALU.subtract))
                    parts, rest = [], 2 * np.pi
                    for bits in (5, 16):
                        part = float(np.floor(rest * 2.0 ** bits) / 2.0 ** bits)
                        parts.append(part)
                        rest -= part
                    parts.append(float(rest))
                    for part in parts:
                        link(nc.vector.scalar_tensor_tensor(out=ang[r, :], in0=turns[r, :], scalar=-part,
                                                            in1=ang[r, :], op0=ALU.mult, op1=ALU.add))
                    link(nc.vector.tensor_scalar(ang[rc, :], ang[rc, :], float(np.pi / 2), None, ALU.add))
                    link(nc.vector.tensor_scalar(two_pi[rc, :], ang[rc, :], float(np.pi), 2 * float(np.pi),
                                                 ALU.is_gt, ALU.mult))
                    link(nc.vector.tensor_tensor(ang[rc, :], ang[rc, :], two_pi[rc, :], ALU.subtract))
                    nc.vector.tensor_scalar(ang[r, :], ang[r, :], float(np.float32(3.1415925)),
                                            -float(np.float32(3.1415925)), ALU.min, ALU.max).then_inc(angled, 1)
                    dve.wait_ge(made, 7)
                    nc.vector.tensor_copy(pick[:], pick_f[:].rearrange("r t h f -> r t (h f)"))
                    for t in range(ST):
                        dve.wait_ge(turned, t + 1)
                        nc.vector.tensor_copy(hT[:, 4:8, t * P:(t + 1) * P], xt[:, t % 2, 4:8, :]).then_inc(from_dve, 1)

            sp.end()


    h_parked = G.sem("h_parked")
    h_sq = [None]

    class Front(Norm):

        def __init__(self, sp, gain, u, from_x=False):
            super().__init__(sp)
            self.gain, self.u, self.from_x = gain, u, from_x
            self.scaled = sp.sem("f_scaled")
            self.hi_done = sp.sem("f_hi_done")
            self.lo_pool = sp.sem("f_lo_pool")
            self.lo_dve = sp.sem("f_lo_dve")

        def pe_norm(self, pe):
            if not self.from_x:
                self.pe_sum(pe, 0, h_sq[0], ind_all[:])
            self.pe_flatten(pe, 0)
            self.pe_rows(pe, 0)

        def act_split(self, act):
            for k in range(KD):
                act.wait_ge(self.scaled, k + 1)
                nc.scalar.activation(a_hi[:, k, :], self.u[k % 4], ACT.Copy).then_inc(self.hi_done, 1)

        def pool_split(self, pool):
            for k in range(0, KD, 2):
                pool.wait_ge(self.hi_done, k + 1)
                nc.gpsimd.tensor_tensor(a_lo[:, k, :], self.u[k % 4], a_hi[:, k, :].bitcast(F32),
                                        ALU.subtract).then_inc(self.lo_pool, 1)

        def dve_norm(self, dve):
            if self.from_x:
                sums = x_ss[:].unsqueeze(2).to_broadcast([P, ST, 2])
                nc.vector.tensor_scalar(self.r1[:], sums, 1.0 / D, EPS, ALU.mult, ALU.add).then_inc(self.eps_in, 1)
                dve.wait_ge(self.eps_in, 1)
                nc.vector.reciprocal(self.r2[:], self.r1[:]).then_inc(self.inverted, 1)
            else:
                self.dve_invert(dve, 0)
            self.dve_spread(dve, 0)

        def dve_apply(self, dve):
            dve.wait_ge(self.on_rows, 1)
            for k in range(KD):
                if k >= 4:
                    dve.wait_ge(self.lo_dve if k % 2 else self.lo_pool, k // 2 - 1)
                nc.vector.scalar_tensor_tensor(out=self.u[k % 4], in0=self.bc[:], scalar=self.gain[:, k:k + 1],
                                               in1=hT[:, k, :], op0=ALU.mult, op1=ALU.mult)\
                    .then_inc(self.scaled, 1)
                if k % 2:
                    dve.wait_ge(self.hi_done, k + 1)
                    nc.vector.tensor_tensor(a_lo[:, k, :], self.u[k % 4], a_hi[:, k, :].bitcast(F32),
                                            ALU.subtract).then_inc(self.lo_dve, 1)

        def pe_tile(self, pe, k):
            pe.wait_ge(self.lo_dve if k % 2 else self.lo_pool, k // 2 + 1)

        def all_split(self, eng):
            eng.wait_ge(self.lo_pool, KD // 2)
            eng.wait_ge(self.lo_dve, KD // 2)

    class Squares:

        def __init__(self, sp, added):
            self.sq = sp.sb("sq", [P, 2, S])
            self.added = added
            self.squared = sp.sem("squared")
            self.gathered = sp.sem("gathered")

        def act_square(self, act, c, b):
            act.wait_ge(self.added, c + 1)
            first = isinstance(c, int) and c == 0
            wait(act, self.gathered, c - 2)
            nc.scalar.activation(h_sq[0][:] if first else self.sq[:, b, :],
                                 hT[:, bass.ds(c, 1), :].rearrange("q o n -> q (o n)"), ACT.Square)\
                .then_inc(self.squared, 1)

        def dve_gather(self, dve, c, b):
            if isinstance(c, int) and c == 0:
                return
            dve.wait_ge(self.squared, c + 1)
            wait(dve, self.gathered, c - 1)
            nc.vector.tensor_tensor(h_sq[0][:], h_sq[0][:], self.sq[:, b, :], ALU.add).then_inc(self.gathered, 1)

    class Weights:

        def __init__(self, sp, kt):
            self.raw = sp.sb("w_raw", [P, 2, kt, P])
            self.hi = sp.sb("w_hi", [P, 2, kt, P], F32R)
            self.lo = sp.sb("w_lo", [P, 2, kt, P], F32R)
            self.loaded = [sp.sem("w_loaded0"), sp.sem("w_loaded1")]
            self.hi_done = sp.sem("w_hi_done")
            self.lo_done = sp.sem("w_lo_done")
            self.used = sp.sem("w_used")

        def load(self, sync, c, b, pieces):
            wait(sync, self.lo_done, c - 1)
            for at, k0, src in pieces:
                n, kt = src.shape[1], src.shape[0] // P
                sync.dma_start(self.raw[:, b, k0:k0 + kt, at:at + n], src.rearrange("(k q) n -> q k n", q=P))\
                    .then_inc(self.loaded[b], 16)

        def act_hi(self, act, c, b, loaded, kt):
            act.wait_ge(self.loaded[b], loaded)
            wait(act, self.used, c - 1)
            nc.scalar.activation(self.hi[:, b, 0:kt, :], self.raw[:, b, 0:kt, :], ACT.Copy).then_inc(self.hi_done, 1)

        def dve_lo(self, dve, c, b, kt):
            dve.wait_ge(self.hi_done, c + 1)
            nc.vector.tensor_tensor(self.lo[:, b, 0:kt, :], self.raw[:, b, 0:kt, :],
                                    self.hi[:, b, 0:kt, :].bitcast(F32), ALU.subtract).then_inc(self.lo_done, 1)

        def pe_multiply(self, pe, dst, b, kts, first, last, m_hi, m_lo, k0=0, tile=None):
            for k in kts:
                if tile:
                    tile(pe, k)
                for w, m in ((self.hi, m_hi), (self.hi, m_lo), (self.lo, m_hi)):
                    for h in range(NH):
                        ins = nc.tensor.matmul(dst[:, h * HALF:(h + 1) * HALF], w[:, b, k0 + k, :],
                                               m[:, k, h * HALF:(h + 1) * HALF],
                                               start=(k == first and w is self.hi and m is m_hi),
                                               stop=(k == last and w is self.lo))
            return ins

    def stage_project_ab(rot):
        with ExitStack() as st:
            sp = Space(st, "pa")
            wt = Weights(sp, KD)
            y = sp.sb("y", [P, 4, S])
            front = Front(sp, g_norm[:, 0, :], [y[:, n, :] for n in range(4)], from_x=True)
            norm = Norm(sp, front)
            acc = sp.ps("acc", [P, 2, S])
            lat = hT[:, 0:5, :]
            kr = hT[:, 5, :]
            vout = hT[:, 6:8, :]
            l_hi = sp.sb("l_hi", [P, 5, S], F32R)
            l_lo = sp.sb("l_lo", [P, 5, S], F32R)
            sq = sp.sb("sq", [P, 2, S])
            lsq = y[:, 2:4, :]
            rope_t = sp.sb("rope_t", [P, S])
            acc_free = sp.sem("acc_free")
            squares = sp.sem("squares")
            copied = sp.sem("copied")
            lat_sq = sp.sem("lat_sq")
            lat_added = sp.sem("lat_added")
            lat_scaled = sp.sem("lat_scaled")
            lat_hi = sp.sem("lat_hi")
            lat_lo = sp.sem("lat_lo")
            mq_ready = sp.sem("mq_ready")
            mk_ready = sp.sem("mk_ready")
            roped = sp.sem("roped")
            stored = [sp.sem("stored0"), sp.sem("stored1")]
            v_stored = [sp.sem("v_stored0"), sp.sem("v_stored1")]
            m_stored = [sp.sem(f"m_stored{n}") for n in range(4)]
            swapped = sp.sem("swapped")
            w_in, w_uq, w_ukv = ab_w_in[0], mla_w_uq[0], mla_w_ukv[0]
            half = ROPE // 2

            def pieces(c):
                c, seg = c
                if seg == "lat":
                    return [(0, 0, w_in[:, c * P:(c + 1) * P])]
                if seg == "kr":
                    return [(0, 0, w_in[:, C_KR - 64:C_KR + ROPE]), (96, 0, w_in[:, C_KR + half:C_KR + ROPE]),
                            (96 + half, 0, w_in[:, C_KR:C_KR + half])]
                if seg == "b":
                    return [(0, 0, w_in[:, bass.ds((c - QB0) * P + C_QB, P)])]
                if seg == "ga":
                    return [(0, 0, w_in[:, bass.ds((c - GB1) * P + C_GA, P)])]
                if seg == "mq":
                    o = (c - GA1) * QK
                    return [(0, 0, w_uq[:, bass.ds(o, QK)]), (QK, 0, w_uq[:, bass.ds(o + NOPE + half, half)]),
                            (QK + half, 0, w_uq[:, bass.ds(o + NOPE, half)])]
                return [(0, 0, w_ukv[:, bass.ds((c - MQ1) * P, P)])]

            SEGS = [("lat", 0, KR), ("kr", KR, QB0), ("b", QB0, GB1), ("ga", GB1, GA1), ("mq", GA1, MQ1),
                    ("mk", MQ1, MK1)]

            def seg_at(c):
                return next(s for s, a, z in SEGS if a <= c < z)

            def kt_of(seg):
                return {"mq": QLORA // P, "mk": KVLORA // P}.get(seg, KD)

            def loaded(c, b, seg):
                i = (c - b) // 2 if isinstance(c, int) else c[1]
                c = c if isinstance(c, int) else c[0]
                extra = 0
                if seg in ("kr", "b", "ga", "mq", "mk") and b == 1:
                    extra += 32
                if seg == "mq":
                    return 16 + 16 * i + extra + 32 * (i + 1) - 32 * (GA1 // 2)
                if seg == "mk":
                    extra += 32 * (MQ1 - GA1) // 2
                return 16 + 16 * i + extra

            LOOPS = [("qk", QB0 // 2, QB1 // 2), ("v", QB1 // 2, VB1 // 2), ("g", VB1 // 2, GA1 // 2),
                     ("mq", GA1 // 2, MQ1 // 2), ("mk", MQ1 // 2, MK1 // 2)]

            def loop(eng, lo, hi, body, edges):
                i = lo
                while i < hi:
                    if i in edges:
                        body(i)
                        i += 1
                        continue
                    end = i
                    while end < hi and end not in edges:
                        end += 1
                    if end - i == 1:
                        body(i)
                    else:
                        with eng.Fori(i, end) as r:
                            body(r)
                    i = end

            EDGES = {QB0 // 2, QB1 // 2, VB1 // 2, GB1 // 2, GA1 // 2, MQ1 // 2,
                     GB1 // 2 - 1, GA1 // 2 - 1, MQ1 // 2 - 1, MK1 // 2 - 1}
            EDGES |= set(range(GA1 // 2, MK1 // 2))

            def seg_for(kind, i, ahead):
                if isinstance(i, int):
                    c = 2 * (i + ahead)
                    return seg_at(c) if c < MK1 else None
                return {"qk": "b", "v": "b", "g": "ga" if kind == "g" else "b", "mq": "mq", "mk": "mk"}[kind]

            with nc.Block() as block:

                @block.gpsimd
                def _(pool):
                    front.pool_split(pool)
                    for c in range(GA1, MK1):
                        pool.wait_ge(norm.applied, c - 16 + 1)
                        if c > GA1:
                            pool.wait_ge(mq_ready if c <= MQ1 else mk_ready, c - GA1 if c <= MQ1 else c - MQ1)
                        nc.gpsimd.tensor_tensor(rope_t[64:96, :], y[96:128, c % 4, :], rot[96:128, :], ALU.mult)\
                            .then_inc(swapped, 1)

                @block.sync
                def _(sync):
                    def store_m(c):
                        if c < MQ1:
                            sync.wait_ge(mq_ready, c - GA1 + 1)
                            sync.dma_start(s_mq[c - GA1], y[0:QK, c % 4, :]).then_inc(m_stored[c % 4], 16)
                        else:
                            sync.wait_ge(mk_ready, c - MQ1 + 1)
                            sync.dma_start(s_mk[c - MQ1], y[0:QK, c % 4, :]).then_inc(m_stored[c % 4], 16)

                    def load(c, i, b, seg):
                        wt.load(sync, c, b, pieces((c, seg)))

                    def load_ahead(kind, i, b):
                        seg = seg_for(kind, i, 1)
                        if isinstance(i, int) and 2 * i + 2 + b == KR:
                            seg = "kr"
                        if seg:
                            load(2 * i + 2 + b, i, b, seg)

                    load(0, 0, 0, "lat")
                    sync.dma_start(s_h, hT[:]).then_inc(h_parked, 16)
                    load(1, 0, 1, "lat")
                    for i in range(QB0 // 2):
                        for b in range(2):
                            load_ahead("lat", i, b)
                    sync.wait_ge(bias_wrote, 32)
                    for h in range(HEADS):
                        rows = bass.AP(tensor=s_rep.tensor, offset=h * P * 768 + P - 1, ap=[[767, P], [1, BAND]])
                        sync.dma_start(s_bias[h], rows).then_inc(bias_wrote, 16)

                    def segment(kind, lo, hi):
                        def body(i):
                            for b in range(2):
                                c = 2 * i + b
                                load_ahead(kind, i, b)
                                if kind == "qk":
                                    sync.wait_ge(norm.applied, c - 4 + 1)
                                    sync.dma_start(s_ab[bass.ds(c - QB0, 1)].rearrange("o q n -> (o q) n"), y[:, b, :])\
                                        .then_inc(stored[b], 16)
                                elif kind in ("v", "g"):
                                    sync.wait_ge(acc_free, c + 1)
                                    sync.dma_start(s_ab[bass.ds(c - QB0, 1)].rearrange("o q n -> (o q) n"), y[:, b, :])\
                                        .then_inc(stored[b], 16)
                                else:
                                    if kind == "mk":
                                        sync.wait_ge(acc_free, c + 1)
                                        sync.dma_start(s_mv[c - MQ1], vout[64:128, b, :]).then_inc(v_stored[b], 16)
                                    if c - 2 >= GA1:
                                        store_m(c - 2)
                        loop(sync, lo, hi, body, EDGES)

                    for kind, lo, hi in LOOPS:
                        segment(kind, lo, hi)
                    sync.wait_ge(bias_wrote, 16 * (HEADS + 2))
                    store_m(MK1 - 2)
                    store_m(MK1 - 1)
                    for b in range(2):
                        sync.wait_ge(stored[b], 16 * (GA1 - QB0) // 2)
                        sync.wait_ge(v_stored[b], 16 * (MK1 - MQ1) // 2)
                    for n in range(4):
                        sync.wait_ge(m_stored[n], 16 * (MK1 - GA1) // 4)

                @block.scalar
                def _(act):
                    def split(i, b, kind):
                        seg = seg_for(kind, i, 1)
                        if isinstance(i, int) and 2 * i + 2 + b == KR:
                            seg = "kr"
                        if seg:
                            c = 2 * i + 2 + b
                            wt.act_hi(act, c, b, loaded(c, b, seg) if isinstance(i, int)
                                      else loaded((c, i + 1), b, seg), kt_of(seg))

                    def to_y(i, b):
                        wait(act, stored[b], 16 * i - 16 * (QB0 // 2))

                    def to_y_m(c):
                        if c < GA1 + 4:
                            act.wait_ge(stored[c % 2], 16 * (GA1 - QB0) // 2)
                        else:
                            act.wait_ge(m_stored[c % 4], 16 * ((c - GA1) // 4))

                    front.act_root(act, 0)
                    front.act_rows(act, 0)
                    wt.act_hi(act, 0, 0, 16, KD)
                    front.act_split(act)
                    wt.act_hi(act, 1, 1, 16, KD)
                    act.wait_ge(h_parked, 16)
                    for c in range(QB0):
                        act.wait_ge(wt.used, c + 1)
                        if c < KR:
                            j = 0 if c < LAT_KV else 1
                            first = c in (LAT_Q, LAT_KV)
                            if not first:
                                wait(act, lat_added, {1: 0, 2: 1, 4: 2}[c])
                            dst = lsq[:, j, :] if first else sq[:, 0, :]
                            nc.scalar.activation(dst, acc[:, c % 2, :], ACT.Square).then_inc(lat_sq, 1)
                            nc.scalar.activation(lat[:, c, :], acc[:, c % 2, :], ACT.Copy).then_inc(acc_free, 1)
                        else:
                            nc.scalar.activation(kr[64:128, :], acc[64:128, c % 2, :], ACT.Copy).then_inc(acc_free, 1)
                        split(c // 2, c % 2, "lat")
                        if c == LAT_KV:
                            norm.act_root(act, 0)
                            norm.act_rows(act, 0)

                    def lat_split(k):
                        act.wait_ge(lat_scaled, k + 1)
                        nc.scalar.activation(l_hi[:, k, :], lat[:, k, :], ACT.Copy).then_inc(lat_hi, 1)

                    for k in range(LAT_KV):
                        lat_split(k)
                    norm.act_root(act, 1)
                    norm.act_rows(act, 1)

                    def segment(kind, lo, hi):
                        def body(i):
                            for b in range(2):
                                c = 2 * i + b
                                if kind == "qk":
                                    act.wait_ge(wt.used, c + 1)
                                    to_y(i, b)
                                    if isinstance(i, int) and c == QB0:
                                        act.wait_ge(lat_added, 3)
                                        front.all_split(act)
                                    wait(act, norm.summed, c - 4 - 1)
                                    nc.scalar.activation(sq[:, b, :], acc[:, b, :], ACT.Square).then_inc(squares, 1)
                                    nc.scalar.activation(y[:, b, :], acc[:, b, :], ACT.Copy).then_inc(acc_free, 1)
                                    if isinstance(i, int) and c == QB0:
                                        for k in range(LAT_KV, 5):
                                            lat_split(k)
                                    split(i, b, kind)
                                    norm.act_root(act, c - 4)
                                    norm.act_rows(act, c - 4)
                                elif kind in ("v", "g"):
                                    act.wait_ge(wt.used, c + 1)
                                    to_y(i, b)
                                    nc.scalar.activation(y[:, b, :], acc[:, b, :], ACT.Copy if kind == "v" else ACT.Silu)\
                                        .then_inc(acc_free, 1)
                                    split(i, b, kind)
                                elif kind == "mq":
                                    act.wait_ge(wt.used, c + 1)
                                    to_y_m(c)
                                    wait(act, norm.summed, c - 16 - 1)
                                    nc.scalar.activation(sq[:, b, :], acc[:, b, :], ACT.Square).then_inc(squares, 1)
                                    nc.scalar.activation(y[:, c % 4, :], acc[:, b, :], ACT.Copy).then_inc(acc_free, 1)
                                    split(i, b, kind)
                                    if c > GA1:
                                        norm.act_rows(act, c - 16 - 1)
                                    norm.act_root(act, c - 16)
                                else:
                                    to_y_m(c)
                                    nc.scalar.activation(y[64:128, c % 4, :], kr[64:128, :], ACT.Copy).then_inc(copied, 1)
                                    act.wait_ge(wt.used, c + 1)
                                    nc.scalar.activation(y[0:64, c % 4, :], acc[0:64, b, :], ACT.Copy).then_inc(copied, 1)
                                    wait(act, v_stored[b], 16 * i - 16 * (MQ1 // 2))
                                    nc.scalar.activation(vout[64:128, b, :], acc[64:128, b, :], ACT.Copy)\
                                        .then_inc(acc_free, 1)
                                    act.wait_ge(copied, 2 * (c - MQ1) + 2)
                                    wait(act, norm.summed, c - 16 - 1)
                                    nc.scalar.activation(sq[:, b, :], y[:, c % 4, :], ACT.Square).then_inc(squares, 1)
                                    split(i, b, kind)
                                    if c > GA1:
                                        norm.act_rows(act, c - 16 - 1)
                                    norm.act_root(act, c - 16)
                        loop(act, lo, hi, body, EDGES)

                    for kind, lo, hi in LOOPS:
                        segment(kind, lo, hi)
                    norm.act_rows(act, MK1 - 1 - 16)

                @block.tensor
                def _(pe):
                    def main(c, b, seg, hooks={}, end=None):
                        kt = kt_of(seg)
                        m_hi, m_lo = (a_hi, a_lo)
                        if seg == "mq":
                            m_hi, m_lo = l_hi[:, 0:3], l_lo[:, 0:3]
                        if seg == "mk":
                            m_hi, m_lo = l_hi[:, 3:5], l_lo[:, 3:5]
                        pe.wait_ge(wt.lo_done, c + 1)
                        wait(pe, acc_free, c - 1)
                        tile = front.pe_tile if isinstance(c, int) and c == 0 else None
                        for k in range(kt):
                            if k in hooks:
                                hooks[k]()
                            last = wt.pe_multiply(pe, acc[:, b, :], b, [k], 0, kt - 1, m_hi, m_lo, tile=tile)
                        last.then_inc(wt.used, 1)
                        if end:
                            end()

                    def ss_lat(n):
                        pe.wait_ge(lat_added, 2 + n)
                        norm.pe_sum(pe, n, lsq[:, n, :], ind_lat[:, 2 * n:2 * n + 2])

                    front.pe_norm(pe)
                    for c in range(QB0):
                        if c == LAT_KV + 1:
                            main(c, c % 2, seg_at(c), {KD // 2: lambda: ss_lat(0), KD - 1: lambda: norm.pe_flatten(pe, 0)},
                                 lambda: norm.pe_rows(pe, 0))
                        else:
                            main(c, c % 2, seg_at(c))

                    def hooks(kind, c, b):
                        n = c - (4 if kind == "qk" else 16)
                        ind = ind_head if kind == "qk" else ind_mla
                        done = c - (QB0 if kind == "qk" else GA1 - 8) + 1

                        def sums():
                            pe.wait_ge(squares, done)
                            norm.pe_sum(pe, n, sq[:, b, :], ind[:])
                        return {KD // 2: sums, KD - 1: lambda: norm.pe_flatten(pe, n)}, lambda: norm.pe_rows(pe, n)

                    def segment(kind, lo, hi):
                        def body(i):
                            for b in range(2):
                                c = 2 * i + b
                                mid, end = {}, None
                                if isinstance(i, int) and c == QB0:
                                    mid = {KD // 2: lambda: ss_lat(1), KD - 1: lambda: norm.pe_flatten(pe, 1)}
                                    end = lambda: norm.pe_rows(pe, 1)
                                elif isinstance(i, int) and c == QB1:
                                    mid, end = hooks("qk", c - 1, 1 - b)
                                elif isinstance(i, int) and c == GA1:
                                    pe.wait_ge(lat_lo, 5)
                                elif kind == "qk":
                                    mid, end = hooks(kind, c - 1, 1 - b)
                                elif kind in ("mq", "mk"):
                                    mid = late(c)
                                main(c, b, seg_for(kind, i, 0), mid, end)
                        loop(pe, lo, hi, body, EDGES)

                    def late(c):
                        def flatten():
                            if c - 2 >= GA1:
                                norm.pe_flatten(pe, c - 2 - 16)

                        def mid():
                            if c - 2 >= GA1:
                                norm.pe_rows(pe, c - 2 - 16)
                            if c - 1 >= GA1:
                                hooks("mk", c - 1, (c - 1) % 2)[0][KD // 2]()
                        return {1: flatten, 2: mid} if c < MQ1 else {0: flatten, 1: mid}

                    for kind, lo, hi in LOOPS:
                        segment(kind, lo, hi)
                    for step in late(MK1).values():
                        step()
                    norm.pe_flatten(pe, MK1 - 1 - 16)
                    norm.pe_rows(pe, MK1 - 1 - 16)

                @block.vector
                def _(dve):
                    def split(i, b, kind):
                        seg = seg_for(kind, i, 1)
                        if isinstance(i, int) and 2 * i + 2 + b == KR:
                            seg = "kr"
                        if seg:
                            wt.dve_lo(dve, 2 * i + 2 + b, b, kt_of(seg))

                    def lat_norm(n, ks):
                        dve.wait_ge(norm.on_rows, n + 1)
                        for k in ks:
                            nc.vector.scalar_tensor_tensor(out=lat[:, k, :], in0=norm.bc[:], scalar=g_lat[:, k:k + 1],
                                                           in1=lat[:, k, :], op0=ALU.mult, op1=ALU.mult)\
                                .then_inc(lat_scaled, 1)
                        dve.wait_ge(lat_scaled, ks[-1] + 1)
                        dve.sem_inc(norm.applied, 1)
                        for k in ks:
                            dve.wait_ge(lat_hi, k + 1)
                            nc.vector.tensor_tensor(l_lo[:, k, :], lat[:, k, :], l_hi[:, k, :].bitcast(F32),
                                                    ALU.subtract).then_inc(lat_lo, 1)

                    front.dve_norm(dve)
                    wt.dve_lo(dve, 0, 0, KD)
                    front.dve_apply(dve)
                    wt.dve_lo(dve, 1, 1, KD)
                    added = 0
                    for c in range(QB0):
                        if c < KR and c not in (LAT_Q, LAT_KV):
                            j = 0 if c < LAT_KV else 1
                            dve.wait_ge(lat_sq, c + 1)
                            wait(dve, lat_added, added)
                            nc.vector.tensor_tensor(lsq[:, j, :], lsq[:, j, :], sq[:, 0, :], ALU.add)\
                                .then_inc(lat_added, 1)
                            added += 1
                        split(c // 2, c % 2, "lat")
                        if c == LAT_KV:
                            norm.dve_invert(dve, 0)
                            norm.dve_spread(dve, 0)
                    lat_norm(0, [0, 1, 2])

                    def segment(kind, lo, hi):
                        def body(i):
                            for b in range(2):
                                c = 2 * i + b
                                if kind != "qk":
                                    split(i, b, kind)
                                    continue
                                if isinstance(i, int) and c == QB0:
                                    norm.dve_invert(dve, 1)
                                    norm.dve_spread(dve, 1)
                                    lat_norm(1, [3, 4])
                                n = c - 4
                                norm.dve_invert(dve, n)
                                norm.dve_spread(dve, n)
                                split(i, b, kind)
                                dve.wait_ge(norm.on_rows, n + 1)
                                nc.vector.scalar_tensor_tensor(out=y[:, b, :], in0=norm.bc[:],
                                                               scalar=g_chk[:, bass.ds(c - QB0, 1)], in1=y[:, b, :],
                                                               op0=ALU.mult, op1=ALU.mult).then_inc(norm.applied, 1)
                        loop(dve, lo, hi, body, EDGES)

                    for kind, lo, hi in LOOPS[:3]:
                        segment(kind, lo, hi)
                    for c in range(GA1, MK1 + 1):
                        if c < MK1:
                            split(c // 2, c % 2, "mq")
                        if c > GA1:
                            at = y[:, (c - 1) % 4, :]
                            dve.wait_ge(norm.on_rows, c - 16)
                            nc.vector.scalar_tensor_tensor(out=at, in0=norm.bc[:],
                                                           scalar=g_mla[:, 0:1] if c - 1 < MQ1 else g_mla[:, 1:2],
                                                           in1=at, op0=ALU.mult, op1=ALU.mult)\
                                .then_inc(norm.applied, 1)
                        if c < MK1:
                            norm.dve_invert(dve, c - 16)
                        if c > GA1:
                            at = y[64:96, (c - 1) % 4, :]
                            dve.wait_ge(norm.applied, c - 16)
                            nc.vector.tensor_tensor(at, at, rot[64:96, :], ALU.mult).then_inc(roped, 1)
                        if c < MK1:
                            norm.dve_spread(dve, c - 16)
                        if c > GA1:
                            dve.wait_ge(roped, c - GA1)
                            dve.wait_ge(swapped, c - GA1)
                            nc.vector.tensor_tensor(at, at, rope_t[64:96, :], ALU.add)\
                                .then_inc(mq_ready if c - 1 < MQ1 else mk_ready, 1)
            sp.end()

    def stage_project_fox():
        with ExitStack() as st:
            sp = Space(st, "pf")
            NQK, NALL = 2 * FH // 2, 4 * FH // 2
            wt = Weights(sp, KD)
            y = sp.sb("y", [P, 2, S])
            sq = sp.sb("sq", [P, 2, S])
            front = Front(sp, g_norm[:, 1, :], [t[:, n, :] for t in (y, sq) for n in range(2)])
            norm = Norm(sp, front)
            acc = sp.ps("acc", [P, 2, S])
            f_raw = sp.sb("f_raw", [P, KD, FH])
            f_hi = sp.sb("f_hi", [P, KD, FH], F32R)
            f_lo = sp.sb("f_lo", [P, KD, FH], F32R)
            wf_in, wf_hi_done, wf_lo_done = sp.sem("wf_in"), sp.sem("wf_hi_done"), sp.sem("wf_lo_done")
            wf_summed = sp.sem("wf_summed")
            ones_made = sp.sem("ones_made")
            z = sp.sb("z", [FH, S])
            e = sp.sb("e", [FH, S])
            ones = sp.sb("ones", [FH, S])
            neg_cum = sp.sb("neg_cum", [FH, S])
            acc_free = sp.sem("acc_free")
            squares = sp.sem("squares")
            gate_act = sp.sem("gate_act")
            gate_dve = sp.sem("gate_dve")
            stored = [sp.sem("stored0"), sp.sem("stored1")]
            cum_stored = sp.sem("cum_stored")
            w = fox_w_in[0]
            with nc.Block() as block:

                def run(eng, lo, hi, body):
                    body(lo)
                    if hi - lo > 3:
                        with eng.Fori(lo + 1, hi - 1) as i:
                            body(i)
                    else:
                        for i in range(lo + 1, hi - 1):
                            body(i)
                    body(hi - 1)

                @block.gpsimd
                def _(pool):
                    pool.memset(ones[:], 1.0).then_inc(ones_made, 1)
                    front.pool_split(pool)

                @block.sync
                def _(sync):
                    def load(c, b):
                        wt.load(sync, c, b, [(0, 0, w[:, bass.ds(c * P, P)])])

                    load(0, 0)
                    load(1, 1)
                    sync.dma_start(s_h[0:64, 0, :], hT[0:64, 0, :]).then_inc(h_parked, 16)

                    def segment(lo, hi):
                        def body(i):
                            for b in range(2):
                                c = 2 * i + b
                                if not isinstance(i, int) or c + 2 < NALL:
                                    load(c + 2, b)
                                sync.wait_ge(norm.applied if hi <= NQK // 2 else acc_free, c + 1)
                                sync.dma_start(s_fox[bass.ds(c, 1)].rearrange("o q n -> (o q) n"), y[:, b, :])\
                                    .then_inc(stored[b], 16)
                        run(sync, lo, hi, body)
                    sync.dma_start(f_raw[:], w[:, NALL * P:NALL * P + FH].rearrange("(k q) n -> q k n", q=P))\
                        .then_inc(wf_in, 16)
                    segment(0, NQK // 2)
                    segment(NQK // 2, NALL // 2)
                    sync.wait_ge(gate_dve, 3)
                    sync.dma_start(s_cum, neg_cum[:]).then_inc(cum_stored, 16)
                    sync.wait_ge(cum_stored, 16)
                    for b in range(2):
                        sync.wait_ge(stored[b], 16 * NALL // 2)

                @block.scalar
                def _(act):
                    def log_gates():
                        act.wait_ge(wf_summed, 1)
                        nc.scalar.activation(z[:], norm.bc[0:FH, :], ACT.Identity, bias=b_f[:]).then_inc(gate_act, 1)
                        act.wait_ge(gate_act, 1)
                        nc.scalar.activation(e[:], z[:], ACT.Abs).then_inc(gate_act, 1)
                        act.wait_ge(gate_act, 2)
                        nc.scalar.activation(e[:], e[:], ACT.Exp, scale=-1.0).then_inc(gate_act, 1)
                        act.wait_ge(gate_act, 3)
                        nc.scalar.activation(e[:], e[:], ACT.Ln, bias=1.0).then_inc(gate_act, 1)

                    def hi_of(i, b):
                        c = 2 * i + b
                        if not isinstance(i, int) or c < NALL:
                            wt.act_hi(act, c, b, 16 * i + 16, KD)

                    front.act_root(act, 0)
                    front.act_rows(act, 0)
                    hi_of(0, 0)
                    front.act_split(act)
                    hi_of(0, 1)
                    act.wait_ge(wf_in, 16)
                    nc.scalar.activation(f_hi[:], f_raw[:], ACT.Copy).then_inc(wf_hi_done, 1)

                    def segment(kind, lo, hi):
                        def body(i):
                            for b in range(2):
                                c = 2 * i + b
                                act.wait_ge(wt.used, c + 1)
                                if isinstance(i, int) and c == 0:
                                    front.all_split(act)
                                if kind == "qk":
                                    wait(act, norm.summed, c - 1)
                                    nc.scalar.activation(sq[:, b, :], acc[:, b, :], ACT.Square).then_inc(squares, 1)
                                wait(act, stored[b], 16 * i)
                                nc.scalar.activation(y[:, b, :], acc[:, b, :], ACT.Silu if kind == "g" else ACT.Copy)\
                                    .then_inc(acc_free, 1)
                                hi_of(i + 1, b)
                                if kind == "qk":
                                    norm.act_root(act, c)
                                    norm.act_rows(act, c)
                                if isinstance(i, int) and c == NQK + 1:
                                    log_gates()
                        run(act, lo, hi, body)
                    segment("qk", 0, NQK // 2)
                    segment("v", NQK // 2, 3 * NALL // 8)
                    segment("g", 3 * NALL // 8, NALL // 2)

                @block.tensor
                def _(pe):
                    front.pe_norm(pe)

                    def main(c, b, mid, end):
                        pe.wait_ge(wt.lo_done, c + 1)
                        wait(pe, acc_free, c - 1)
                        tile = front.pe_tile if isinstance(c, int) and c == 0 else None
                        for k in range(KD):
                            if k in mid:
                                mid[k]()
                            last = wt.pe_multiply(pe, acc[:, b, :], b, [k], 0, KD - 1, a_hi, a_lo, tile=tile)
                        last.then_inc(wt.used, 1)
                        if end:
                            end()

                    def gates():
                        pe.wait_ge(wf_lo_done, 1)
                        pe.wait_ge(norm.applied, NQK)
                        for k in range(KD):
                            for w, m in ((f_hi, a_hi), (f_hi, a_lo), (f_lo, a_hi)):
                                for h in range(NH):
                                    ins = nc.tensor.matmul(norm.bc[0:FH, h * HALF:(h + 1) * HALF], w[:, k, :],
                                                           m[:, k, h * HALF:(h + 1) * HALF],
                                                           start=(k == 0 and w is f_hi and m is a_hi),
                                                           stop=(k == KD - 1 and w is f_lo))
                        ins.then_inc(wf_summed, 1)

                    def segment(kind, lo, hi):
                        def body(i):
                            for b in range(2):
                                c = 2 * i + b
                                mid, end = {}, None
                                first = isinstance(i, int) and i == lo and b == 0
                                if (kind == "qk") != first:

                                    def sums():
                                        pe.wait_ge(squares, c)
                                        norm.pe_sum(pe, c - 1, sq[:, 1 - b, :], ind_head[:])
                                    mid = {KD // 2: sums, KD - 1: lambda: norm.pe_flatten(pe, c - 1)}

                                    def end():
                                        norm.pe_rows(pe, c - 1)
                                main(c, b, mid, end)
                                if isinstance(i, int) and c == NQK + 1:
                                    gates()
                        run(pe, lo, hi, body)
                    segment("qk", 0, NQK // 2)
                    segment("vg", NQK // 2, NALL // 2)

                @block.vector
                def _(dve):
                    def sum_gates():
                        dve.wait_ge(gate_act, 4)
                        nc.vector.tensor_scalar(z[:], z[:], 0.0, None, ALU.min).then_inc(gate_dve, 1)
                        dve.wait_ge(gate_dve, 1)
                        nc.vector.tensor_tensor(e[:], e[:], z[:], ALU.subtract).then_inc(gate_dve, 1)
                        dve.wait_ge(gate_dve, 2)
                        dve.wait_ge(ones_made, 1)
                        nc.vector.tensor_tensor_scan(neg_cum[:], ones[:], e[:], 0.0, ALU.mult, ALU.add)\
                            .then_inc(gate_dve, 1)

                    def lo_of(i, b):
                        c = 2 * i + b
                        if not isinstance(i, int) or c < NALL:
                            wt.dve_lo(dve, c, b, KD)

                    front.dve_norm(dve)
                    lo_of(0, 0)
                    front.dve_apply(dve)
                    lo_of(0, 1)
                    dve.wait_ge(wf_hi_done, 1)
                    nc.vector.tensor_tensor(f_lo[:], f_raw[:], f_hi[:].bitcast(F32), ALU.subtract).then_inc(wf_lo_done, 1)

                    def segment(kind, lo, hi):
                        def body(i):
                            for b in range(2):
                                c = 2 * i + b
                                if kind == "qk":
                                    norm.dve_invert(dve, c)
                                    norm.dve_spread(dve, c)
                                lo_of(i + 1, b)
                                if kind == "qk":
                                    dve.wait_ge(norm.on_rows, c + 1)
                                    nc.vector.scalar_tensor_tensor(out=y[:, b, :], in0=norm.bc[:],
                                                                   scalar=g_fox[:, bass.ds(c, 1)], in1=y[:, b, :],
                                                                   op0=ALU.mult, op1=ALU.mult)\
                                        .then_inc(norm.applied, 1)
                                if isinstance(i, int) and c == NALL - 2:
                                    sum_gates()
                        run(dve, lo, hi, body)
                    segment("qk", 0, NQK // 2)
                    segment("vg", NQK // 2, NALL // 2)
            sp.end()

    def stage_attention(kind, heads, first_pair, q_of, k_of, v_of, g_of, extra_of):
        mla, chk, fox = (kind == k for k in ("mla", "chk", "fox"))
        NT = ST
        NP2 = heads // 2

        def lowest(t):
            return max(0, t - BAND // P + 1) if chk else 0

        def turned(t):
            js = list(range(lowest(t), t + 1))
            cut = (len(js) + 1) // 2 if len(js) > 4 else 4
            return [js[n:n + cut] for n in range(0, len(js), cut)]

        PIECES = [len(turned(t)) for t in range(NT)]
        BEFORE = [sum(PIECES[:t]) for t in range(NT + 1)]
        NPC = BEFORE[NT]
        assert NPC % 2 == 0

        with ExitStack() as st:
            sp = Space(st, kind)
            raw = sp.sb("raw", [P, 2, S])
            q_hi = sp.sb("q_hi", [P, 2, S], F32R)
            k_hi = sp.sb("k_hi", [P, 2, S], F32R)
            k_lo = sp.sb("k_lo", [P, 2, S], F32R)
            q_lo = sp.sb("q_lo", [P, 2, S], F32R) if mla else None
            extra = None if mla else sp.sb("extra", [P, 2, BAND if chk else S])
            v_raw = hT[0:64, 0, :]
            v = sp.sb("v", [P, 2, ST, P], F32R)
            gate = sp.sb("gate", [P, S])
            o = sp.sb("o", [P, S])
            WIDE = BAND if chk else S
            prob = sp.sb("prob", [P, 4, WIDE])
            pt_hi = sp.sb("pt_hi", [P, 2, WIDE // P + chk, 2 * P], F32R)
            pt_lo = sp.sb("pt_lo", [P, 2, WIDE // P + chk, 2 * P], F32R)
            neg_max = sp.sb("neg_max", [P, 4])
            total = sp.sb("total", [P, 4])
            inverse = sp.sb("inverse", [P, 4])
            spare = sp.sb("spare", [P, 2])
            scores = sp.ps("scores", [P, 2, S])
            turn = sp.ps("turn", [P, 2, 4, P])
            pv = sp.ps("pv", [64, 2 * P])
            vt = sp.ps("vt", [P, ST, 64])

            in_q, in_k, in_v = sp.sem("in_q"), sp.sem("in_k"), sp.sem("in_v")
            in_g = [sp.sem("in_g0"), sp.sem("in_g1")]
            in_x = [sp.sem("in_x0"), sp.sem("in_x1")]
            q_hi_done, q_lo_done = sp.sem("q_hi_done"), sp.sem("q_lo_done")
            k_hi_done, k_lo_done = sp.sem("k_hi_done"), sp.sem("k_lo_done")
            v_turned, v_hi_done, v_lo_done = sp.sem("v_turned"), sp.sem("v_hi_done"), sp.sem("v_lo_done")
            scored = sp.sem("scored")
            maxed = sp.sem("maxed")
            exped = sp.sem("exped")
            inverted = sp.sem("inverted")
            normed = sp.sem("normed")
            pieces_turned = sp.sem("pieces_turned")
            pt_hi_done, pt_lo_done = sp.sem("pt_hi_done"), sp.sem("pt_lo_done")
            pv_done = sp.sem("pv_done")
            o_done = sp.sem("o_done")
            gated, out_hi, out_lo = sp.sem("gated"), sp.sem("out_hi"), sp.sem("out_lo")
            NDMA = 1 if mla else 2
            KROWS = QK if mla else P

            def over_heads(eng, head, tail=None):
                def body(i, final=False):
                    for b in range(2):
                        head(i, b, 2 * i + b, final and b == 1)
                body(0)
                if NP2 > 3:
                    with eng.Fori(1, NP2 - 1) as i:
                        body(i)
                else:
                    for i in range(1, NP2 - 1):
                        body(i)
                body(NP2 - 1, True)

            with nc.Block() as block:

                @block.sync
                def _(sync):
                    def load(hd, b, m):
                        for dst, src, sem, done in ((0, q_of(hd), in_q, q_lo_done), (1, k_of(hd), in_k, k_lo_done)):
                            wait(sync, done, hd)
                            rows = src.shape[0]
                            for n in range(NDMA):
                                sync.dma_start(raw[n * rows:(n + 1) * rows, dst, :], src).then_inc(sem, 16)
                        wait(sync, v_turned, hd)
                        sync.dma_start(v_raw, v_of(hd)).then_inc(in_v, 16)
                        if extra is not None:
                            wait(sync, maxed, NT * (hd - 1))
                            sync.dma_start(extra[:, b, :], extra_of(hd)).then_inc(in_x[b], 16)
                        wait(sync, gated, hd - 1)
                        sync.dma_start(gate[64 * b:64 * b + 64, :], g_of(hd)).then_inc(in_g[b], 16)

                    sync.wait_ge(h_parked, 32 if fox else 16)
                    load(0, 0, 0)

                    def head(i, b, hd, last):
                        if not last:
                            load(hd + 1, 1 - b, i + b)
                    over_heads(sync, head)

                def lo_slices():
                    return (q_lo, slice(0, QK)) if mla else (q_hi, slice(64, P))

                @block.scalar
                def _(act):
                    def split_q(hd, b):
                        act.wait_ge(in_q, 16 * NDMA * (hd + 1))
                        wait(act, scored, NT * (hd - 1))
                        nc.scalar.activation(q_hi[0:KROWS, b, :], raw[0:KROWS, 0, :], ACT.Copy).then_inc(q_hi_done, 1)

                    def split_k(hd, b):
                        act.wait_ge(in_k, 16 * NDMA * (hd + 1))
                        nc.scalar.activation(k_hi[0:KROWS, b, :], raw[0:KROWS, 1, :], ACT.Copy).then_inc(k_hi_done, 1)

                    def split_v(hd, b):
                        act.wait_ge(v_turned, hd + 1)
                        wait(act, pv_done, NT // 2 * (hd - 1))
                        nc.scalar.activation(v[:, b, :, 0:64], vt[:], ACT.Copy).then_inc(v_hi_done, 1)

                    def evacuate(hd, t):
                        for n, js in enumerate(turned(t)):
                            g = BEFORE[t] + n
                            u = t // 2
                            act.wait_ge(pieces_turned, NPC * hd + g + 1)
                            wait(act, pv_done, NT // 2 * hd + u - 1)
                            at = js[0] - lowest(2 * u)
                            nc.scalar.activation(pt_hi[:, u % 2, at:at + len(js), (t % 2) * P:(t % 2 + 1) * P],
                                                 turn[:, g % 2, 0:len(js), :], ACT.Copy).then_inc(pt_hi_done, 1)

                    def take_o(hd, b, u):
                        act.wait_ge(pv_done, NT // 2 * hd + u + 1)
                        if u == 0:
                            wait(act, out_lo, hd - 1)
                        nc.scalar.activation(o[64 * b:64 * b + 64, 2 * u * P:2 * (u + 1) * P], pv[:], ACT.Copy)\
                            .then_inc(o_done, 1)

                    def give(m, b, hd):
                        act.wait_ge(gated, hd + 1)
                        r = slice(64 * b, 64 * b + 64)
                        nc.scalar.activation(a_hi[r, bass.ds(m + first_pair, 1), :].rearrange("q o n -> q (o n)"), o[r, :],
                                             ACT.Copy).then_inc(out_hi, 1)

                    split_q(0, 0)
                    split_k(0, 0)
                    split_v(0, 0)

                    def head(i, b, hd, last):
                        for t in range(NT):
                            before = hd if t >= 3 else hd - 1
                            if not (isinstance(hd, int) and before < 0):
                                evacuate(before, (t - 3) % NT)
                            if t % 2 == 0:
                                if t >= 6:
                                    take_o(hd, b, (t - 6) // 2)
                                elif not (isinstance(hd, int) and hd == 0):
                                    take_o(hd - 1, 1 - b, (t + NT - 6) // 2)
                            if t == 7 and not (isinstance(hd, int) and hd == 0):
                                give(i - 1 + b, 1 - b, hd - 1)
                            if not last:
                                if t == 1:
                                    split_q(hd + 1, 1 - b)
                                if t == 2:
                                    split_k(hd + 1, 1 - b)
                                if t == 5:
                                    split_v(hd + 1, 1 - b)
                            s = NT * hd + t
                            act.wait_ge(maxed, s + 1)
                            n = (t + 1 - lowest(t)) * P
                            src = scores[:, t % 2, 0:n] if mla else prob[:, t % 4, 0:n]
                            if mla:
                                wait(act, pieces_turned, NPC * hd + BEFORE[t - 4] + PIECES[t - 4] if t >= 4 else
                                     NPC * (hd - 1) + BEFORE[t + NT - 4] + PIECES[t + NT - 4])
                            nc.scalar.activation(prob[:, t % 4, 0:n], src, ACT.Exp, bias=neg_max[:, t % 4:t % 4 + 1],
                                                 scale=1.0 if mla else -1.0,
                                                 accum_out=total[:, t % 4:t % 4 + 1]).then_inc(exped, 1)
                    over_heads(act, head)
                    hd = heads - 1
                    evacuate(hd, NT - 3)
                    take_o(hd, 1, NT // 2 - 3)
                    evacuate(hd, NT - 2)
                    evacuate(hd, NT - 1)
                    take_o(hd, 1, NT // 2 - 2)
                    take_o(hd, 1, NT // 2 - 1)
                    give(NP2 - 1, 1, hd)

                @block.gpsimd
                def _(pool):
                    def split(hd, b, first=False):
                        dst, r = lo_slices()
                        wait(pool, out_lo, hd - 2)
                        wait(pool, k_lo_done, hd)
                        if not first:
                            pool.wait_ge(q_hi_done, hd + 1)
                            nc.gpsimd.tensor_tensor(dst[r, b, :], raw[r, 0, :], q_hi[r, b, :].bitcast(F32),
                                                    ALU.subtract).then_inc(q_lo_done, 1)
                            pool.wait_ge(q_lo_done, hd + 1)
                        pool.wait_ge(k_hi_done, hd + 1)
                        nc.gpsimd.tensor_tensor(k_lo[0:KROWS, b, :], raw[0:KROWS, 1, :],
                                                k_hi[0:KROWS, b, :].bitcast(F32), ALU.subtract).then_inc(k_lo_done, 1)

                    def give(m, b, hd, final):
                        r = slice(64 * b, 64 * b + 64)
                        pool.wait_ge(k_lo_done, heads if final else hd + 3)
                        wait(pool, out_lo, hd)
                        pool.wait_ge(o_done, NT // 2 * (hd + 1))
                        pool.wait_ge(in_g[b], 16 * (m + 1))
                        nc.gpsimd.tensor_tensor(o[r, :], o[r, :], gate[r, :], ALU.mult).then_inc(gated, 1)
                        pool.wait_ge(gated, hd + 1)
                        pool.wait_ge(out_hi, hd + 1)
                        at = bass.ds(m + first_pair, 1)
                        nc.gpsimd.tensor_tensor(a_lo[r, at, :].rearrange("q o n -> q (o n)"), o[r, :],
                                                a_hi[r, at, :].rearrange("q o n -> q (o n)").bitcast(F32),
                                                ALU.subtract).then_inc(out_lo, 1)

                    split(0, 0, True)

                    def head(i, b, hd, last):
                        if not last:
                            split(hd + 1, 1 - b)
                        if not (isinstance(hd, int) and hd == 0):
                            give(i - 1 + b, 1 - b, hd - 1, last)
                    over_heads(pool, head)

                @block.tensor
                def _(pe):
                    def before_turn_v(hd):
                        pe.wait_ge(in_v, 16 * (hd + 1))
                        wait(pe, v_lo_done, hd)

                    def turn_v(hd):
                        for j in range(ST):
                            last = nc.tensor.transpose(vt[:, j, :], v_raw[:, j * P:(j + 1) * P], ident[0:64, 0:64])
                        last.then_inc(v_turned, 1)

                    def score(hd, b, t):
                        s = NT * hd + t
                        if t == 0:
                            pe.wait_ge(q_lo_done, hd + 1)
                            pe.wait_ge(k_lo_done, hd + 1)
                        wait(pe, exped if mla else maxed, s - 1)
                        lo = lowest(t)
                        n = (t + 1 - lo) * P
                        q = slice(t * P, (t + 1) * P)
                        for c in range(0, n, HALF):
                            w = min(HALF, n - c)
                            dst = scores[:, t % 2, c:c + w]
                            keys = slice(lo * P + c, lo * P + c + w)
                            R = slice(0, KROWS)
                            terms = [(q_hi, k_hi), (q_lo, k_hi), (q_hi, k_lo)] if mla else [(q_hi, k_hi), (q_hi, k_lo)]
                            masks = []
                            if c + w == n:
                                if chk:
                                    masks.append((slice(w - CHUNK, w), low_q))
                                else:
                                    masks.append((slice(w - P, w), causal if fox else blockc))
                            if chk and c == 0 and t >= BAND // P - 1:
                                masks.append((slice(0, CHUNK), high_q))
                            for m, (a, k) in enumerate(terms):
                                ins = nc.tensor.matmul(dst, a[R, b, q], k[R, b, keys], start=(m == 0),
                                                       stop=(m == len(terms) - 1))
                                if m == 0:
                                    for cols, mask in masks:
                                        nc.tensor.matmul(dst[:, cols], ident_b[:], mask[:], start=False, stop=False)
                        ins.then_inc(scored, 1)

                    def turn_p(hd, t):
                        pe.wait_ge(normed, NT * hd + t + 1)
                        lo = lowest(t)
                        for n, js in enumerate(turned(t)):
                            g = BEFORE[t] + n
                            wait(pe, pt_lo_done, NPC * hd + g - 1)
                            for m, j in enumerate(js):
                                last = nc.tensor.transpose(turn[:, g % 2, m, :], prob[:, t % 4, (j - lo) * P:(j - lo + 1) * P],
                                                           ident[:])
                            last.then_inc(pieces_turned, 1)

                    def times_v(hd, b, u):
                        pe.wait_ge(pt_lo_done, NPC * hd + BEFORE[2 * u + 2])
                        wait(pe, o_done, NT // 2 * hd + u)
                        if u == 0:
                            pe.wait_ge(v_lo_done, hd + 1)
                        lo0, lo1 = lowest(2 * u), lowest(2 * u + 1)
                        js = [j for j in range(lo1, 2 * u + 1)] + [2 * u + 1] + list(range(lo0, lo1))
                        HI, LO = slice(0, 64), slice(64, 128)
                        terms = [(j, half, part) for j in js for half, part in ((HI, pt_hi), (HI, pt_lo), (LO, pt_hi))]
                        for m, (j, half, part) in enumerate(terms):
                            cols = slice(P, 2 * P) if j == 2 * u + 1 else slice(0, P) if j < lo1 else slice(0, 2 * P)
                            ins = nc.tensor.matmul(pv[:, cols], v[:, b, j, half], part[:, u % 2, j - lo0, cols],
                                                   start=(m == 0), stop=(m == len(terms) - 1))
                        ins.then_inc(pv_done, 1)

                    before_turn_v(0)
                    turn_v(0)

                    def head(i, b, hd, last):
                        first = isinstance(hd, int) and hd == 0
                        for t in range(NT):
                            score(hd, b, t)
                            if t == 6:
                                times_v(hd, b, 0)
                            if t in (0, 2, 4) and not first:
                                times_v(hd - 1, 1 - b, (t + NT) // 2 - 3)
                            if t == 4 and not last:
                                before_turn_v(hd + 1)
                            if t >= 3:
                                turn_p(hd, t - 3)
                            elif not first:
                                turn_p(hd - 1, t - 3 + NT)
                            if t == 4 and not last:
                                turn_v(hd + 1)
                    over_heads(pe, head)
                    hd = heads - 1
                    times_v(hd, 1, NT // 2 - 3)
                    turn_p(hd, NT - 3)
                    turn_p(hd, NT - 2)
                    times_v(hd, 1, NT // 2 - 2)
                    turn_p(hd, NT - 1)
                    times_v(hd, 1, NT // 2 - 1)

                @block.vector
                def _(dve):
                    def split_v(hd, b):
                        dve.wait_ge(v_hi_done, hd + 1)
                        nc.vector.tensor_tensor(v[:, b, :, 64:128], vt[:], v[:, b, :, 0:64].bitcast(F32), ALU.subtract)\
                            .then_inc(v_lo_done, 1)

                    def invert(hd, t):
                        r = slice(t % 4, t % 4 + 1)
                        dve.wait_ge(exped, NT * hd + t + 1)
                        nc.vector.reciprocal(inverse[:, r], total[:, r]).then_inc(inverted, 1)

                    def normalise(hd, t):
                        s = NT * hd + t
                        lo = lowest(t)
                        n = (t + 1 - lo) * P
                        r = slice(t % 4, t % 4 + 1)
                        dve.wait_ge(inverted, s + 1)
                        nc.vector.tensor_scalar(prob[:, t % 4, 0:n], prob[:, t % 4, 0:n], inverse[:, r], None, ALU.mult)\
                            .then_inc(normed, 1)

                    def row_max(hd, b, t):
                        s = NT * hd + t
                        lo = lowest(t)
                        n = (t + 1 - lo) * P
                        r = slice(t % 4, t % 4 + 1)
                        if mla:
                            dve.wait_ge(scored, s + 1)
                            nc.vector.tensor_reduce(neg_max[:, r], scores[:, t % 2, 0:n], AX_X, ALU.max, negate=True)\
                                .then_inc(maxed, 1)
                            return
                        x = extra[:, b, BAND - n:BAND] if chk else extra[:, b, 0:n]
                        nc.vector.tensor_tensor_reduce(out=prob[:, t % 4, 0:n], in0=scores[:, t % 2, 0:n], in1=x,
                                                       scale=-1.0, scalar=BIG, op0=ALU.add, op1=ALU.min,
                                                       accum_out=neg_max[:, r]).then_inc(maxed, 1)

                    def before_max(i, hd, b, t):
                        s = NT * hd + t
                        if mla:
                            return
                        dve.wait_ge(scored, s + 1)
                        wait(dve, pieces_turned, NPC * hd + BEFORE[t - 4] + PIECES[t - 4] if t >= 4 else
                             NPC * (hd - 1) + BEFORE[t + NT - 4] + PIECES[t + NT - 4])
                        if t == 0:
                            dve.wait_ge(in_x[b], 16 * i + 16)

                    def evacuate(hd, t):
                        for n, js in enumerate(turned(t)):
                            g = BEFORE[t] + n
                            u = t // 2
                            dve.wait_ge(pt_hi_done, NPC * hd + g + 1)
                            at = js[0] - lowest(2 * u)
                            where = (slice(None), u % 2, slice(at, at + len(js)), slice((t % 2) * P, (t % 2 + 1) * P))
                            nc.vector.tensor_tensor(pt_lo[where], turn[:, g % 2, 0:len(js), :], pt_hi[where].bitcast(F32),
                                                    ALU.subtract).then_inc(pt_lo_done, 1)

                    dst, r = lo_slices()
                    dve.wait_ge(q_hi_done, 1)
                    nc.vector.tensor_tensor(dst[r, 0, :], raw[r, 0, :], q_hi[r, 0, :].bitcast(F32), ALU.subtract)\
                        .then_inc(q_lo_done, 1)
                    split_v(0, 0)

                    def head(i, b, hd, last):
                        first = isinstance(hd, int) and hd == 0
                        for t in range(NT):
                            before_max(i, hd, b, t)
                            if t >= 2:
                                normalise(hd, t - 2)
                            elif not first:
                                normalise(hd - 1, NT - 2 + t)
                            elif not mla:
                                nc.vector.memset(spare[:, t:t + 1], 0.0)
                            row_max(hd, b, t)
                            if t >= 1:
                                invert(hd, t - 1)
                            elif not first:
                                invert(hd - 1, NT - 1)
                            if t >= 3:
                                evacuate(hd, t - 3)
                            elif not first:
                                evacuate(hd - 1, t - 3 + NT)
                            if t == 5 and not last:
                                split_v(hd + 1, 1 - b)
                    over_heads(dve, head)
                    hd = heads - 1
                    invert(hd, NT - 1)
                    normalise(hd, NT - 2)
                    evacuate(hd, NT - 3)
                    normalise(hd, NT - 1)
                    evacuate(hd, NT - 2)
                    evacuate(hd, NT - 1)
                    r = slice(64, P)
                    dve.wait_ge(out_lo, heads - 1)
                    dve.wait_ge(o_done, NT // 2 * heads)
                    dve.wait_ge(in_g[1], 16 * NP2)
                    nc.vector.tensor_tensor(o[r, :], o[r, :], gate[r, :], ALU.mult).then_inc(gated, 1)
                    dve.wait_ge(out_hi, heads)
                    at = first_pair + NP2 - 1
                    nc.vector.tensor_tensor(a_lo[r, at, :], o[r, :], a_hi[r, at, :].bitcast(F32), ALU.subtract)
            sp.end()

    def stage_output(tag, weights, parked):
        with ExitStack() as st:
            sp = Space(st, tag)
            wt = Weights(sp, KD)
            acc = sp.ps("acc", [P, 2, S])
            added = sp.sem("added")
            h_back = sp.sem("h_back")
            squares = Squares(sp, added)
            with nc.Block() as block:

                @block.sync
                def _(sync):
                    def body(i):
                        for b in range(2):
                            c = 2 * i + b
                            wt.load(sync, c, b, [(0, 0, weights[:, bass.ds(c * P, P)])])
                            if isinstance(i, int) and c == 1:
                                sync.dma_start(hT[parked], s_h[parked]).then_inc(h_back, 16)
                    pairs(sync, 0, KD // 2, body)

                @block.scalar
                def _(act):
                    def body(i):
                        for b in range(2):
                            wt.act_hi(act, 2 * i + b, b, 16 * i + 16, KD)
                            if not (isinstance(i, int) and i == 0 and b == 0):
                                squares.act_square(act, 2 * i + b - 1, 1 - b)
                    pairs(act, 0, KD // 2, body)
                    squares.act_square(act, KD - 1, 1)

                @block.tensor
                def _(pe):
                    def body(i):
                        for b in range(2):
                            c = 2 * i + b
                            pe.wait_ge(wt.lo_done, c + 1)
                            wait(pe, added, c - 1)
                            wt.pe_multiply(pe, acc[:, b, :], b, range(KD), 0, KD - 1, a_hi, a_lo).then_inc(wt.used, 1)
                    pairs(pe, 0, KD // 2, body)

                @block.vector
                def _(dve):
                    def add(c, b):
                        dve.wait_ge(wt.used, c + 1)
                        at = bass.ds(c, 1)
                        rows = hT[:, at, :].rearrange("q o n -> q (o n)")
                        nc.vector.tensor_tensor(rows, acc[:, b, :], rows, ALU.add).then_inc(added, 1)

                    def body(i):
                        for b in range(2):
                            c = 2 * i + b
                            wt.dve_lo(dve, c, b, KD)
                            if isinstance(i, int) and c == 1:
                                dve.wait_ge(h_back, 16)
                            if not (isinstance(i, int) and c == 0):
                                add(c - 1, 1 - b)
                            if not (isinstance(i, int) and c < 2):
                                squares.dve_gather(dve, c - 2, b)
                    pairs(dve, 0, KD // 2, body)
                    squares.dve_gather(dve, KD - 2, 0)
                    add(KD - 1, 1)
                    squares.dve_gather(dve, KD - 1, 1)
            sp.end()

    def stage_ple(tag, layer):
        with ExitStack() as st:
            sp = Space(st, tag)
            KP = PLE // P
            wt = Weights(sp, KD + KP)
            acc = sp.ps("acc", [P, 2, S])
            pt = acc[:].rearrange("q k (t n) -> q k t n", t=ST)
            pr = sp.sb("pr", [P, ST, PLE])
            p_hi = sp.sb("p_hi", [P, KP, S], F32R)
            p_lo = sp.sb("p_lo", [P, KP, S], F32R)
            gate = sp.sb("gate", [P, 2, S])
            p_in = sp.sem("p_in")
            p_turned = sp.sem("p_turned")
            p_hi_done, p_lo_done = sp.sem("p_hi_done"), sp.sem("p_lo_done")
            gates_summed = sp.sem("gates_summed")
            gate_done = sp.sem("gate_done")
            gated = sp.sem("gated")
            added = sp.sem("added")
            spare = sp.sb("spare", [P, 2, S])
            front = Front(sp, g_gate[:, layer, :], [t[:, n, :] for t in (gate, spare) for n in range(2)])
            squares = None if layer == 1 else Squares(sp, added)
            with nc.Block() as block:

                @block.gpsimd
                def _(pool):
                    front.pool_split(pool)

                @block.sync
                def _(sync):
                    sync.dma_start(pr[:], p[layer, 0].rearrange("(t q) n -> q t n", q=P)).then_inc(p_in, 16)

                    def body(i):
                        for b in range(2):
                            c = 2 * i + b
                            cols = bass.ds(c * P, P)
                            wt.load(sync, c, b, [(0, 0, pe_gate_w[layer][:, cols]), (0, KD, pe_w[layer][:, cols])])
                    pairs(sync, 0, KD // 2, body)

                @block.scalar
                def _(act):
                    front.act_root(act, 0)
                    front.act_rows(act, 0)
                    act.wait_ge(p_turned, 1)
                    for k in range(KP):
                        nc.scalar.activation(p_hi[:, k, :].rearrange("q (t n) -> q t n", t=ST), pt[:, k, :, :], ACT.Copy)\
                            .then_inc(p_hi_done, 1)

                    def gates(c, b):
                        act.wait_ge(gates_summed, c + 1)
                        wait(act, gated, c - 1)
                        nc.scalar.activation(gate[:, b, :], acc[:, 0, :], ACT.Sigmoid).then_inc(gate_done, 1)

                    def body(i):
                        for b in range(2):
                            c = 2 * i + b
                            wt.act_hi(act, c, b, 32 * i + 32, KD + KP)
                            if squares and not (isinstance(i, int) and c < 2):
                                squares.act_square(act, c - 2, b)
                            if isinstance(i, int) and c == 0:
                                front.act_split(act)
                                front.all_split(act)
                            else:
                                gates(c - 1, 1 - b)
                    pairs(act, 0, KD // 2, body)
                    if squares:
                        squares.act_square(act, KD - 2, 0)
                    gates(KD - 1, 1)
                    if squares:
                        squares.act_square(act, KD - 1, 1)

                @block.tensor
                def _(pe):
                    front.pe_sum(pe, 0, h_sq[0], ind_all[:])
                    pe.wait_ge(p_in, 16)
                    for t in range(ST):
                        for k in range(KP):
                            last = nc.tensor.transpose(pt[:, k, t, :], pr[:, t, k * P:(k + 1) * P], ident[:])
                    last.then_inc(p_turned, 1)
                    front.pe_flatten(pe, 0)
                    front.pe_rows(pe, 0)

                    def body(i):
                        for b in range(2):
                            c = 2 * i + b
                            pe.wait_ge(wt.lo_done, c + 1)
                            wait(pe, gate_done, c)
                            if isinstance(i, int) and c == 0:
                                pe.wait_ge(p_lo_done, KP)
                            wt.pe_multiply(pe, acc[:, 0, :], b, range(KD), 0, KD - 1, a_hi, a_lo,
                                           tile=front.pe_tile if isinstance(i, int) and c == 0 else None)\
                                .then_inc(gates_summed, 1)
                            wait(pe, gated, c)
                            wt.pe_multiply(pe, acc[:, 1, :], b, range(KP), 0, KP - 1, p_hi, p_lo, k0=KD)\
                                .then_inc(wt.used, 1)
                    pairs(pe, 0, KD // 2, body)

                @block.vector
                def _(dve):
                    front.dve_norm(dve)
                    for k in range(KP):
                        dve.wait_ge(p_hi_done, k + 1)
                        nc.vector.tensor_tensor(p_lo[:, k, :].rearrange("q (t n) -> q t n", t=ST), pt[:, k, :, :],
                                                p_hi[:, k, :].rearrange("q (t n) -> q t n", t=ST).bitcast(F32),
                                                ALU.subtract).then_inc(p_lo_done, 1)

                    def add(c, b):
                        dve.wait_ge(wt.used, c + 1)
                        dve.wait_ge(gate_done, c + 1)
                        nc.vector.tensor_tensor(gate[:, b, :], acc[:, 1, :], gate[:, b, :], ALU.mult).then_inc(gated, 1)
                        dve.wait_ge(gated, c + 1)
                        rows = hT[:, bass.ds(c, 1), :].rearrange("q o n -> q (o n)")
                        nc.vector.tensor_tensor(rows, rows, gate[:, b, :], ALU.add).then_inc(added, 1)

                    def body(i):
                        for b in range(2):
                            c = 2 * i + b
                            wt.dve_lo(dve, c, b, KD + KP)
                            if isinstance(i, int) and c == 0:
                                front.dve_apply(dve)
                            else:
                                add(c - 1, 1 - b)
                            if squares and not (isinstance(i, int) and c < 3):
                                squares.dve_gather(dve, c - 3, 1 - b)
                    pairs(dve, 0, KD // 2, body)
                    if squares:
                        squares.dve_gather(dve, KD - 3, 1)
                        squares.dve_gather(dve, KD - 2, 0)
                    add(KD - 1, 1)
                    if squares:
                        squares.dve_gather(dve, KD - 1, 1)
            sp.end()

    def stage_result():
        with ExitStack() as st:
            sp = Space(st, "re")
            ht = sp.ps("ht", [P, 2, KD, P])
            row = sp.sb("row", [P, 2, D])
            turned = sp.sem("turned")
            from_act, from_dve = sp.sem("from_act"), sp.sem("from_dve")
            stored = [sp.sem("stored0"), sp.sem("stored1")]
            H2 = KD // 2 * P
            with nc.Block() as block:

                @block.sync
                def _(sync):
                    for t in range(ST):
                        sync.wait_ge(from_act, t + 1)
                        sync.wait_ge(from_dve, t + 1)
                        sync.dma_start(out[0, t * P:(t + 1) * P, :], row[:, t % 2, :]).then_inc(stored[t % 2], 16)
                    for b in range(2):
                        sync.wait_ge(stored[b], 16 * ST // 2)

                @block.tensor
                def _(pe):
                    for t in range(ST):
                        wait(pe, from_act, t - 1)
                        wait(pe, from_dve, t - 1)
                        for k in range(KD):
                            last = nc.tensor.transpose(ht[:, t % 2, k, :], hT[:, k, t * P:(t + 1) * P], ident[:])
                        last.then_inc(turned, 1)

                @block.scalar
                def _(act):
                    for t in range(ST):
                        act.wait_ge(turned, t + 1)
                        wait(act, stored[t % 2], 16 * (t // 2))
                        nc.scalar.activation(row[:, t % 2, 0:H2], ht[:, t % 2, 0:KD // 2, :].rearrange("q k n -> q (k n)"),
                                             ACT.Copy).then_inc(from_act, 1)

                @block.vector
                def _(dve):
                    for t in range(ST):
                        dve.wait_ge(turned, t + 1)
                        wait(dve, stored[t % 2], 16 * (t // 2))
                        nc.vector.tensor_copy(row[:, t % 2, H2:D], ht[:, t % 2, KD // 2:KD, :].rearrange("q k n -> q (k n)"))\
                            .then_inc(from_dve, 1)
            sp.end()

    with top, nc.allow_non_contiguous_dma(reason="gains, a column each"):
        with ExitStack() as first:
            rot = Space(first, "r").sb("rot", [P, S])
            stage_entry(rot)
            stage_project_ab(rot)

        def slab(src, rows, at=0):
            return lambda hd: src[bass.ds(hd + at, 1)].rearrange("o q n -> (o q) n")

        ab = s_ab.rearrange("c (h q) n -> (c h) q n", h=2)
        fx = s_fox.rearrange("c (h q) n -> (c h) q n", h=2)
        stage_attention("mla", HEADS, 0, slab(s_mq, QK), slab(s_mk, QK), slab(s_mv, VDIM),
                        slab(ab, 64, 4 * HEADS), None)
        stage_attention("chk", HEADS, HEADS // 2, slab(ab, 64), slab(ab, 64, HEADS), slab(ab, 64, 2 * HEADS),
                        slab(ab, 64, 3 * HEADS), slab(s_bias, P))
        with ExitStack() as between:
            h_sq[0] = Space(between, "b0").sb("h_sq", [P, S])
            stage_output("o0", ab_w_out[0], slice(0, P))
            stage_ple("e0", 0)
            stage_project_fox()
        stage_attention("fox", FH, 0, slab(fx, 64), slab(fx, 64, FH), slab(fx, 64, 2 * FH), slab(fx, 64, 3 * FH),
                        lambda hd: s_cum[bass.ds(hd, 1), :].to_broadcast([P, S]))
        with ExitStack() as between:
            h_sq[0] = Space(between, "b1").sb("h_sq", [P, S])
            stage_output("o1", fox_w_out[0], (slice(0, 64), slice(0, 1)))
            stage_ple("e1", 1)
        stage_result()


_INS = ["x", "p", "positions", "norm_g", "ab_w_in", "mla_q_norm", "mla_w_uq", "mla_kv_norm", "mla_w_ukv",
        "mla_q_gain", "mla_k_gain", "chk_q_gain", "chk_k_gain", "chk_rel_bias", "ab_w_out",
        "fox_w_in", "fox_b_f", "fox_q_gain", "fox_k_gain", "fox_w_out", "pe_w", "pe_gate_norm", "pe_gate_w"]


def kernel(**inputs):
    import concourse.bacc as bacc
    from concourse.bass_utils import run_bass_kernel_spmd

    nc = bacc.Bacc("TRN2", target_bir_lowering=False, num_devices=1)
    arrays = {name: np.ascontiguousarray(inputs[name]) for name in _INS}
    half = ROPE // 2
    freq = (np.float32(1.0) / (np.float32(10000.0) ** (np.arange(half, dtype=np.float32) / np.float32(half))))
    arrays["rope_freq"] = np.concatenate([freq, freq, -freq, freq]).astype(np.float32)[:, None]
    args = {name: nc.dram_tensor(f"in_{name}", a.shape, mybir.dt.from_np(a.dtype), kind="ExternalInput").ap()
            for name, a in arrays.items()}
    out = nc.dram_tensor("out_0", (1, S, D), F32, kind="ExternalOutput").ap()
    build(nc, **args, out=out)
    r = run_bass_kernel_spmd(nc, [{f"in_{name}": a for name, a in arrays.items()}], core_ids=[0])
    return r.results[0]["out_0"]
```
